# Optimizing a Trainium2 kernel written in Bass

```python
import math
import jax
import jax.numpy as jnp
from jax import lax
import numpy as np

D_MODEL = 1024
BATCH = 1
SEQ = 256
DEPTH = 1

MEM_LEN = 256
EPS = 1e-6

MLSTM_HEADS = 4
MLSTM_DH = 128
MLSTM_W = MLSTM_HEADS * MLSTM_DH
MLSTM_CHUNK = 64
CONV_WIDTH = 4

ATTN_PATTERNS = ((128, 1), (512, 4), (2048, 16))
N_ATTN_GROUPS = len(ATTN_PATTERNS)
HEADS_PER_GROUP = 4
ATTN_HEADS = N_ATTN_GROUPS * HEADS_PER_GROUP
ATTN_DH = 64
ATTN_W = ATTN_HEADS * ATTN_DH
ATTN_BLOCK = 128

GMLP_GROUPS = 4
GMLP_GC = 128
GMLP_W = GMLP_GROUPS * GMLP_GC
GMLP_CHUNK = 128

REL_BUCKETS = 32
REL_MAX_DIST = 2048

XATTN_HEADS = 4
XATTN_DH = 128
XATTN_W = XATTN_HEADS * XATTN_DH

N_EXPERTS = 16
N_EXPERT_GROUPS = 4
EXPERTS_PER_GROUP = N_EXPERTS // N_EXPERT_GROUPS
TOP_K = 2
D_FF_EXPERT = 512

N_BRANCH = 3
SPLIT_SIZES = (MLSTM_W, MLSTM_W, MLSTM_W, MLSTM_W, MLSTM_HEADS, MLSTM_HEADS,
               ATTN_W, ATTN_W, ATTN_W, GMLP_W, GMLP_W, N_BRANCH * D_MODEL)
SPLIT_POINTS = tuple(int(p) for p in np.cumsum(SPLIT_SIZES)[:-1])
N_IN = int(sum(SPLIT_SIZES))

kernel_name = 'hybrid_mlstm_dilated_gmlp_moe'

def rms_norm(x, gain):
    xf = x.astype(jnp.float32)
    y = xf * lax.rsqrt(jnp.mean(xf * xf, axis=-1, keepdims=True) + EPS)
    return (y * gain.astype(jnp.float32)).astype(x.dtype)

def causal_depthwise_conv(x, w):
    k = w.shape[0]
    xp = jnp.pad(x, ((0, 0), (k - 1, 0), (0, 0)))
    return lax.conv_general_dilated(xp, w[:, None, :].astype(x.dtype), window_strides=(1,), padding='VALID',
                                    dimension_numbers=('NWC', 'WIO', 'NWC'), feature_group_count=x.shape[-1])

def mlstm_chunkwise(q, k, v, i_pre, f_pre):
    b_, h_, s_, dh = q.shape
    L = MLSTM_CHUNK
    nc = s_ // L
    log_f = jax.nn.log_sigmoid(f_pre)

    def chunks(t):
        return jnp.moveaxis(t.reshape(b_, h_, nc, L, *t.shape[3:]), 2, 0)

    causal = jnp.tril(jnp.ones((L, L), dtype=bool))

    def step(carry, inp):
        c_st, n_st, m_st = carry
        qj, kj, vj, ij, fj = inp
        b = jnp.cumsum(fj, axis=-1)
        d_mat = jnp.where(causal, b[..., :, None] - b[..., None, :] + ij[..., None, :], -jnp.inf)
        inter = b + m_st[..., None]
        m_t = jnp.maximum(inter, jnp.max(d_mat, axis=-1))
        w_intra = jnp.exp(d_mat - m_t[..., None])
        w_inter = jnp.exp(inter - m_t)
        s = jnp.einsum('bhtd,bhrd->bhtr', qj, kj) * w_intra
        num = jnp.einsum('bhtr,bhre->bhte', s, vj) + w_inter[..., None] * jnp.einsum('bhtd,bhde->bhte', qj, c_st)
        den = jnp.sum(s, axis=-1) + w_inter * jnp.einsum('bhtd,bhd->bht', qj, n_st)
        h = num / jnp.maximum(jnp.abs(den), jnp.exp(-m_t))[..., None]
        b_last = b[..., -1]
        dec = b_last[..., None] - b + ij
        m_new = jnp.maximum(b_last + m_st, jnp.max(dec, axis=-1))
        w_k = jnp.exp(dec - m_new[..., None])
        w_c = jnp.exp(b_last + m_st - m_new)
        c_new = w_c[..., None, None] * c_st + jnp.einsum('bhr,bhrd,bhre->bhde', w_k, kj, vj)
        n_new = w_c[..., None] * n_st + jnp.einsum('bhr,bhrd->bhd', w_k, kj)
        return (c_new, n_new, m_new), h

    init = (jnp.zeros((b_, h_, dh, dh), jnp.float32), jnp.zeros((b_, h_, dh), jnp.float32),
            jnp.zeros((b_, h_), jnp.float32))
    _, hs = lax.scan(step, init, (chunks(q), chunks(k), chunks(v), chunks(i_pre), chunks(log_f)))
    return jnp.moveaxis(hs, 0, 2).reshape(b_, h_, s_, dh)

def mixer_mlstm(mq, mk, mv, mo, mi, mf, conv_w, gate_b, norm_g):
    b_, s_, _ = mq.shape
    qk = jax.nn.silu(causal_depthwise_conv(jnp.concatenate([mq, mk], axis=-1), conv_w))
    q, k = jnp.split(qk, 2, axis=-1)

    def heads(t):
        return t.reshape(b_, s_, MLSTM_HEADS, MLSTM_DH).transpose(0, 2, 1, 3).astype(jnp.float32)

    i_pre = (mi + gate_b[:MLSTM_HEADS]).astype(jnp.float32).transpose(0, 2, 1)
    f_pre = (mf + gate_b[MLSTM_HEADS:]).astype(jnp.float32).transpose(0, 2, 1)
    h = mlstm_chunkwise(heads(q), heads(k) * (MLSTM_DH ** -0.5), heads(mv), i_pre, f_pre)
    h = rms_norm(h.transpose(0, 2, 1, 3), norm_g.reshape(MLSTM_HEADS, MLSTM_DH))
    return (h.reshape(b_, s_, MLSTM_W) * jax.nn.sigmoid(mo.astype(jnp.float32))).astype(mq.dtype)

def rel_bucket(n):
    max_exact = REL_BUCKETS // 2
    nf = jnp.maximum(n, 1).astype(jnp.float32)
    log_b = max_exact + (jnp.log(nf / max_exact) / math.log(REL_MAX_DIST / max_exact)
                         * (REL_BUCKETS - max_exact)).astype(jnp.int32)
    return jnp.where(n < max_exact, n, jnp.minimum(log_b, REL_BUCKETS - 1))

def dilated_window_attention(q, k, v, bias_steps, dilation, steps):
    b_, hg, s_, dh = q.shape
    ls = s_ // dilation
    nb = -(-ls // ATTN_BLOCK)
    lp = nb * ATTN_BLOCK

    def gather_stride(t):
        t = t.reshape(b_, hg, ls, dilation, dh).transpose(0, 1, 3, 2, 4)
        t = jnp.pad(t, ((0, 0), (0, 0), (0, 0), (0, lp - ls), (0, 0)))
        return t.reshape(b_, hg, dilation, nb, ATTN_BLOCK, dh)

    def with_previous_block(t):
        prev = jnp.pad(t, ((0, 0), (0, 0), (0, 0), (1, 0), (0, 0), (0, 0)))[:, :, :, :-1]
        return jnp.concatenate([prev, t], axis=4)

    qb = gather_stride(q)
    kb = with_previous_block(gather_stride(k))
    vb = with_previous_block(gather_stride(v))
    qi = jnp.arange(ATTN_BLOCK)[:, None]
    ki = jnp.arange(2 * ATTN_BLOCK)[None, :]
    dist = ATTN_BLOCK + qi - ki
    local_ok = (dist >= 0) & (dist <= steps)
    first_ok = (jnp.arange(nb) > 0)[:, None, None] | (ki >= ATTN_BLOCK)[None]
    valid = local_ok[None] & first_ok
    bias = bias_steps[:, jnp.clip(dist, 0, steps)]
    logits = jnp.einsum('bhrnqd,bhrnkd->bhrnqk', qb, kb).astype(jnp.float32) * (ATTN_DH ** -0.5)
    logits = logits + bias.astype(jnp.float32)[None, :, None, None]
    logits = jnp.where(valid[None, None, None], logits, -jnp.inf)
    m = jnp.max(logits, axis=-1, keepdims=True)
    p = jnp.exp(logits - m)
    l = jnp.sum(p, axis=-1, keepdims=True)
    o = jnp.einsum('bhrnqk,bhrnkd->bhrnqd', p, vb.astype(jnp.float32)) / l
    lse = m + jnp.log(l)

    def scatter_back(t):
        c = t.shape[-1]
        t = t.reshape(b_, hg, dilation, lp, c)[:, :, :, :ls]
        return t.transpose(0, 1, 3, 2, 4).reshape(b_, hg, s_, c)

    return scatter_back(o), scatter_back(lse)[..., 0]

def mixer_dilated_attention(aq, ak, av, qk_g, rel_bias):
    b_, s_, _ = aq.shape

    def heads(t):
        return t.reshape(b_, s_, ATTN_HEADS, ATTN_DH)

    q = rms_norm(heads(aq), qk_g[0]).transpose(0, 2, 1, 3)
    k = rms_norm(heads(ak), qk_g[1]).transpose(0, 2, 1, 3)
    v = heads(av).transpose(0, 2, 1, 3)
    outs, lses = [], []
    for g, (window, dilation) in enumerate(ATTN_PATTERNS):
        steps = window // dilation
        hs = slice(g * HEADS_PER_GROUP, (g + 1) * HEADS_PER_GROUP)
        bias_steps = rel_bias[rel_bucket(jnp.arange(steps + 1) * dilation)][:, hs].T
        o, lse = dilated_window_attention(q[:, hs], k[:, hs], v[:, hs], bias_steps, dilation, steps)
        outs.append(o)
        lses.append(lse)
    alpha = jax.nn.softmax(jnp.stack(lses), axis=0)
    o = jnp.stack(outs) * alpha[..., None]
    return o.transpose(1, 3, 0, 2, 4).reshape(b_, s_, ATTN_W).astype(aq.dtype)

def mixer_spatial_gating(gu, gv, norm_g, w_s, b_s):
    b_, s_, _ = gu.shape
    nch = s_ // GMLP_CHUNK
    u = jax.nn.gelu(gu).reshape(b_, nch, GMLP_CHUNK, GMLP_GROUPS, GMLP_GC)
    v = rms_norm(jax.nn.gelu(gv).reshape(b_, nch, GMLP_CHUNK, GMLP_GROUPS, GMLP_GC),
                 norm_g.reshape(GMLP_GROUPS, GMLP_GC))
    w_causal = jnp.where(jnp.tril(jnp.ones((GMLP_CHUNK, GMLP_CHUNK), dtype=bool)), w_s, 0.0)
    mixed = jnp.einsum('gts,bnsgc->bntgc', w_causal.astype(v.dtype), v) + b_s.T.astype(v.dtype)[None, None, :, :, None]
    return (u * mixed).reshape(b_, s_, GMLP_W)

def memory_cross_attention(h, mem_n, w_q, w_kv, qk_g, w_o):
    b_, s_, _ = h.shape
    m_ = mem_n.shape[1]
    q = rms_norm((h @ w_q).reshape(b_, s_, XATTN_HEADS, XATTN_DH), qk_g[0])
    k, v = jnp.split(mem_n @ w_kv, 2, axis=-1)
    k = rms_norm(k.reshape(b_, m_, XATTN_HEADS, XATTN_DH), qk_g[1])
    v = v.reshape(b_, m_, XATTN_HEADS, XATTN_DH)
    logits = jnp.einsum('bshd,bmhd->bhsm', q, k).astype(jnp.float32) * (XATTN_DH ** -0.5)
    p = jax.nn.softmax(logits, axis=-1).astype(v.dtype)
    o = jnp.einsum('bhsm,bmhd->bshd', p, v).reshape(b_, s_, XATTN_W)
    return o @ w_o

def grouped_moe(h, router_w, router_b, w_gate, w_up, w_down):
    logits = (h @ router_w).astype(jnp.float32) + router_b.astype(jnp.float32)
    probs = jax.nn.softmax(logits, axis=-1)
    grouped = probs.reshape(*probs.shape[:-1], N_EXPERT_GROUPS, EXPERTS_PER_GROUP)
    group_score = jnp.sum(lax.top_k(grouped, TOP_K)[0], axis=-1)
    best = jnp.argmax(group_score, axis=-1)
    in_group = (best[..., None] == jnp.arange(N_EXPERT_GROUPS))[..., None]
    masked = jnp.where(in_group, grouped, -1.0).reshape(probs.shape)
    top_p, top_i = lax.top_k(masked, TOP_K)
    top_w = top_p / jnp.sum(top_p, axis=-1, keepdims=True)
    gates = jnp.sum(jax.nn.one_hot(top_i, N_EXPERTS, dtype=jnp.float32) * top_w[..., None], axis=-2).astype(h.dtype)
    out = jnp.zeros_like(h)
    for e in range(N_EXPERTS):
        a = jax.nn.silu(h @ w_gate[e]) * (h @ w_up[e])
        out = out + gates[..., e:e + 1] * (a @ w_down[e])
    return out

def setup_inputs(seed: int = 0) -> dict:
    key = jax.random.key(seed)
    ks = iter(jax.random.split(key, 40))

    def nrm(shape, scale):
        return jax.random.normal(next(ks), shape, jnp.float32) * scale

    def gain(shape):
        return 1.0 + nrm(shape, 0.05)

    L = DEPTH
    forget_b = jnp.broadcast_to(jnp.linspace(3.0, 6.0, MLSTM_HEADS), (L, MLSTM_HEADS))
    mlstm_gate_b = jnp.concatenate([nrm((L, MLSTM_HEADS), 0.5) - 2.0,
                                    forget_b + nrm((L, MLSTM_HEADS), 0.1)], axis=-1)
    return {
        'x': nrm((BATCH, SEQ, D_MODEL), 1.0),
        'mem': nrm((BATCH, MEM_LEN, D_MODEL), 1.0),
        'norm_mix': gain((L, D_MODEL)),
        'w_in': nrm((L, D_MODEL, N_IN), D_MODEL ** -0.5),
        'mlstm_conv': nrm((L, CONV_WIDTH, 2 * MLSTM_W), CONV_WIDTH ** -0.5),
        'mlstm_gate_b': mlstm_gate_b,
        'mlstm_norm': gain((L, MLSTM_W)),
        'attn_qk_norm': gain((L, 2, ATTN_DH)),
        'gmlp_norm': gain((L, GMLP_W)),
        'gmlp_ws': nrm((L, GMLP_GROUPS, GMLP_CHUNK, GMLP_CHUNK), GMLP_CHUNK ** -0.5),
        'gmlp_bs': 1.0 + nrm((L, GMLP_GROUPS, GMLP_CHUNK), 0.1),
        'w_branch_a': nrm((L, MLSTM_W, D_MODEL), MLSTM_W ** -0.5),
        'w_branch_b': nrm((L, ATTN_W, D_MODEL), ATTN_W ** -0.5),
        'w_branch_c': nrm((L, GMLP_W, D_MODEL), GMLP_W ** -0.5),
        'w_out': nrm((L, D_MODEL, D_MODEL), 0.5 * D_MODEL ** -0.5),
        'rel_bias': nrm((REL_BUCKETS, ATTN_HEADS), 0.5),
        'norm_xattn': gain((L, D_MODEL)),
        'norm_mem': gain((L, D_MODEL)),
        'w_xq': nrm((L, D_MODEL, XATTN_W), D_MODEL ** -0.5),
        'w_xkv': nrm((L, D_MODEL, 2 * XATTN_W), D_MODEL ** -0.5),
        'xattn_qk_norm': gain((L, 2, XATTN_DH)),
        'w_xo': nrm((L, XATTN_W, D_MODEL), 0.5 * XATTN_W ** -0.5),
        'norm_ffn': gain((L, D_MODEL)),
        'router_w': nrm((D_MODEL, N_EXPERTS), D_MODEL ** -0.5),
        'router_b': nrm((N_EXPERTS,), 0.01),
        'w_expert_gate': nrm((L, N_EXPERTS, D_MODEL, D_FF_EXPERT), D_MODEL ** -0.5),
        'w_expert_up': nrm((L, N_EXPERTS, D_MODEL, D_FF_EXPERT), D_MODEL ** -0.5),
        'w_expert_down': nrm((L, N_EXPERTS, D_FF_EXPERT, D_MODEL), 0.5 * D_FF_EXPERT ** -0.5),
    }

def reference(x, mem, norm_mix, w_in, mlstm_conv, mlstm_gate_b, mlstm_norm, attn_qk_norm, gmlp_norm,
              gmlp_ws, gmlp_bs, w_branch_a, w_branch_b, w_branch_c, w_out, rel_bias, norm_xattn, norm_mem,
              w_xq, w_xkv, xattn_qk_norm, w_xo, norm_ffn, router_w, router_b, w_expert_gate, w_expert_up,
              w_expert_down):
    b_, s_, _ = x.shape
    for l in range(DEPTH):
        h = rms_norm(x, norm_mix[l])
        (mq, mk, mv, mo, mi, mf, aq, ak, av, gu, gv, gate_pre) = jnp.split(h @ w_in[l], SPLIT_POINTS, axis=-1)
        ya = mixer_mlstm(mq, mk, mv, mo, mi, mf, mlstm_conv[l], mlstm_gate_b[l], mlstm_norm[l])
        yb = mixer_dilated_attention(aq, ak, av, attn_qk_norm[l], rel_bias)
        yc = mixer_spatial_gating(gu, gv, gmlp_norm[l], gmlp_ws[l], gmlp_bs[l])
        g = jax.nn.sigmoid(gate_pre.reshape(b_, s_, N_BRANCH, D_MODEL))
        merged = (g[:, :, 0] * (ya @ w_branch_a[l]) + g[:, :, 1] * (yb @ w_branch_b[l])
                  + g[:, :, 2] * (yc @ w_branch_c[l]))
        x = x + merged @ w_out[l]
        x = x + memory_cross_attention(rms_norm(x, norm_xattn[l]), rms_norm(mem, norm_mem[l]),
                                       w_xq[l], w_xkv[l], xattn_qk_norm[l], w_xo[l])
        x = x + grouped_moe(rms_norm(x, norm_ffn[l]), router_w, router_b,
                            w_expert_gate[l], w_expert_up[l], w_expert_down[l])
    return x


_drawn_inputs = setup_inputs


def setup_inputs(seed=0):
    import zlib

    import numpy as np

    out = dict(_drawn_inputs(seed))
    spreads = {}
    factors = {'attn_qk_norm': 2.813,
     'gmlp_norm': 3.136,
     'norm_xattn': 2.806,
     'norm_mem': 2.99,
     'xattn_qk_norm': 3.534,
     'router_b': 3.093}
    for name, (base, spread) in spreads.items():
        noise = np.random.default_rng([zlib.crc32(name.encode()), seed]).standard_normal(out[name].shape)
        drawn = base * np.exp(spread * noise) if base else spread * noise
        out[name] = jnp.asarray(drawn.astype(out[name].dtype))
    for name, factor in factors.items():
        out[name] = (out[name] * factor).astype(out[name].dtype)
    return out
```

```python
import math
from contextlib import ExitStack

import numpy as np
import concourse.bass as bass
from concourse import mybir

P = 128
S = 256
NT = S // P
D = 1024
EPS = 1e-6
MH, MDH = 4, 128
MW = MH * MDH
AG, AHG, ADH = 3, 4, 64
AH = AG * AHG
AW = AH * ADH
DILATION = (1, 4, 16)
STEPS = 128
GG, GC = 4, 128
GW = GG * GC
XH, XDH = 4, 128
XW = XH * XDH
REL_BUCKETS, REL_MAX_DIST = 32, 2048
NE, NG, EPG, FF = 16, 4, 4, 512
SLOTS = 64
NEG = -1.0e30
KD = D // P
COLS = 512
BLK = 2048
RING = 4
E_RING = 8
DIRECT = {"gate": 1, "up": 1, "down": 1}
TOEP = 384

C_IF = 4 * MW
C_AQ = C_IF + 2 * MH
C_GU = C_AQ + 3 * AW
C_GATE = C_GU + 2 * GW
N_IN = C_GATE + 3 * D
C_WIDE = 264


def shape_constants():
    r = np.arange(P)
    ident = np.eye(P, dtype=np.float32)
    neg_future = np.where(r[:, None] > r[None, :], np.float32(NEG), np.float32(0))
    before = (r[:, None] < r[None, :]).astype(np.float32)
    keep_past = (r[:, None] >= r[None, :]).astype(np.float32)
    ones = np.ones((P, P), np.float32)
    minus_head = np.zeros((P, MH, P), np.float32)
    for h in range(MH):
        minus_head[h, h] = -1
    iota = np.tile(np.arange(SLOTS, dtype=np.float32), 2)[None].repeat(P, 0)
    tie = (np.arange(EPG)[None, :] < np.arange(EPG)[:, None]).astype(np.float32)
    tie = tie.reshape(1, -1).repeat(P, 0)
    both = np.tile(np.eye(SLOTS, dtype=np.float32), (2, 2))
    minus_half = np.full((P, 48), -0.5, np.float32)
    parts = [neg_future, before, keep_past, ones, minus_head.reshape(P, -1), iota, tie, both, minus_half]
    onehot = np.zeros((REL_BUCKETS + 1, AG, TOEP), np.float32)
    exact = REL_BUCKETS // 2
    for g, dil in enumerate(DILATION):
        for y in range(TOEP):
            d = S - 1 - y
            if d < 0 or d % dil or d // dil > STEPS:
                onehot[REL_BUCKETS, g, y] = 1
            elif d < exact:
                onehot[d, g, y] = 1
            else:
                b = exact + int(math.log(d / exact) / math.log(REL_MAX_DIST / exact) * (REL_BUCKETS - exact))
                onehot[min(b, REL_BUCKETS - 1), g, y] = 1
    return ident, np.ascontiguousarray(np.concatenate(parts, 1)), onehot.reshape(REL_BUCKETS + 1, -1)


N_CONST = P * 4 + MH * P + P + EPG * EPG + P + 48


def build_program(nc, d_in, out):
    fp32, f32r, i32 = mybir.dt.float32, mybir.dt.float32r, mybir.dt.int32
    ALU, ACT, AX = mybir.AluOpType, mybir.ActivationFunctionType, mybir.AxisListType
    scratch = nc.dram_tensor("bias_rows", (AG * AHG, TOEP), fp32)
    bias_square = nc.dram_tensor("bias_square", (AG * AHG, P, S), fp32).ap()

    ctx = ExitStack()
    with ctx:
        base = -(-nc.sbuf_base // 64) * 64
        place = {"at": base}

        def region(nbytes):
            at = place["at"]
            place["at"] += -(-nbytes // 32) * 32
            assert place["at"] <= nc.sbuf_usable_end, place["at"]
            return at

        def at(name, offset, shape, dt=fp32):
            return nc.alloc_sbuf_tensor_at(name, shape, dt, offset=offset)

        def sb(name, shape, dt=fp32):
            return at(name, region(4 * int(np.prod(shape[1:]))), shape, dt)

        w_raw = sb("w_raw", [P, RING, BLK])
        w_hi = sb("w_hi", [P, RING, BLK], f32r)
        w_lo = sb("w_lo", [P, RING, BLK], f32r)
        x_res = sb("x_res", [P, NT, D])
        act_at = place["at"]
        act_hi = sb("act_hi", [P, KD, S], f32r)
        act_lo = sb("act_lo", [P, KD, S], f32r)
        act_hi_mem = at("e_raw_4", act_at, [P, BLK])
        act_lo_mem = at("e_raw_5", act_at + 4 * KD * S, [P, BLK])
        ident = sb("ident", [P, P])
        const = sb("const", [P, N_CONST])
        off = 0

        def part(n):
            nonlocal off
            v = const[:, off:off + n]
            off += n
            return v

        neg_future, before, keep_past, ones = part(P), part(P), part(P), part(P)
        minus_head = part(MH * P).rearrange("p (h c) -> p h c", h=MH)
        iota = part(P)
        tie = part(EPG * EPG).rearrange("p (j i) -> p j i", j=EPG)
        both = part(P)
        minus_half = part(48)
        gains = sb("gains", [P, 2 * KD + 4])
        g_mix, g_mem, g_mls = gains[:, 0:8], gains[:, 8:16], gains[:, 16:20]
        vec_cols = sb("vec_cols", [P, 8 + 2 * KD])
        g_xat, g_ffn = vec_cols[:, 8:8 + KD], vec_cols[:, 8 + KD:8 + 2 * KD]
        g_qk, g_xqk, gs_b = vec_cols[:, 0:2], vec_cols[:, 2:4], vec_cols[:, 4:8]
        gate_bi, gate_bf = sb("gate_bi", [MH, 1]), sb("gate_bf", [MH, 1])
        stat = sb("stat", [P, 320])
        router_b = sb("router_b", [P, NE])
        n_rounds_i = sb("n_rounds_i", [1, 1], i32)

        q_at = region(8192)
        zq_at, vx_at, zo_at = region(8192), region(NT * MH * 130 * 4), region(4096)
        zqk_at, zv_at, zg_at, tg_at = region(NT * 1536 * 4), region(NT * AW * 4), region(8192), region(NT * 3 * D * 4)
        zif_at = region(NT * 8 * 4)
        m_at = region(8832 + 8192)
        end_at = place["at"]

        mem_x = at("mem_x", q_at, [P, NT, D])
        lg0 = at("lg0", m_at + 12288, [P, AG, S])
        lg1 = at("lg1", q_at, [P, AG, S])
        pT = at("pT", q_at + 3072, [P, AG * S])
        zq = at("zq", zq_at, [P, NT, 2 * MW])
        vx = at("vx", vx_at, [P, NT, MH, 130])
        zo = at("zo", zo_at, [P, NT, MW])
        zqk = at("zqk", zqk_at, [P, NT, 2 * AW])
        zv = at("zv", zv_at, [P, NT, AW])
        zg = at("zg", zg_at, [P, NT, 2 * GW])
        tg = at("tg", tg_at, [P, NT, 3 * D])
        merged = tg[:, :, 0:D]
        zif = at("zif", zif_at, [P, NT, 8])
        pre = at("pre", m_at, [P, KD, S + 3])
        post = at("post", m_at + 8832, [P, KD, S])
        rows = at("rows", zq_at, [MH, 6, S])
        wgt = at("wgt", m_at, [P, 3 * P])
        pm = at("pm", m_at + 1536, [P, 2, 3 * P])
        numer = at("numer", m_at + 4608, [P, NT, MH, 130])
        cw = sb("cw", [P, 32])
        conv_rows = at("conv_rows", tg_at + 14336, [32, P])
        toep = at("toep", zq_at, [P, AH, S])
        qkT = at("qkT", m_at, [P, 12, S])
        table = sb("table", [REL_BUCKETS + 1, AH])
        onehot = at("onehot", tg_at, [REL_BUCKETS + 1, AG, TOEP])
        bias_row = at("bias_row", tg_at + AG * TOEP * 4, [AHG, AG, TOEP])
        yb_hi = at("yb_hi", zqk_at, [P, 6, S], f32r)
        yb_lo = at("yb_lo", zqk_at + 6144, [P, 6, S], f32r)
        vec_rows = at("vec_rows", tg_at + 14848, [8 + 2 * KD, P])
        ws_t = at("ws_t", tg_at + 12288, [P, GG, P])
        wT = sb("wT", [P, GG, P])
        gs_gain = sb("gs_gain", [P, GW])
        ya_hi, ya_lo = at("ya_hi", m_at, [P, 4, S], f32r), at("ya_lo", m_at + 4096, [P, 4, S], f32r)
        yc_hi, yc_lo = at("yc_hi", m_at + 8192, [P, 4, S], f32r), at("yc_lo", m_at + 12288, [P, 4, S], f32r)
        xkv = at("xkv", zq_at, [P, NT, 2 * XW])
        xkT = at("xkT", vx_at, [P, XH, S])
        xq = at("xq", zqk_at, [P, NT, XW])
        xqT = at("xqT", zqk_at + 4096, [P, XH, S])
        sq_s = at("sq_s", q_at, [P, 2 * D])
        mg_hi, mg_lo = at("mg_hi", m_at, [P, KD, S], f32r), at("mg_lo", m_at + 8192, [P, KD, S], f32r)
        sq_g = at("sq_g", q_at + 4096, [P, NT, GW])
        junk_x = at("junk_x", m_at, [P, NT, D])
        junk_1 = at("junk_1", q_at, [P, NT, D])
        junk_mem = at("junk_mem", act_at + 4 * KD * S, [P, NT, D])
        sq_k = at("sq_k", zv_at, [P, NT, XW])
        sq_q = at("sq_q", zv_at, [P, NT, XW])
        xp = at("xp", tg_at, [P, NT, XH * S])
        xpT = at("xpT", tg_at + 8192, [P, XH, NT, S])
        oT_hi, oT_lo = at("oT_hi", zg_at, [P, XH, S], f32r), at("oT_lo", zg_at + 4096, [P, XH, S], f32r)

        place["at"] = zq_at
        xg_at = region(KD * EPG * P * 4)
        xg = at("xg", xg_at, [P, KD, EPG, P], f32r)
        x2T = at("x2T", xg_at, [P, KD, S])
        h_hi, h_lo = sb("h_hi", [P, NT, D], f32r), sb("h_lo", [P, NT, D], f32r)
        h_full = sb("h_full", [P, NT, D])
        sel = sb("sel", [P, NT, EPG, P], f32r)
        selT = sb("selT", [P, EPG, S], f32r)
        w_slot, w_slot_next = sb("w_slot", [P, EPG]), sb("w_slot_next", [P, EPG])
        gu = sb("gu", [P, 2, FF])
        e_act = sb("e_act", [P, 2, FF // P, SLOTS])
        a_st = sb("a_st", [P, FF // P, P], f32r)
        y_hi, y_lo = sb("y_hi", [P, D], f32r), sb("y_lo", [P, D], f32r)
        route = sb("route", [P, 1024])
        router_w = sb("router_w", [P, KD, NE])
        g_ffn_row = sb("g_ffn_row", [P, D])
        zeros = sb("zeros", [P, P])[:]
        assert place["at"] <= m_at + 8832, (place["at"], m_at)
        e_raw = [None] * RING + [act_hi_mem, act_lo_mem, at("e_raw_6", q_at, [P, BLK]), at("e_raw_7", m_at + 8832, [P, BLK])]

        ps = ctx.enter_context(nc.psum_tensor("ps", [P, 8, 512], fp32))

        def sem(name):
            return ctx.enter_context(nc.semaphore(name))

        w_in_slot = [sem(f"w_landed_{i}") for i in range(RING)]
        e_in_slot = [None] * RING + [sem(f"e_landed_{i}") for i in range(RING, E_RING)]
        hi_done, lo_done = sem("w_hi_done"), sem("w_lo_done")
        mm_done = sem("w_block_used")
        ev_act, ev_dve = sem("chunk_moved_by_act"), sem("chunk_moved_by_dve")
        ld = {n: sem("loaded_" + n) for n in (
            "x", "ident", "const", "aux", "small", "mem", "toep", "bias_rows", "moe", "out")}
        ST = ("x", "mem", "a", "c", "merged", "x1", "o", "x2")
        sT = {n: sem(f"turned_{n}") for n in ST}
        sH = {n: sem(f"hi_of_{n}") for n in ST}
        sL = {n: sem(f"lo_of_{n}") for n in ST}
        RM = ("x", "mls", "att", "gml", "mem", "xk", "x1", "xq", "x2")
        s_sq = {n: sem(f"squared_{n}") for n in RM}
        s_ms = {n: sem(f"mean_square_{n}") for n in RM}
        s_rs = {n: sem(f"rsqrt_{n}") for n in RM}
        names = """aux_pe aux qk_turned conv_in pad_ready conv_out tanh_qk silu_qk gates_turned neg_abs log_done decay_done
            floor_done cols_turned cols_moved decay_logit score w_exp prob_ready pv_done numer_moved numer_used ya_done
            att_sq_read aqk_ready aqk_turned aqk_moved a_logit a_logit_moved a_max a_exp a_norm a_pturned a_pmoved
            a_pv a_yhi a_ylo gelu_done gv_ready g_mixed yc_done xk_ready xk_turned xk_moved xq_turned
            xq_moved x_logit x_max x_exp x_norm x_pturned x_pmoved merged_ready 
            x2T_moved r_logit r_max r_exp chosen pos_pe rounds_ready h_full_done h_hi_done
            h_lo_done selected selT_pe selT_done gath_pe gath_moved wslot_pe gu_moved et_pe et_tanh
            a_ready yhi_done ylo_done scat_pe moe_done zeros_set out_ready vone wslot_moved xq_scaled zeros""".split()
        s = {n: sem(n) for n in names}

        win = d_in["w_in"][0].rearrange("(p t) n -> p t n", t=KD)

        def rows_of(w, t):
            return w[0].rearrange("(p t) n -> p t n", t=t)

        def tiles_of(w, t):
            return w[0].rearrange("(t p) n -> p t n", t=t)

        cols = [(c * COLS, COLS) for c in range(4)] + [(C_IF, C_WIDE)]
        cols += [(C_IF + C_WIDE + c * COLS, COLS) for c in range(12)]
        chunks = [[win[:, 4 * k:4 * k + 4, c0:c0 + n] for k in range(2)] for c0, n in cols]

        def halves(v, nt, width):
            per = nt if nt <= 4 else nt // 2
            return [[v[:, k:k + per, n:n + COLS] for k in range(0, nt, per)] for n in range(0, width, COLS)]

        keys, values = halves(rows_of(d_in["w_xkv"], KD), KD, 2 * XW)
        chunks += halves(tiles_of(d_in["w_branch_b"], 6), 6, D)
        chunks += halves(rows_of(d_in["w_branch_a"], 4), 4, D)
        chunks += halves(rows_of(d_in["w_branch_c"], 4), 4, D)
        chunks += [keys]
        chunks += halves(tiles_of(d_in["w_out"], KD), KD, D)
        chunks += [values[:1]] + halves(tiles_of(d_in["w_xq"], KD), KD, XW) + [values[1:]]
        chunks += halves(tiles_of(d_in["w_xo"], XH), XH, D)
        C_B, C_A, C_C, C_K, C_OUT, C_V0, C_XQ, C_V1, C_XO = 17, 19, 21, 23, 24, 26, 27, 28, 29
        by_act = [c for c in range(C_B)] + [C_K, C_V1]
        by_dve = [c for c in range(C_B, C_XO + 2) if c not in by_act and c != C_V0]

        def moved(c):
            return (ev_act, by_act.index(c) + 1) if c in by_act else (ev_dve, by_dve.index(c) + 1)

        blocks = [b for c in chunks for b in c]
        first_block = [sum(len(c) for c in chunks[:n]) for n in range(len(chunks) + 1)]
        NB1 = len(blocks)
        GB = 6 * EPG
        assert NB1 % 2 == 0 and GB % RING == 0
        ex_order = []
        for j in range(EPG):
            ex_order += [(j, "gate")] + ([(j - 1, "down")] if j else []) + [(j, "up")]
        ex_order += [(EPG - 1, "down")]
        ex_block = {k: 2 * n for n, k in enumerate(ex_order)}
        direct = {2 * m: DIRECT[which] for m, (_, which) in enumerate(ex_order) if which in DIRECT and 2 < m < len(ex_order) - 1}

        FREE = 1

        def split_steps(m, more, ahead=0):
            return range(max(2 * m - 2 + ahead, 0) + RING, min(2 * m + ahead + RING, GB + RING if more else GB))

        def bview(t, b, shape):
            n = int(np.prod(shape[1:]))
            return t[:, b % RING, 0:n].rearrange("p (t n) -> p t n", t=shape[1])

        def bc(v, shape):
            return v.to_broadcast(list(shape))

        rt_at = [0]

        def rt(*shape):
            n = int(np.prod(shape))
            v = route[:, rt_at[0]:rt_at[0] + n]
            rt_at[0] += n
            assert rt_at[0] <= 1024
            return v

        prob, posm, gates, chosen, topw = (rt(NT * NE) for _ in range(5))
        gt, ge = rt(NT * NE * EPG), rt(NT * NE * EPG)
        rank, r2 = rt(NT * NE), rt(NT * NE)
        score, eq, earlier, first = (rt(NT * NG) for _ in range(4))
        rmax, rsum, rrec, best = rt(NT), rt(NT), rt(NT), rt(NT)
        total, gcur = rt(NE), rt(NT * EPG)

        st_at = {}

        def stats(name, n):
            if name not in st_at:
                st_at[name] = (sum(v[1] for v in st_at.values()), n)
            o, m = st_at[name]
            assert o + m <= 320
            return stat[:, o:o + m]

        ss_x, rs_x, rsh_x = stats("ss_x", 2), stats("rs_x", 2), stats("rsh_x", 2)
        aT, emT, den, rden = stats("aT", 8), stats("emT", 8), stats("den", 8), stats("rden", 8)
        ss_m, rs_m = stats("ss_m", 8), stats("rs_m", 8)
        ss_a, rs_a = stats("ss_a", 48), stats("rs_a", 48)
        a_nm, a_sum, a_rec = stats("a_nm", 8), stats("a_sum", 8), stats("a_rec", 8)
        ss_g, rs_g = stats("ss_g", 8), stats("rs_g", 8)
        ss_mem, rs_mem = stats("ss_mem", 2), stats("rs_mem", 2)
        ss_k, rs_k, ss_q, rs_q = stats("ss_k", 8), stats("rs_k", 8), stats("ss_q", 8), stats("rs_q", 8)
        x_nm, x_sum, x_rec = stats("x_nm", 8), stats("x_sum", 8), stats("x_rec", 8)
        ss_1, rs_1, ss_2, rs_2 = stats("ss_1", 2), stats("rs_1", 2), stats("ss_2", 2), stats("rs_2", 2)

        turn_fills = [[(0, 3)], [(0, 4), (4, 2)]]
        fills_before = [sum(len(turn_fills[v // 2 % 2]) for v in range(u)) for u in range(9)]
        scratch_rows = scratch.ap().rearrange("(g h) y -> h g y", g=AG)
        bias_shifted = bass.AP(tensor=scratch.ap().tensor, offset=P - 1, ap=[[TOEP, AH], [-1, P], [1, S]])

        def e_slot(n):
            k = n % E_RING
            if k >= RING:
                return e_raw[k], e_in_slot[k], n // E_RING + 1
            k = (NB1 + k) % RING
            return w_raw[:, k, :], w_in_slot[k], -(-(NB1 - k) // RING) + n // E_RING + 1

        expert_block = [(j, which, half) for j, which in ex_order for half in range(2)]

        block = ctx.enter_context(nc.Block())

        def f32(v):
            return v.bitcast(fp32)

        @block.sync
        def _(sp):
            def load(name, *pairs):
                for dst, src in pairs:
                    sp.dma_start(dst, src).then_inc(ld[name], 16)

            def col(v):
                return v.rearrange("(n o) -> n o", o=1)

            def weight_block(b):
                if b >= RING:
                    sp.wait_ge(hi_done, b - RING + 1)
                    sp.wait_ge(lo_done, b - RING + 1)
                sp.dma_start(bview(w_raw, b, blocks[b].shape), blocks[b]).then_inc(w_in_slot[b % RING], 16)

            load("x", *[(x_res[:, i, :], d_in["x"][0, i * P:(i + 1) * P, :]) for i in range(NT)])
            load("ident", (ident[:], d_in["c_ident"]), (g_mix, d_in["norm_mix"][0].rearrange("(p t) -> p t", t=KD)))
            for b in range(4):
                weight_block(b)
            load("const", (const[:], d_in["c_const"]))
            load("aux", (conv_rows[:], d_in["mlstm_conv"][0].rearrange("w (f p) -> (w f) p", p=P)),
                 (ws_t[:], d_in["gmlp_ws"][0].rearrange("g t s -> t g s")),
                 (table[0:REL_BUCKETS, :], d_in["rel_bias"]),
                 (vec_rows[0:2, 0:ADH], d_in["attn_qk_norm"][0]), (vec_rows[0:2, ADH:P], d_in["attn_qk_norm"][0]),
                 (vec_rows[2:4, :], d_in["xattn_qk_norm"][0]), (vec_rows[4:8, :], d_in["gmlp_bs"][0]),
                 (onehot[:], d_in["c_onehot"].rearrange("b (g y) -> b g y", g=AG)))
            load("aux", (vec_rows[8:8 + KD, :], d_in["norm_xattn"][0].rearrange("(t p) -> t p", t=KD)),
                 (vec_rows[8 + KD:8 + 2 * KD, :], d_in["norm_ffn"][0].rearrange("(t p) -> t p", t=KD)))
            load("aux", (gate_bi[:], col(d_in["mlstm_gate_b"][0, 0:MH])),
                 (gate_bf[:], col(d_in["mlstm_gate_b"][0, MH:2 * MH])))
            for b in range(4, 8):
                weight_block(b)
            load("small", (g_mls, d_in["mlstm_norm"][0].rearrange("(p t) -> p t", t=4)),
                 (g_mem, d_in["norm_mem"][0].rearrange("(p t) -> p t", t=KD)),
                 (gs_gain[:], d_in["gmlp_norm"].to_broadcast([P, GW])),
                 (router_b[:], d_in["router_b"].rearrange("(o n) -> o n", o=1).to_broadcast([P, NE])))
            for b in range(8, NB1):
                weight_block(b)

            expert_w = {"gate": d_in["w_expert_gate"], "up": d_in["w_expert_up"], "down": d_in["w_expert_down"]}

            def expert_loads(r, g):
                q = r * NG + g
                for n, (j, which, half) in enumerate(expert_block):
                    b = NB1 + n
                    sp.wait_ge(hi_done, q * GB + (b - E_RING + 1))
                    sp.wait_ge(lo_done, q * GB + (b - E_RING + 1))
                    if (n - E_RING) % GB in direct:
                        sp.wait_ge(mm_done, q * GB + (b - E_RING + 1))
                    w = expert_w[which][0, bass.ds(g * EPG + j, 1), :, :]
                    if which == "down":
                        src = w.rearrange("e (p t) n -> p (e t) n", t=4)[:, :, half * COLS:(half + 1) * COLS]
                    else:
                        src = w.rearrange("e (p t) n -> p (e t) n", t=KD)[:, 4 * half:4 * half + 4, :]
                    raw, landed, _ = e_slot(n)
                    sp.dma_start(raw[:, :].rearrange("p (t n) -> p t n", t=4), src).then_inc(landed, 16)

            sp.wait_ge(hi_done, NB1)
            sp.wait_ge(lo_done, NB1)
            sp.wait_ge(mm_done, first_block[C_V1 + 1])
            with sp.Fori(0, NG) as g:
                expert_loads(0, g)
            sp.wait_ge(s["rounds_ready"], 1)
            rounds = sp.value_load(n_rounds_i[0:1, 0:1], min_val=1, max_val=S // SLOTS)
            with sp.If(rounds > 1):
                with sp.Fori(1, rounds) as r:
                    with sp.Fori(0, NG) as g:
                        expert_loads(r, g)
            with sp.Else():
                sp.nop()
            for i in range(NT):
                sp.wait_ge(s["out_ready"], i + 1)
                sp.dma_start(out[0, i * P:(i + 1) * P, :], x_res[:, i, :]).then_inc(ld["out"], 16)
            sp.wait_ge(ld["out"], 16 * NT)

        @block.scalar
        def _(act):
            A = nc.scalar.activation

            def w_hi_part(b):
                act.wait_ge(w_in_slot[b % RING], 16 * (b // RING + 1))
                if b >= RING:
                    act.wait_ge(mm_done, b - RING + 1)
                A(bview(w_hi, b, blocks[b].shape), bview(w_raw, b, blocks[b].shape), ACT.Copy).then_inc(hi_done, 1)

            def w_chunk(c):
                for b in range(first_block[c], first_block[c + 1]):
                    w_hi_part(b)

            def acc(c, i, n=COLS):
                return ps[:, (c % 2) * 2 + i, 0:n]

            def move(c, *triples):
                act.wait_ge(mm_done, first_block[c + 1])
                for k, (dst, src, func, scale) in enumerate(triples):
                    ins = A(dst, src, func, scale=scale)
                ins.then_inc(ev_act, 1)

            def act_hi_part(n, banks, dst, gain=None, bank0=4):
                for hb in banks:
                    act.wait_ge(sT[n], hb + 1)
                    if gain is None:
                        ins = A(dst[:, 2 * hb:2 * hb + 2, :],
                                ps[:, bank0 + hb, :].rearrange("p (k s) -> p k s", k=2), ACT.Copy)
                    else:
                        for k in range(2):
                            ins = A(dst[:, 2 * hb + k, :], ps[:, bank0 + hb, k * S:(k + 1) * S], ACT.Copy,
                                    scale=gain[:, 2 * hb + k:2 * hb + k + 1])
                    ins.then_inc(sH[n], 1)

            def numer_out(h):
                act.wait_ge(s["pv_done"], h + 1)
                A(numer[:, :, h, 0:MDH + 1], ps[:, 6 + h % 2, :].rearrange("p (i n) -> p i n", i=NT)[:, :, 0:MDH + 1],
                  ACT.Copy).then_inc(s["numer_moved"], 1)

            def attn_out(u):
                jp, t, jo = u // 4, u // 2 % 2, u % 2
                if u >= 1:
                    act.wait_ge(s["a_pv"], u)
                for f, (lo, n) in enumerate(turn_fills[t]):
                    act.wait_ge(s["a_pturned"], fills_before[u] + f + 1)
                    A(pT[:, lo * P:(lo + n) * P], ps[:, 6, 0:n * P], ACT.Copy).then_inc(s["a_pmoved"], 1)
                if jo:
                    act.wait_ge(s["a_pv"], u + 1)
                    A(yb_hi[:, jp:jp + 5:2, t * P:(t + 1) * P], ps[:, 7, 0:AG * P].rearrange("p (g t) -> p g t", g=AG),
                      ACT.Copy).then_inc(s["a_yhi"], 1)

            for k in range(2):
                act_hi_part("x", range(2 * k, 2 * k + 2), act_hi, g_mix)
                w_hi_part(k)
            for i in range(NT):
                ins = A(junk_x[:, i, :], x_res[:, i, :], ACT.Square, accum_out=ss_x[:, i:i + 1])
            ins.then_inc(s_sq["x"], 1)
            w_chunk(1)
            act.wait_ge(s_rs["x"], 1)
            for c in range(2):
                move(c, *[(zq[:, i, c * MW:(c + 1) * MW], acc(c, i), ACT.Copy, rs_x[:, i:i + 1]) for i in range(NT)])
                w_chunk(c + 2)
            move(2, *[(vx[:, i, :, 0:MDH], acc(2, i).rearrange("p (h d) -> p h d", h=MH), ACT.Copy, rs_x[:, i:i + 1])
                      for i in range(NT)])
            w_chunk(4)
            act.wait_ge(s["vone"], 1)
            move(3, *[(zo[:, i, :], acc(3, i), ACT.Tanh, rsh_x[:, i:i + 1]) for i in range(NT)])
            w_chunk(5)
            act.wait_ge(s["aux"], 1)
            act.dma_start(scratch_rows, bias_row[:]).then_inc(ld["bias_rows"], 16)
            move(4, *[m for i in range(NT) for m in (
                (zif[:, i, :], acc(4, i)[:, 0:8], ACT.Copy, rs_x[:, i:i + 1]),
                (zqk[:, i, 0:256], acc(4, i)[:, 8:C_WIDE], ACT.Copy, rs_x[:, i:i + 1]))])
            for hb in range(4):
                act.wait_ge(s["qk_turned"], hb + 1)
                A(pre[:, 2 * hb:2 * hb + 2, 3:S + 3], ps[:, 4 + hb, :].rearrange("p (k s) -> p k s", k=2),
                  ACT.Copy).then_inc(s["conv_in"], 1)
            act.wait_ge(s["neg_abs"], 1)
            A(rows[:, 3, :], rows[:, 2, :], ACT.Exp)
            act.drain()
            A(rows[:, 4, :], rows[:, 3, :], ACT.Ln, bias=1.0).then_inc(s["log_done"], 1)
            w_chunk(6)

            def attn_in(c):
                lo = C_WIDE - 8 + (c - 5) * COLS
                out_ = []
                for i in range(NT):
                    nqk = min(COLS, max(0, 2 * AW - lo))
                    if nqk:
                        out_.append((zqk[:, i, lo:lo + nqk], acc(c, i)[:, 0:nqk], ACT.Copy, rs_x[:, i:i + 1]))
                    if nqk < COLS:
                        v0 = lo + nqk - 2 * AW
                        out_.append((zv[:, i, v0:v0 + COLS - nqk], acc(c, i)[:, nqk:COLS], ACT.Copy, rs_x[:, i:i + 1]))
                move(c, *out_)

            attn_in(5)
            w_chunk(7)
            act.wait_ge(s["decay_done"], 1)
            A(rows[:, 5, :], rows[:, 4, :], ACT.Exp, scale=-1.0).then_inc(s["floor_done"], 1)
            attn_in(6)
            w_chunk(8)
            act.wait_ge(s["conv_out"], 1)
            A(pre[:, :, 0:S], post[:], ACT.Tanh, scale=0.5).then_inc(s["tanh_qk"], 1)
            attn_in(7)
            act.wait_ge(ld["bias_rows"], 16)
            act.dma_start(bias_square, bias_shifted).then_inc(ld["bias_rows"], 16)

            def qk_squares(i):
                if i:
                    act.wait_ge(s["att_sq_read"], i)
                A(sq_s[:, 0:2 * AW], zqk[:, i, :], ACT.Square).then_inc(s_sq["att"], 1)

            def gmlp_in(c):
                move(c, *[(zg[:, i, (c - 9) * GW:(c - 8) * GW], acc(c, i), ACT.Copy, rs_x[:, i:i + 1])
                          for i in range(NT)])

            def gate_in(c):
                o = (c - 11) * COLS
                move(c, *[(tg[:, i, o:o + COLS], acc(c, i), ACT.Tanh, rsh_x[:, i:i + 1]) for i in range(NT)])

            w_chunk(9)
            act.wait_ge(ev_act, moved(7)[1])
            qk_squares(0)
            attn_in(8)
            w_chunk(10)
            qk_squares(1)
            gmlp_in(9)
            for b in range(22, 25):
                w_hi_part(b)
            act.wait_ge(s["silu_qk"], 1)
            act.wait_ge(s["cols_moved"], 1)
            for h in range(MH):
                act.wait_ge(s["decay_logit"], h + 1)
                if h >= 1:
                    act.wait_ge(s["prob_ready"], h)
                A(wgt[:, 0:2 * P], ps[:, 4, 0:2 * P], ACT.Exp, bias=aT[:, h:h + 1])
                A(wgt[:, 2 * P:3 * P], ps[:, 4, 2 * P:3 * P], ACT.Exp, bias=aT[:, MH + h:MH + h + 1]).then_inc(s["w_exp"], 1)
                if h == 0:
                    gmlp_in(10)
                else:
                    numer_out(h - 1)
                if h == 2:
                    gate_in(11)
                w_hi_part(25 + h)
            numer_out(MH - 1)
            act.wait_ge(ld["bias_rows"], 32)
            act.dma_start(toep[:], bias_square.rearrange("h p x -> p h x")).then_inc(ld["toep"], 16)
            act.wait_ge(s["numer_moved"], MH)
            act.wait_ge(s["att_sq_read"], NT)
            A(sq_s[:, 0:MH * NT * P].rearrange("p (i h d) -> p i h d", i=NT, h=MH), numer[:, :, :, 0:MDH],
              ACT.Square).then_inc(s_sq["mls"], 1)
            gate_in(12)
            A(zg[:], zg[:], ACT.Gelu_apprx_tanh).then_inc(s["gelu_done"], 1)
            act.wait_ge(s["gelu_done"], 1)
            A(sq_g[:], zg[:, :, GW:2 * GW], ACT.Square).then_inc(s_sq["gml"], 1)
            w_hi_part(29)
            act.wait_ge(s["numer_used"], 1)
            for n in range(6):
                if n == 4:
                    w_hi_part(30)
                act.wait_ge(s["aqk_turned"], n + 1)
                A(qkT[:, 2 * n:2 * n + 2, :], ps[:, 4 + n % 4, :].rearrange("p (k s) -> p k s", k=2), ACT.Copy,
                  scale=g_qk[:, n // 3:n // 3 + 1]).then_inc(s["aqk_moved"], 1)
            gate_in(13)

            def attn_exp(u):
                t = u // 2 % 2
                lg = (lg0, lg1)[u % 2]
                act.wait_ge(s["a_max"], u + 1)
                A(lg[:, :, 0:(t + 1) * P], lg[:, :, 0:(t + 1) * P], ACT.Exp, bias=a_nm[:, u:u + 1],
                  accum_out=a_sum[:, u:u + 1]).then_inc(s["a_exp"], 1)

            attn_exp(0)
            for u in range(8):
                if u < 7:
                    w_hi_part(31 + u)
                    attn_exp(u + 1)
                attn_out(u)
                if u in (1, 3, 5):
                    gate_in(14 + u // 2)
            act.wait_ge(s["a_pv"], 8)
            for i in range(NT):
                act.dma_start(mem_x[:, i, :], d_in["mem"][0, i * P:(i + 1) * P, :]).then_inc(ld["mem"], 16)
            w_hi_part(38)
            act_hi_part("a", range(2), ya_hi, g_mls)
            act_hi_part("c", range(2), yc_hi, bank0=6)
            w_hi_part(39)
            act.wait_ge(ld["mem"], 16 * NT)
            for i in range(NT):
                ins = A(junk_mem[:, i, :], mem_x[:, i, :], ACT.Square, accum_out=ss_mem[:, i:i + 1])
            ins.then_inc(s_sq["mem"], 1)
            w_hi_part(40)
            act_hi_part("mem", range(4), act_hi, g_mem)
            for b in range(41, 46):
                w_hi_part(b)
            act_hi_part("merged", range(2), mg_hi)
            w_hi_part(46)
            act_hi_part("merged", range(2, 4), mg_hi)
            act.wait_ge(s_rs["mem"], 1)
            move(C_K, *[(xkv[:, i, 0:XW], acc(C_K, i), ACT.Copy, rs_mem[:, i:i + 1]) for i in range(NT)])
            w_hi_part(47)
            act.wait_ge(*moved(C_K))
            A(sq_k[:], xkv[:, :, 0:XW], ACT.Square).then_inc(s_sq["xk"], 1)
            w_hi_part(48)
            w_hi_part(49)
            act_hi_part("x1", range(2), mg_hi, g_xat)
            w_hi_part(50)
            w_hi_part(51)
            act.wait_ge(*moved(C_OUT + 1))
            for i in range(NT):
                ins = A(junk_1[:, i, :], x_res[:, i, :], ACT.Square, accum_out=ss_1[:, i:i + 1])
            ins.then_inc(s_sq["x1"], 1)
            act_hi_part("x1", range(2, 4), mg_hi, g_xat)
            w_hi_part(52)
            w_hi_part(53)
            for hb in range(2):
                act.wait_ge(s["xk_turned"], hb + 1)
                A(xkT[:, 2 * hb:2 * hb + 2, :], ps[:, 6 + hb, :].rearrange("p (k s) -> p k s", k=2), ACT.Copy,
                  scale=g_xqk[:, 1:2]).then_inc(s["xk_moved"], 1)
            act.wait_ge(*moved(C_XQ))
            A(sq_q[:], xq[:], ACT.Square).then_inc(s_sq["xq"], 1)
            act.dma_start(router_w[:], d_in["router_w"].rearrange("(t p) e -> p t e", t=KD)).then_inc(ld["moe"], 16)
            act.dma_start(g_ffn_row[:], d_in["norm_ffn"].to_broadcast([P, D])).then_inc(ld["moe"], 16)
            move(C_V1, *[(xkv[:, i, XW:2 * XW], acc(C_V1, i), ACT.Copy, rs_mem[:, i:i + 1]) for i in range(NT)])
            for hb in range(2):
                act.wait_ge(s["xq_turned"], hb + 1)
                A(xqT[:, 2 * hb:2 * hb + 2, :], ps[:, 4 + hb, :].rearrange("p (k s) -> p k s", k=2), ACT.Copy,
                  scale=g_xqk[:, 0:1]).then_inc(s["xq_moved"], 1)
            for v in range(2 * NT):
                act.wait_ge(s["x_max"], v + 1)
                for k in range(2):
                    ins = A(xp[:, v // 2, (v % 2 * 2 + k) * S:(v % 2 * 2 + k + 1) * S], ps[:, 4 + v, k * S:(k + 1) * S],
                            ACT.Exp, scale=XDH ** -0.5, bias=x_nm[:, 2 * v + k:2 * v + k + 1],
                            accum_out=x_sum[:, 2 * v + k:2 * v + k + 1])
                ins.then_inc(s["x_exp"], 1)
            for t in range(NT):
                for hb in range(2):
                    act.wait_ge(s["x_pturned"], 2 * t + hb + 1)
                    A(xpT[:, 2 * hb:2 * hb + 2, :, t * P:(t + 1) * P],
                      ps[:, 4 + 2 * t + hb, :].rearrange("p (h m t) -> p h m t", h=2, m=NT), ACT.Copy).then_inc(s["x_pmoved"], 1)
            act_hi_part("o", range(2), oT_hi)

            def e_hi(q, n):
                b, nt = NB1 + n, 4 - direct.get(n % GB, 0)
                raw, landed, nth = e_slot(n)
                act.wait_ge(landed, 16 * (GB // E_RING) * q + 16 * nth)
                act.wait_ge(mm_done, GB * q + (b - RING + 1))
                A(w_hi[:, b % RING, 0:nt * COLS], raw[:, 0:nt * COLS], ACT.Copy).then_inc(hi_done, 1)

            for n in range(2):
                e_hi(0, n)

            act.wait_ge(*moved(C_XO))

            def x2_out(hb):
                act.wait_ge(sT["x2"], hb + 1)
                for k in range(2):
                    ins = A(x2T[:, 2 * hb + k, :], ps[:, 4 + hb, k * S:(k + 1) * S], ACT.Copy,
                            scale=g_ffn[:, 2 * hb + k:2 * hb + k + 1])
                ins.then_inc(s["x2T_moved"], 1)

            x2_out(0)
            x2_out(1)
            act.wait_ge(*moved(C_XO + 1))
            for i in range(NT):
                ins = A(h_full[:, i, :], x_res[:, i, :], ACT.Square, accum_out=ss_2[:, i:i + 1])
            ins.then_inc(s_sq["x2"], 1)
            x2_out(2)
            x2_out(3)
            act.wait_ge(s["h_full_done"], 1)
            A(h_hi[:].rearrange("q i (t p) -> q i t p", t=KD), h_full[:].rearrange("q i (p t) -> q i t p", t=KD),
              ACT.Copy).then_inc(s["h_hi_done"], 1)
            act.wait_ge(s["r_max"], 1)
            A(prob[:], prob[:], ACT.Exp).then_inc(s["r_exp"], 1)
            for n in range(2, RING):
                e_hi(0, n)

            act.wait_ge(s["rounds_ready"], 1)
            rounds = act.value_load(n_rounds_i[0:1, 0:1], min_val=1, max_val=S // SLOTS)

            def gathered(q, tiles):
                for t in tiles:
                    act.wait_ge(s["gath_pe"], FREE + KD * q + (t + 1))
                    A(xg[:, t, :, :].rearrange("p e (w c) -> p w e c", w=2),
                      ps[:, t % 2, :].rearrange("p (w e c) -> p w e c", w=2, e=EPG), ACT.Copy).then_inc(s["gath_moved"], 1)

            def y_hi_part(q, m, j):
                act.wait_ge(mm_done, GB * q + (NB1 + 2 * m + 2))
                act.wait_ge(s["scat_pe"], FREE + EPG * q + j)
                for half in range(2):
                    ins = A(y_hi[:, half * COLS:(half + 1) * COLS], ps[:, 2 + half, :], ACT.Copy, scale=w_slot[:, j:j + 1])
                ins.then_inc(s["yhi_done"], 1)

            def expert_group(q, more):
                for m, (j, which) in enumerate(ex_order[:-1]):
                    for n in split_steps(m, more, ahead=1):
                        e_hi(q, n)
                    if which == "gate":
                        act.wait_ge(mm_done, GB * q + (NB1 + 2 * m + 2))
                        A(gu[:, 0, :], ps[:, 0, :], ACT.Copy).then_inc(s["gu_moved"], 1)
                        if j == 0:
                            for half in range(2):
                                act.wait_ge(s["selT_pe"], FREE + 2 * q + (half + 1))
                                A(selT[:, 2 * half:2 * half + 2, :], ps[:, 2 + half, :].rearrange("p (e t) -> p e t", e=2),
                                  ACT.Copy).then_inc(s["selT_done"], 1)
                    elif which == "up":
                        act.wait_ge(mm_done, GB * q + (NB1 + 2 * m + 2))
                        A(gu[:, 1, :], ps[:, 1, :], ACT.Copy).then_inc(s["gu_moved"], 1)
                        act.wait_ge(s["et_pe"], EPG * q + (j + 1))
                        A(e_act[:, 0], ps[:, 2, :].rearrange("p (k c) -> p k c", c=P)[:, :, 0:SLOTS], ACT.Tanh,
                          scale=0.5).then_inc(s["et_tanh"], 1)
                    else:
                        y_hi_part(q, m, j)
                for k, n in enumerate(split_steps(len(ex_order) - 1, True, ahead=1)):
                    if more:
                        gathered(q + 1, (2 * k, 2 * k + 1))
                        e_hi(q, n)
                y_hi_part(q, len(ex_order) - 1, EPG - 1)
                if more:
                    gathered(q + 1, range(KD // 2, KD))
                for n in split_steps(len(ex_order), more, ahead=1):
                    e_hi(q, n)

            for name in ("yhi_done", "gu_moved"):
                act.drain().then_inc(s[name], FREE)
            with act.Fori(0, rounds) as r:
                gathered(r * NG, range(KD))
                with act.If(r > 0):
                    for n in range(RING):
                        e_hi(r * NG, n)
                with act.Fori(0, NG - 1) as g:
                    expert_group(r * NG + g, True)
                expert_group(r * NG + (NG - 1), False)

        @block.gpsimd
        def _(pool):
            def rsqrt(n, dst, src, w):
                pool.wait_ge(s_ms[n], 1)
                nc.gpsimd.tensor_tensor(dst, src, minus_half[:, 0:w], ALU.pow).then_inc(s_rs[n], 1)

            pool.wait_ge(ld["const"], 16)
            rsqrt("x", rs_x, ss_x, 2)
            rsqrt("att", rs_a, ss_a, 48)
            rsqrt("mls", rs_m, ss_m, 8)
            rsqrt("gml", rs_g, ss_g, 8)
            rsqrt("mem", rs_mem, ss_mem, 2)
            rsqrt("xk", rs_k, ss_k, 8)
            rsqrt("x1", rs_1, ss_1, 2)
            rsqrt("xq", rs_q, ss_q, 8)
            rsqrt("x2", rs_2, ss_2, 2)
            pool.wait_ge(s["h_hi_done"], 1)
            nc.gpsimd.tensor_tensor(h_lo[:].rearrange("q i (t p) -> q i t p", t=KD),
                                    h_full[:].rearrange("q i (p t) -> q i t p", t=KD),
                                    f32(h_hi[:]).rearrange("q i (t p) -> q i t p", t=KD),
                                    ALU.subtract).then_inc(s["h_lo_done"], 1)

        @block.vector
        def _(dve):
            V = nc.vector

            def w_lo_part(b):
                dve.wait_ge(hi_done, b + 1)
                if b >= RING:
                    dve.wait_ge(mm_done, b - RING + 1)
                sh = blocks[b].shape
                V.tensor_tensor(bview(w_lo, b, sh), bview(w_raw, b, sh), f32(bview(w_hi, b, sh)),
                                ALU.subtract).then_inc(lo_done, 1)

            def w_chunk(c):
                for b in range(first_block[c], first_block[c + 1]):
                    w_lo_part(b)

            def act_lo_part(n, banks, dst, hi, gain=None, bank0=4):
                for hb in banks:
                    dve.wait_ge(sH[n], hb + 1)
                    if gain is None:
                        ins = V.tensor_tensor(dst[:, 2 * hb:2 * hb + 2, :],
                                              ps[:, bank0 + hb, :].rearrange("p (k s) -> p k s", k=2),
                                              f32(hi[:, 2 * hb:2 * hb + 2, :]), ALU.subtract)
                    else:
                        for k in range(2):
                            ins = V.scalar_tensor_tensor(dst[:, 2 * hb + k, :], ps[:, bank0 + hb, k * S:(k + 1) * S],
                                                         gain[:, 2 * hb + k:2 * hb + k + 1], f32(hi[:, 2 * hb + k, :]),
                                                         ALU.mult, ALU.subtract)
                    ins.then_inc(sL[n], 1)

            def mean_square(n, ss, width, sq_=None):
                dve.wait_ge(s_sq[n], 1)
                if sq_ is not None:
                    V.reduce_sum(ss, sq_, AX.X)
                    dve.drain()
                V.tensor_scalar(ss, ss, 1.0 / width, EPS, ALU.mult, ALU.add).then_inc(s_ms[n], 1)

            def acc(c, i, n=COLS):
                return ps[:, (c % 2) * 2 + i, 0:n]

            def by_row(v, n, m):
                return bc(v.unsqueeze(2), (P, n, m))

            for k in range(2):
                act_lo_part("x", range(2 * k, 2 * k + 2), act_lo, act_hi, g_mix)
                w_lo_part(k)
            mean_square("x", ss_x, D)
            w_chunk(1)
            V.memset(vx[:, :, :, MDH:MDH + 2], 1.0)
            V.memset(pre[:, :, 0:3], 0.0).then_inc(s["pad_ready"], 1)
            dve.wait_ge(s_rs["x"], 1)
            V.tensor_scalar(rsh_x, rs_x, 0.5, None, ALU.mult).then_inc(s["vone"], 1)
            w_chunk(2)
            w_chunk(3)
            dve.wait_ge(ld["aux"], 192)
            dve.wait_ge(ld["const"], 16)
            V.memset(table[REL_BUCKETS:REL_BUCKETS + 1, :], NEG)
            V.tensor_tensor(ws_t[:], ws_t[:], bc(keep_past.unsqueeze(1), (P, GG, P)), ALU.mult).then_inc(s["zeros_set"], 1)
            w_chunk(4)
            dve.wait_ge(s["aux_pe"], 1)
            V.tensor_copy(cw[:], ps[:, 4, 0:32])
            V.tensor_copy(vec_cols[:], ps[:, 4, 32:40 + 2 * KD])
            V.tensor_copy(wT[:], ps[:, 5, :].rearrange("p (g t) -> p g t", g=GG))
            V.tensor_copy(bias_row[:, 0, :], ps[0:AHG, 6, 0:TOEP])
            V.tensor_copy(bias_row[:, 1, :], ps[0:AHG, 7, 0:TOEP])
            V.tensor_copy(bias_row[:, 2, :], ps[0:AHG, 4, P:P + TOEP]).then_inc(s["aux"], 1)
            w_chunk(5)
            dve.wait_ge(s["gates_turned"], 1)
            V.memset(rows[:, 5, :], 1.0)
            V.tensor_scalar(rows[:, 0, :], ps[0:MH, 4, 0:S], gate_bi[:], None, ALU.add)
            V.tensor_scalar(rows[:, 1, :], ps[0:MH, 4, S:2 * S], gate_bf[:], None, ALU.add)
            dve.drain()
            V.scalar_tensor_tensor(rows[:, 2, :], rows[:, 1, :], -1.0, rows[:, 1, :], ALU.mult, ALU.min).then_inc(s["neg_abs"], 1)
            w_chunk(6)
            dve.wait_ge(s["log_done"], 1)
            V.scalar_tensor_tensor(rows[:, 1, :], rows[:, 1, :], 0.0, rows[:, 4, :], ALU.min, ALU.subtract)
            dve.drain()
            V.tensor_tensor_scan(rows[:, 2, :], rows[:, 5, :], rows[:, 1, :], 0.0, ALU.mult, ALU.add)
            dve.drain()
            V.tensor_tensor(rows[:, 0, :], rows[:, 0, :], rows[:, 2, :], ALU.subtract)
            dve.drain()
            V.tensor_tensor_scan(rows[:, 3, :], rows[:, 5, :], rows[:, 0, :], 0.0, ALU.mult, ALU.max)
            dve.drain()
            V.tensor_tensor(rows[:, 4, :], rows[:, 2, :], rows[:, 3, :], ALU.add).then_inc(s["decay_done"], 1)
            w_chunk(7)
            dve.wait_ge(s["conv_in"], 4)

            def tap(w):
                for f in range(KD):
                    c = cw[:, w * KD + f:w * KD + f + 1]
                    if w == 0:
                        ins = V.tensor_scalar(post[:, f, :], pre[:, f, 0:S], c, None, ALU.mult)
                    else:
                        ins = V.scalar_tensor_tensor(post[:, f, :], pre[:, f, w:w + S], c, post[:, f, :], ALU.mult, ALU.add)
                return ins

            tap(0)
            dve.drain()
            tap(1)
            w_chunk(8)
            dve.drain()
            tap(2)
            dve.drain()
            tap(3).then_inc(s["conv_out"], 1)
            w_chunk(9)
            dve.wait_ge(s["cols_turned"], 1)
            V.tensor_copy(stat[:, st_at["aT"][0]:st_at["aT"][0] + 16], ps[:, 5, 0:16]).then_inc(s["cols_moved"], 1)
            dve.wait_ge(s["tanh_qk"], 1)
            V.scalar_tensor_tensor(post[:], pre[:, :, 0:S], 1.0, post[:], ALU.add, ALU.mult).then_inc(s["silu_qk"], 1)
            w_chunk(10)
            for i in range(NT):
                dve.wait_ge(s_sq["att"], i + 1)
                V.reduce_sum(ss_a[:, 24 * i:24 * i + 24], sq_s[:, 0:2 * AW].rearrange("p (n d) -> p n d", d=ADH),
                             AX.X).then_inc(s["att_sq_read"], 1)
            dve.drain()
            V.tensor_scalar(ss_a, ss_a, 1.0 / ADH, EPS, ALU.mult, ALU.add).then_inc(s_ms["att"], 1)
            for b in range(22, 25):
                w_lo_part(b)
            for h in range(MH):
                dve.wait_ge(s["score"], h + 1)
                dve.wait_ge(s["w_exp"], h + 1)
                if h >= 2:
                    dve.wait_ge(s["pv_done"], h - 1)
                V.scalar_tensor_tensor(pm[:, h % 2, :], ps[:, 5, 0:3 * P], 0.25 * MDH ** -0.5, wgt[:], ALU.mult,
                                       ALU.mult).then_inc(s["prob_ready"], 1)
                w_lo_part(25 + h)
                if h == 0:
                    dve.wait_ge(s_rs["att"], 1)
                    zqk48 = zqk[:].rearrange("p i (n d) -> p (i n) d", d=ADH)
                    V.tensor_tensor(zqk48, zqk48, by_row(rs_a, 48, ADH), ALU.mult).then_inc(s["aqk_ready"], 1)
            dve.wait_ge(s["numer_moved"], MH)
            dn = numer[:, :, :, MDH]
            v8 = lambda v: v.rearrange("p (i h) -> p i h", i=NT)
            V.scalar_tensor_tensor(v8(den), dn, -1.0, dn, ALU.mult, ALU.max)
            zo8 = zo[:].rearrange("p i (h d) -> p (i h) d", d=MDH)
            V.scalar_tensor_tensor(zo8, zo8, 1.0, numer[:].rearrange("p i h d -> p (i h) d")[:, :, 0:MDH], ALU.add,
                                   ALU.mult).then_inc(s["numer_used"], 1)
            dve.drain()
            V.tensor_tensor(den, den, emT, ALU.max)
            dve.drain()
            V.reciprocal(rden, den)
            dve.wait_ge(s_sq["mls"], 1)
            V.reduce_sum(ss_m, sq_s[:, 0:NT * MW].rearrange("p (n d) -> p n d", d=MDH), AX.X)
            dve.drain()
            V.tensor_tensor(ss_m, ss_m, rden, ALU.mult)
            dve.drain()
            V.tensor_tensor(ss_m, ss_m, rden, ALU.mult)
            dve.drain()
            V.tensor_scalar(ss_m, ss_m, 1.0 / MDH, EPS, ALU.mult, ALU.add).then_inc(s_ms["mls"], 1)
            mean_square("gml", ss_g, GC, sq_g[:].rearrange("p i (n d) -> p (i n) d", d=GC))
            w_lo_part(29)
            dve.wait_ge(s_rs["mls"], 1)
            V.scalar_tensor_tensor(den, rden, 0.5, rs_m, ALU.mult, ALU.mult)
            dve.drain()
            V.tensor_tensor(zo8, zo8, by_row(den, NT * MH, MDH), ALU.mult).then_inc(s["ya_done"], 1)
            dve.wait_ge(s_rs["gml"], 1)
            for i in range(NT):
                gv = zg[:, i, GW:2 * GW].rearrange("p (n d) -> p n d", d=GC)
                V.tensor_tensor(gv, gv, by_row(rs_g[:, GG * i:GG * i + GG], GG, GC), ALU.mult)
            dve.drain()
            dve.wait_ge(ld["small"], 16 * 4)
            for i in range(NT):
                ins = V.tensor_tensor(zg[:, i, GW:2 * GW], zg[:, i, GW:2 * GW], gs_gain[:], ALU.mult)
            ins.then_inc(s["gv_ready"], 1)
            w_lo_part(30)
            dve.wait_ge(ld["toep"], 16)

            def attn_logits(u):
                jp, t, jo = u // 4, u // 2 % 2, u % 2
                j, w = 2 * jp + jo, (t + 1) * P
                lg = (lg0, lg1)[u % 2]
                dve.wait_ge(s["a_logit"], u + 1)
                if u >= 2:
                    dve.wait_ge(s["a_pturned"], fills_before[u - 1])
                else:
                    dve.wait_ge(s["aqk_moved"], 6)
                heads = toep[:, :, P * (1 - t):P * (1 - t) + w]
                V.scalar_tensor_tensor(lg[:, 0:2, 0:w], ps[:, 4, :].rearrange("p (g x) -> p g x", g=2)[:, :, 0:w],
                                       ADH ** -0.5, heads[:, j:j + 5:4, :], ALU.mult, ALU.add)
                V.scalar_tensor_tensor(lg[:, 2, 0:w], ps[:, 5, 0:w], ADH ** -0.5, heads[:, 8 + j, :], ALU.mult,
                                       ALU.add).then_inc(s["a_logit_moved"], 1)
                dve.drain()
                V.tensor_reduce(a_nm[:, u:u + 1], lg[:, :, 0:w], AX.XY, ALU.max, negate=True).then_inc(s["a_max"], 1)

            def attn_norm(u):
                t = u // 2 % 2
                lg = (lg0, lg1)[u % 2]
                dve.wait_ge(s["a_exp"], u + 1)
                V.reciprocal(a_rec[:, u:u + 1], a_sum[:, u:u + 1])
                dve.drain()
                V.tensor_scalar(lg[:, :, 0:(t + 1) * P], lg[:, :, 0:(t + 1) * P], a_rec[:, u:u + 1], None,
                                ALU.mult).then_inc(s["a_norm"], 1)

            def attn_lo(u):
                jp, t, jo = u // 4, u // 2 % 2, u % 2
                dve.wait_ge(s["a_yhi"], u // 2 + 1)
                V.tensor_tensor(yb_lo[:, jp:jp + 5:2, t * P:(t + 1) * P],
                                ps[:, 7, 0:AG * P].rearrange("p (g t) -> p g t", g=AG),
                                f32(yb_hi[:, jp:jp + 5:2, t * P:(t + 1) * P]), ALU.subtract).then_inc(s["a_ylo"], 1)

            attn_logits(0)
            for n in range(NT):
                dve.wait_ge(s["g_mixed"], n + 1)
                for g in range(GG):
                    u_ = zg[:, n, g * GC:(g + 1) * GC]
                    ins = V.scalar_tensor_tensor(u_, ps[:, 6 + n, g * GC:(g + 1) * GC], gs_b[:, g:g + 1], u_, ALU.add, ALU.mult)
                ins.then_inc(s["yc_done"], 1)
            attn_norm(0)
            for u in range(8):
                if u < 7:
                    attn_logits(u + 1)
                    w_lo_part(31 + u)
                    attn_norm(u + 1)
                if u % 2:
                    attn_lo(u)

            def branch(c):
                k, n = {C_B: 1, C_A: 0, C_C: 2}[c - (c - C_B) % 2], (c - C_B) % 2
                dve.wait_ge(mm_done, first_block[c + 1])
                for i in range(NT):
                    t_ = tg[:, i, k * D + n * COLS:k * D + (n + 1) * COLS]
                    ins = V.scalar_tensor_tensor(t_, t_, 1.0, acc(c, i), ALU.add, ALU.mult)
                ins.then_inc(ev_dve, 1)
                if c >= C_A:
                    other = 2 if k else 1
                    dve.drain()
                    for i in range(NT):
                        m_ = merged[:, i, n * COLS:(n + 1) * COLS]
                        ins = V.tensor_tensor(m_, m_, tg[:, i, other * D + n * COLS:other * D + (n + 1) * COLS], ALU.add)
                    if k == 2:
                        ins.then_inc(s["merged_ready"], 1)
                    dve.drain()

            def residual_add(c, n, scale):
                dve.wait_ge(mm_done, first_block[c + 1])
                for i in range(NT):
                    x_ = x_res[:, i, n * COLS:(n + 1) * COLS]
                    ins = V.scalar_tensor_tensor(x_, acc(c, i), scale, x_, ALU.mult, ALU.add)
                ins.then_inc(ev_dve, 1)

            w_lo_part(38)
            act_lo_part("a", range(2), ya_lo, ya_hi, g_mls)
            act_lo_part("c", range(2), yc_lo, yc_hi, bank0=6)
            branch(C_B)
            w_lo_part(39)
            mean_square("mem", ss_mem, D)
            w_lo_part(40)
            branch(C_B + 1)
            act_lo_part("mem", range(4), act_lo, act_hi, g_mem)
            w_lo_part(41)
            branch(C_A)
            w_lo_part(42)
            branch(C_A + 1)
            w_lo_part(43)
            branch(C_C)
            w_lo_part(44)
            branch(C_C + 1)
            w_lo_part(45)
            act_lo_part("merged", range(2), mg_lo, mg_hi)
            w_lo_part(46)
            act_lo_part("merged", range(2, 4), mg_lo, mg_hi)
            w_lo_part(47)
            mean_square("xk", ss_k, XDH, sq_k[:].rearrange("p i (h d) -> p (i h) d", d=XDH))
            w_lo_part(48)
            dve.wait_ge(s_rs["xk"], 1)
            for i in range(NT):
                kk = xkv[:, i, 0:XW].rearrange("p (n d) -> p n d", d=XDH)
                ins = V.tensor_tensor(kk, kk, by_row(rs_k[:, XH * i:XH * i + XH], XH, XDH), ALU.mult)
            ins.then_inc(s["xk_ready"], 1)
            residual_add(C_OUT, 0, 0.5)
            w_lo_part(49)
            act_lo_part("x1", range(2), mg_lo, mg_hi, g_xat)
            w_lo_part(50)
            residual_add(C_OUT + 1, 1, 0.5)
            w_lo_part(51)
            mean_square("x1", ss_1, D)
            act_lo_part("x1", range(2, 4), mg_lo, mg_hi, g_xat)
            w_lo_part(52)
            w_lo_part(53)
            dve.wait_ge(s_rs["x1"], 1)
            dve.wait_ge(mm_done, first_block[C_XQ + 1])
            for i in range(NT):
                ins = V.tensor_scalar(xq[:, i, :], acc(C_XQ, i), rs_1[:, i:i + 1], None, ALU.mult)
            ins.then_inc(ev_dve, 1)
            dve.wait_ge(*moved(C_XQ))
            mean_square("xq", ss_q, XDH, sq_q[:].rearrange("p i (h d) -> p (i h) d", d=XDH))
            dve.wait_ge(s_rs["xq"], 1)
            qv = xq[:].rearrange("p i (h d) -> p (i h) d", d=XDH)
            V.tensor_tensor(qv, qv, by_row(rs_q, NT * XH, XDH), ALU.mult).then_inc(s["xq_scaled"], 1)

            def x_maxima(v):
                dve.wait_ge(s["x_logit"], v + 1)
                nm = x_nm[:, 2 * v:2 * v + 2]
                V.reduce_max(nm, ps[:, 4 + v, :].rearrange("p (h m) -> p h m", h=2), AX.X)
                dve.drain()
                V.tensor_scalar(nm, nm, -(XDH ** -0.5), None, ALU.mult).then_inc(s["x_max"], 1)

            def x_normalise(v):
                dve.wait_ge(s["x_exp"], v + 1)
                V.reciprocal(x_rec[:, 2 * v:2 * v + 2], x_sum[:, 2 * v:2 * v + 2])
                dve.drain()
                pv_ = xp[:, v // 2, v % 2 * 2 * S:(v % 2 + 1) * 2 * S].rearrange("p (h m) -> p h m", h=2)
                V.tensor_tensor(pv_, pv_, by_row(x_rec[:, 2 * v:2 * v + 2], 2, S), ALU.mult).then_inc(s["x_norm"], 1)

            x_maxima(0)
            x_maxima(1)
            for v in range(2 * NT):
                if v + 2 < 2 * NT:
                    x_maxima(v + 2)
                x_normalise(v)
            act_lo_part("o", range(2), oT_lo, oT_hi)
            V.memset(zeros, 0.0).then_inc(s["zeros"], 1)

            def e_lo(q, n):
                b, nt = NB1 + n, 4 - direct.get(n % GB, 0)
                dve.wait_ge(hi_done, GB * q + (b + 1))
                V.tensor_tensor(w_lo[:, b % RING, 0:nt * COLS], e_slot(n)[0][:, 0:nt * COLS], f32(w_hi[:, b % RING, 0:nt * COLS]),
                                ALU.subtract).then_inc(lo_done, 1)

            for k in range(2):
                e_lo(0, k)
            for n in range(2):
                residual_add(C_XO + n, n, 1.0)
            dve.wait_ge(*moved(C_XO + 1))

            mean_square("x2", ss_2, D)
            dve.wait_ge(s_rs["x2"], 1)
            dve.wait_ge(ld["moe"], 32)
            for i in range(NT):
                ins = V.scalar_tensor_tensor(h_full[:, i, :], x_res[:, i, :], rs_2[:, i:i + 1], g_ffn_row[:], ALU.mult, ALU.mult)
            ins.then_inc(s["h_full_done"], 1)
            dve.wait_ge(s["r_logit"], 1)
            v2 = lambda v: v.rearrange("p (i e) -> p i e", i=NT)
            v84 = lambda v: v.rearrange("p (n e) -> p n e", e=EPG)
            v24 = lambda v: v.rearrange("p (i g) -> p i g", g=NG)

            def two(v, n):
                return bc(v.unsqueeze(2), (P, NT, n))

            for i in range(NT):
                V.scalar_tensor_tensor(prob[:, i * NE:(i + 1) * NE], ps[:, 2 + i, 0:NE], rs_2[:, i:i + 1],
                                       router_b[:], ALU.mult, ALU.add)
            dve.drain()
            V.reduce_max(rmax, v2(prob), AX.X)
            dve.drain()
            V.tensor_tensor(v2(prob), v2(prob), two(rmax, NE), ALU.subtract).then_inc(s["r_max"], 1)
            dve.wait_ge(s["r_exp"], 1)
            V.reduce_sum(rsum, v2(prob), AX.X)
            dve.drain()
            V.reciprocal(rrec, rsum)
            dve.drain()
            V.tensor_tensor(v2(prob), v2(prob), two(rrec, NE), ALU.mult)
            dve.drain()
            four = (P, NT * NG, EPG, EPG)
            p_i, p_j = bc(v84(prob).unsqueeze(2), four), bc(v84(prob).unsqueeze(3), four)
            m4 = lambda v: v.rearrange("p (n j i) -> p n j i", j=EPG, i=EPG)
            V.tensor_tensor(m4(gt), p_i, p_j, ALU.is_gt)
            V.tensor_tensor(m4(ge), p_i, p_j, ALU.is_ge)
            dve.drain()
            V.tensor_tensor(ge, ge, gt, ALU.subtract)
            dve.drain()
            V.tensor_tensor(m4(ge), m4(ge), bc(tie.unsqueeze(1), four), ALU.mult)
            dve.drain()
            V.tensor_tensor(gt, gt, ge, ALU.add)
            dve.drain()
            V.reduce_sum(v84(rank), m4(gt), AX.X)
            dve.drain()
            V.scalar_tensor_tensor(r2, rank, 2.0, prob, ALU.is_lt, ALU.mult)
            dve.drain()
            V.reduce_sum(score, v84(r2), AX.X)
            dve.drain()
            V.reduce_max(best, v24(score), AX.X)
            V.memset(earlier, 0.0)
            dve.drain()
            V.tensor_tensor(v24(eq), v24(score), two(best, NG), ALU.is_equal)
            dve.drain()
            for g in range(1, NG):
                V.tensor_tensor(v24(earlier)[:, :, g], v24(earlier)[:, :, g - 1], v24(eq)[:, :, g - 1], ALU.add)
                dve.drain()
            V.scalar_tensor_tensor(first, earlier, 0.0, eq, ALU.is_equal, ALU.mult)
            dve.drain()
            one_group = bc(first.unsqueeze(2), (P, NT * NG, EPG))
            V.tensor_tensor(v84(topw), v84(r2), one_group, ALU.mult)
            V.scalar_tensor_tensor(v84(chosen), v84(rank), 2.0, one_group, ALU.is_lt, ALU.mult).then_inc(s["chosen"], 1)
            dve.drain()
            V.reduce_sum(rsum, v2(topw), AX.X)
            dve.drain()
            V.reciprocal(rrec, rsum)
            dve.drain()
            V.tensor_tensor(v2(gates), v2(topw), two(rrec, NE), ALU.mult)
            dve.wait_ge(s["pos_pe"], 1)
            V.scalar_tensor_tensor(posm, ps[:, 1, 0:NT * NE], 1.0, chosen, ALU.add, ALU.mult)
            V.reduce_max(total[:, 0:1], ps[:, 1, NT * NE:NT * NE + NE], AX.X)
            dve.drain()
            V.tensor_scalar(posm, posm, -1.0, None, ALU.add)
            V.tensor_scalar(total[:, 1:2], total[:, 0:1], float(SLOTS), 1.0, ALU.is_gt, ALU.add)
            dve.drain()
            for k in range(2, S // SLOTS):
                V.scalar_tensor_tensor(total[:, 1:2], total[:, 0:1], float(k * SLOTS), total[:, 1:2], ALU.is_gt, ALU.add)
                dve.drain()
            V.tensor_copy(n_rounds_i[:], total[0:1, 1:2]).then_inc(s["rounds_ready"], 1)

            dve.wait_ge(s["rounds_ready"], 1)
            rounds = dve.value_load(n_rounds_i[0:1, 0:1], min_val=1, max_val=S // SLOTS)

            def select(q, g):
                dve.wait_ge(s["gath_pe"], FREE + KD * q)
                dve.wait_ge(s["selT_pe"], FREE + 2 * q)
                for i in range(NT):
                    V.tensor_copy(gcur[:, i * EPG:(i + 1) * EPG], v2(gates)[:, i, bass.ds(g * EPG, EPG)])
                    ins = V.tensor_tensor(sel[:, i], bc(iota.unsqueeze(1), (P, EPG, P)),
                                          bc(v2(posm)[:, i, bass.ds(g * EPG, EPG)].unsqueeze(2), (P, EPG, P)), ALU.is_equal)
                ins.then_inc(s["selected"], 1)

            def slot_gates(q):
                dve.wait_ge(s["wslot_pe"], q + 1)
                V.tensor_copy(w_slot_next[:], ps[:, 1, 0:EPG * EPG:EPG + 1]).then_inc(s["wslot_moved"], 1)

            def y_lo_part(q, j):
                dve.wait_ge(s["yhi_done"], FREE + EPG * q + (j + 1))
                for half in range(2):
                    cs = slice(half * COLS, (half + 1) * COLS)
                    ins = V.scalar_tensor_tensor(y_lo[:, cs], ps[:, 2 + half, :], w_slot[:, j:j + 1], f32(y_hi[:, cs]),
                                                 ALU.mult, ALU.subtract)
                ins.then_inc(s["ylo_done"], 1)

            def expert_group(q, g, more):
                dve.drain()
                dve.wait_ge(s["yhi_done"], FREE + EPG * q)
                V.tensor_copy(w_slot[:], w_slot_next[:])
                for m, (j, which) in enumerate(ex_order[:-1]):
                    for n in split_steps(m, more):
                        e_lo(q, n)
                    if which == "up":
                        kc = lambda v: v.rearrange("p (k c) -> p k c", c=P)[:, :, 0:SLOTS]
                        dve.wait_ge(s["et_tanh"], EPG * q + (j + 1))
                        V.scalar_tensor_tensor(e_act[:, 1], e_act[:, 0], 1.0, kc(ps[:, 2, :]), ALU.add, ALU.mult)
                        dve.drain()
                        V.tensor_tensor(e_act[:, 1], e_act[:, 1], kc(ps[:, 3, :]), ALU.mult)
                        dve.drain()
                        dve.wait_ge(mm_done, GB * q + (NB1 + (ex_block[j - 1, "down"] + 2 if j else 0)))
                        V.tensor_copy(a_st[:, :, 0:SLOTS], e_act[:, 1])
                        dve.drain()
                        V.tensor_tensor(a_st[:, :, SLOTS:P], e_act[:, 1], f32(a_st[:, :, 0:SLOTS]),
                                        ALU.subtract).then_inc(s["a_ready"], 1)
                    elif which == "down":
                        y_lo_part(q, j)
                        if more and j == 1:
                            select(q + 1, g + 1)
                if more:
                    slot_gates(q + 1)
                for n in split_steps(len(ex_order) - 1, more):
                    e_lo(q, n)
                y_lo_part(q, EPG - 1)
                for n in split_steps(len(ex_order), more):
                    e_lo(q, n)

            select(0, 0)
            dve.drain().then_inc(s["ylo_done"], FREE)
            with dve.Fori(0, rounds) as r:
                slot_gates(r * NG)
                with dve.If(r > 0):
                    for n in range(RING):
                        e_lo(r * NG, n)
                with dve.Else():
                    for n in range(2, RING):
                        e_lo(0, n)
                with dve.Fori(0, NG - 1) as g:
                    expert_group(r * NG + g, g, True)
                expert_group(r * NG + (NG - 1), NG - 1, False)
                V.tensor_scalar(iota, iota, float(SLOTS), None, ALU.add)
                dve.drain()
                select(r * NG + NG, 0)
            dve.wait_ge(s["moe_done"], 1)
            for i in range(NT):
                for half in range(2):
                    x_ = x_res[:, i, half * COLS:(half + 1) * COLS]
                    ins = V.scalar_tensor_tensor(x_, ps[:, 4 + 2 * i + half, :], 0.5, x_, ALU.mult, ALU.add)
                ins.then_inc(s["out_ready"], 1)

        @block.tensor
        def _(pe):
            MM = nc.tensor.matmul

            def turn(dst, src, n):
                return nc.tensor.transpose(dst, src, ident[0:n, 0:n])

            def turn_act(name, src, nt, banks, tiled=False, bank0=4):
                for hb in banks:
                    for k in range(2):
                        f = 2 * hb + k
                        for i in range(NT):
                            ins = turn(ps[:, bank0 + hb, (k * NT + i) * P:(k * NT + i + 1) * P],
                                       src[:, i, f * P:(f + 1) * P] if tiled else src[:, i, f:nt * P:nt], P)
                    ins.then_inc(sT[name], 1)

            def hi_products(slot, nth, xh, xl, t0, nt, width, banks, first):
                wh = w_hi[:, slot, 0:nt * width].rearrange("p (t n) -> p t n", t=nt)
                pe.wait_ge(hi_done, nth + 1)
                for i in range(NT):
                    for k in range(nt):
                        o = ps[:, banks + i, 0:width]
                        MM(o, xh[:, t0 + k, i * P:(i + 1) * P], wh[:, k], start=first and k == 0, stop=False)
                        MM(o, xl[:, t0 + k, i * P:(i + 1) * P], wh[:, k], start=False, stop=False)

            def lo_products(slot, nth, xh, t0, nt, width, banks, last):
                wl = w_lo[:, slot, 0:nt * width].rearrange("p (t n) -> p t n", t=nt)
                pe.wait_ge(lo_done, nth + 1)
                for i in range(NT):
                    for k in range(nt):
                        ins = MM(ps[:, banks + i, 0:width], xh[:, t0 + k, i * P:(i + 1) * P], wl[:, k], start=False,
                                 stop=last and k == nt - 1)
                ins.then_inc(mm_done, 1)

            def use_block(slot, nth, xh, xl, t0, nt, width, banks, first, last):
                hi_products(slot, nth, xh, xl, t0, nt, width, banks, first)
                lo_products(slot, nth, xh, t0, nt, width, banks, last)

            def in_block(b, xh, xl, t0=None, first=None, last=None, part="both"):
                c = max(c for c in range(len(chunks)) if first_block[c] <= b)
                k = b - first_block[c]
                _, nt, width = blocks[b].shape
                t0 = k * nt if t0 is None else t0
                first = k == 0 if first is None else first
                last = b == first_block[c + 1] - 1 if last is None else last
                if part != "lo":
                    if first and c >= 2:
                        pe.wait_ge(*moved(c - 2))
                    hi_products(b % RING, b, xh, xl, t0, nt, width, c % 2 * 2, first)
                if part != "hi":
                    lo_products(b % RING, b, xh, t0, nt, width, c % 2 * 2, last)

            def chunk(c, xh=None, xl=None):
                for b in range(first_block[c], first_block[c + 1]):
                    in_block(b, xh or act_hi, xl or act_lo)

            pe.wait_ge(ld["x"], 16 * NT)
            pe.wait_ge(ld["ident"], 32)
            turn_act("x", x_res, KD, range(4))

            def pair_loop(c0, count):
                b0, per = first_block[c0], first_block[c0 + 2] - first_block[c0]
                with pe.Fori(0, count) as it:
                    for k in range(2):
                        c = c0 + k
                        if c0 >= 2 or count == 1:
                            pe.wait_ge(ev_act, it * 2 + (c - 1))
                        for hb in range(2):
                            b = b0 + 2 * k + hb
                            use_block(b % RING, it * per + b, act_hi, act_lo, 4 * hb, 4, COLS, (c % 2) * 2, hb == 0, hb == 1)

            for k in range(2):
                pe.wait_ge(sL["x"], 2 * k + 2)
                in_block(k, act_hi, act_lo)
            chunk(1)
            pair_loop(2, 1)
            pe.wait_ge(s["zeros_set"], 1)
            turn(ps[:, 4, 0:32], conv_rows[:], 32)
            turn(ps[:, 4, 32:40 + 2 * KD], vec_rows[:], 8 + 2 * KD)
            for g in range(GG):
                turn(ps[:, 5, g * P:(g + 1) * P], ws_t[:, g, :], P)
            for g, (bank, o) in enumerate(((6, 0), (7, 0), (4, P))):
                ins = MM(ps[0:AHG, bank, o:o + TOEP], table[:, AHG * g:AHG * (g + 1)], onehot[:, g, :], start=True, stop=True)
            ins.then_inc(s["aux_pe"], 1)
            chunk(4)
            pe.wait_ge(s["aux"], 1)
            pe.wait_ge(ev_act, 2)
            for f in range(KD):
                for i in range(NT):
                    ins = turn(ps[:, 4 + f // 2, (f % 2 * NT + i) * P:(f % 2 * NT + i + 1) * P], zq[:, i, f * P:(f + 1) * P], P)
                if f % 2:
                    ins.then_inc(s["qk_turned"], 1)
            pe.wait_ge(ev_act, 5)
            pe.wait_ge(s["conv_in"], 4)
            for k in range(2):
                for i in range(NT):
                    ins = turn(ps[0:MH, 4, (k * NT + i) * P:(k * NT + i + 1) * P], zif[:, i, k * MH:(k + 1) * MH], P)
            ins.then_inc(s["gates_turned"], 1)
            pair_loop(5, 1)
            pe.wait_ge(s["floor_done"], 1)
            for k, row in enumerate((0, 5)):
                for i in range(NT):
                    ins = turn(ps[:, 5, (k * NT + i) * MH:(k * NT + i + 1) * MH], rows[:, row, i * P:(i + 1) * P], MH)
            ins.then_inc(s["cols_turned"], 1)
            pair_loop(7, 2)
            pe.wait_ge(s["silu_qk"], 1)
            pe.wait_ge(s["cols_moved"], 1)

            def mlstm_values(h):
                pe.wait_ge(s["prob_ready"], h + 1)
                if h >= 2:
                    pe.wait_ge(s["numer_moved"], h - 1)
                b = 6 + h % 2
                MM(ps[:, b, 0:MDH + 1], pm[:, h % 2, 0:P], vx[:, 0, h, 0:MDH + 1], start=True, stop=True)
                MM(ps[:, b, S:S + MDH + 1], pm[:, h % 2, P:2 * P], vx[:, 0, h, 0:MDH + 1], start=True, stop=False)
                MM(ps[:, b, S:S + MDH + 1], pm[:, h % 2, 2 * P:3 * P], vx[:, 1, h, 0:MDH + 1], start=False,
                   stop=True).then_inc(s["pv_done"], 1)

            for h in range(MH):
                if h >= 1:
                    pe.wait_ge(s["w_exp"], h)
                MM(ps[:, 4, 0:S], minus_head[0:MH, h, :], rows[:, 3, :], start=True, stop=False, skip_group_check=True)
                MM(ps[:, 4, 0:P], ident[:], neg_future, start=False, stop=False, skip_group_check=True)
                MM(ps[:, 4, S:S + P], minus_head[0:MH, h, :], rows[:, 3, P:S], start=False, stop=False, skip_group_check=True)
                MM(ps[:, 4, S:S + P], ident[:], neg_future, start=False, stop=True,
                   skip_group_check=True).then_inc(s["decay_logit"], 1)
                if h >= 1:
                    pe.wait_ge(s["prob_ready"], h)
                MM(ps[:, 5, 0:S], post[:, MH + h, 0:P], post[:, h, :], start=True, stop=True)
                MM(ps[:, 5, S:S + P], post[:, MH + h, P:S], post[:, h, P:S], start=True, stop=True).then_inc(s["score"], 1)
                if h >= 1:
                    mlstm_values(h - 1)
                in_block(22 + h, act_hi, act_lo)
            mlstm_values(MH - 1)
            in_block(26, act_hi, act_lo)
            pe.wait_ge(s["aqk_ready"], 1)
            pe.wait_ge(s["numer_moved"], MH)
            for n in range(6):
                if n == 4:
                    in_block(27, act_hi, act_lo)
                if n >= 4:
                    pe.wait_ge(s["aqk_moved"], n - 3)
                for k in range(2):
                    for i in range(NT):
                        f = 2 * n + k
                        ins = turn(ps[:, 4 + n % 4, (k * NT + i) * P:(k * NT + i + 1) * P], zqk[:, i, f * P:(f + 1) * P], P)
                ins.then_inc(s["aqk_turned"], 1)
            pe.wait_ge(s["aqk_moved"], 6)

            def attn_scores(u):
                jp, t, jo = u // 4, u // 2 % 2, u % 2
                w = (t + 1) * P
                if u >= 1:
                    pe.wait_ge(s["a_logit_moved"], u)
                for g in range(AG):
                    hd = AHG * g + 2 * jp + jo
                    r0 = hd % 2 * ADH
                    ins = MM(ps[:, 4 + g // 2, g % 2 * S:g % 2 * S + w], qkT[r0:r0 + ADH, hd // 2, t * P:(t + 1) * P],
                             qkT[r0:r0 + ADH, 6 + hd // 2, 0:w], start=True, stop=True)
                ins.then_inc(s["a_logit"], 1)

            squares = [[(g, m) for g in range(AG) for m in range(t + 1)] for t in range(NT)]

            def turn_probs(u, f):
                t = u // 2 % 2
                pe.wait_ge(s["a_norm"], u + 1)
                if fills_before[u] + f:
                    pe.wait_ge(s["a_pmoved"], fills_before[u] + f)
                lo, n = turn_fills[t][f]
                for x in range(lo, lo + n):
                    g, m = squares[t][x]
                    ins = turn(ps[:, 6, (x - lo) * P:(x - lo + 1) * P], (lg0, lg1)[u % 2][:, g, m * P:(m + 1) * P], P)
                ins.then_inc(s["a_pturned"], 1)

            def attn_values(u):
                jp, t, jo = u // 4, u // 2 % 2, u % 2
                pe.wait_ge(s["a_pmoved"], fills_before[u + 1])
                if u >= 2 and not jo:
                    pe.wait_ge(s["a_ylo"], u // 2)
                for x, (g, m) in enumerate(squares[t]):
                    hd = AHG * g + 2 * jp + jo
                    ins = MM(ps[jo * ADH:(jo + 1) * ADH, 7, g * P:(g + 1) * P], zv[:, m, hd * ADH:(hd + 1) * ADH],
                             pT[:, x * P:(x + 1) * P], start=m == 0, stop=m == t)
                ins.then_inc(s["a_pv"], 1)

            attn_scores(0)
            pe.wait_ge(s["gv_ready"], 1)
            for n in range(NT):
                for g in range(GG):
                    ins = MM(ps[:, 6 + n, g * GC:(g + 1) * GC], wT[:, g, :], zg[:, n, GW + g * GC:GW + (g + 1) * GC],
                             start=True, stop=True)
                ins.then_inc(s["g_mixed"], 1)
            for u in range(8):
                b = 28 + u
                if u < 7:
                    attn_scores(u + 1)
                if b < 34:
                    in_block(b, act_hi, act_lo, part="hi")
                if u == 0:
                    pe.wait_ge(s["yc_done"], NT)
                turn_probs(u, 0)
                if b < 34:
                    in_block(b, act_hi, act_lo, part="lo")
                if u // 2 % 2:
                    turn_probs(u, 1)
                attn_values(u)
            pe.wait_ge(s["ya_done"], 1)
            pe.wait_ge(s["a_logit_moved"], 8)
            turn_act("a", zo, 4, range(2))
            pe.wait_ge(s["a_ylo"], 4)
            chunk(C_B, yb_hi, yb_lo)
            turn_act("c", zg, 4, range(2), bank0=6)
            chunk(C_B + 1, yb_hi, yb_lo)
            pe.wait_ge(sL["a"], 2)
            pe.wait_ge(sL["c"], 2)
            pe.wait_ge(ld["mem"], 16 * NT)
            turn_act("mem", mem_x, KD, range(4))
            for n in range(2):
                chunk(C_A + n, ya_hi, ya_lo)
            for n in range(2):
                chunk(C_C + n, yc_hi, yc_lo)
            pe.wait_ge(sL["mem"], KD // 2)
            for n in range(2):
                in_block(first_block[C_K] + n, act_hi, act_lo)
                pe.wait_ge(s["merged_ready"], n + 1)
                turn_act("merged", merged, KD, range(2 * n, 2 * n + 2), tiled=True)
            for c in range(C_OUT, C_OUT + 2):
                for k in range(2):
                    pe.wait_ge(sL["merged"], 2 * k + 2)
                    in_block(first_block[c] + k, mg_hi, mg_lo)
                    if c > C_OUT and k == 0:
                        pe.wait_ge(*moved(C_OUT))
                        turn_act("x1", x_res, KD, range(2), tiled=True)
            in_block(first_block[C_V0], act_hi, act_lo, t0=0, first=True, last=False)
            pe.wait_ge(*moved(C_OUT + 1))
            turn_act("x1", x_res, KD, range(2, 4), tiled=True)
            for k in range(2):
                pe.wait_ge(sL["x1"], 2 * k + 2)
                in_block(first_block[C_XQ] + k, mg_hi, mg_lo)
            pe.wait_ge(s["xk_ready"], 1)

            def turn_heads(src, name, bank0):
                for h in range(XH):
                    for i in range(NT):
                        ins = turn(ps[:, bank0 + h // 2, (h % 2 * NT + i) * P:(h % 2 * NT + i + 1) * P],
                                   src[:, i, h * P:(h + 1) * P], P)
                    if h % 2:
                        ins.then_inc(s[name], 1)

            turn_heads(xkv, "xk_turned", 6)
            in_block(first_block[C_V1], act_hi, act_lo, t0=4, first=False, last=True)
            pe.wait_ge(s["xq_scaled"], 1)
            turn_heads(xq, "xq_turned", 4)
            pe.wait_ge(s["xq_moved"], 2)
            pe.wait_ge(s["xk_moved"], 2)
            for t in range(NT):
                for h in range(XH):
                    ins = MM(ps[:, 4 + 2 * t + h // 2, h % 2 * S:(h % 2 + 1) * S], xqT[:, h, t * P:(t + 1) * P], xkT[:, h, :],
                             start=True, stop=True)
                    if h % 2:
                        ins.then_inc(s["x_logit"], 1)
            pe.wait_ge(*moved(C_V1))
            for t in range(NT):
                for h in range(XH):
                    if h % 2 == 0:
                        pe.wait_ge(s["x_norm"], 2 * t + h // 2 + 1)
                    for m in range(NT):
                        ins = turn(ps[:, 4 + 2 * t + h // 2, (h % 2 * NT + m) * P:(h % 2 * NT + m + 1) * P],
                                   xp[:, t, h * S + m * P:h * S + (m + 1) * P], P)
                    if h % 2:
                        ins.then_inc(s["x_pturned"], 1)
            pe.wait_ge(s["x_pmoved"], 2 * NT)
            for h in range(XH):
                for m in range(NT):
                    ins = MM(ps[:, 4 + h // 2, h % 2 * S:(h % 2 + 1) * S], xkv[:, m, XW + h * XDH:XW + (h + 1) * XDH],
                             xpT[:, h, m, :], start=m == 0, stop=m == NT - 1)
                if h % 2:
                    ins.then_inc(sT["o"], 1)
            pe.wait_ge(sL["o"], 2)
            chunk(C_XO, oT_hi, oT_lo)
            last_block = first_block[C_XO + 1]
            in_block(last_block, oT_hi, oT_lo, part="hi")
            pe.wait_ge(*moved(C_XO))
            turn_act("x2", x_res, KD, range(2), tiled=True)
            in_block(last_block, oT_hi, oT_lo, part="lo")

            def router_products(k0):
                for i in range(NT):
                    for k in range(k0, k0 + KD // 2):
                        ins = MM(ps[:, 2 + i, 0:NE], x2T[:, k, i * P:(i + 1) * P], router_w[:, k, :], start=k == 0,
                                 stop=k == KD - 1)
                return ins

            pe.wait_ge(ld["moe"], 32)
            pe.wait_ge(s["x2T_moved"], 2)
            router_products(0)
            pe.wait_ge(*moved(C_XO + 1))
            turn_act("x2", x_res, KD, range(2, 4), tiled=True)
            pe.wait_ge(s["x2T_moved"], 4)
            router_products(KD // 2).then_inc(s["r_logit"], 1)
            pe.wait_ge(s["zeros"], 1)
            for b in range(4, 8):
                for k in range(4):
                    MM(ps[:, b, k * P:(k + 1) * P], zeros, zeros, start=k == 0, stop=False, skip_group_check=True)
            for name in ("gath_pe", "selT_pe"):
                pe.drain().then_inc(s[name], FREE)
            pe.wait_ge(s["chosen"], 1)
            ch = chosen.rearrange("p (i e) -> p i e", i=NT)
            MM(ps[:, 1, 0:NE], before, ch[:, 0], start=True, stop=True)
            MM(ps[:, 1, NE:2 * NE], before, ch[:, 1], start=True, stop=False)
            MM(ps[:, 1, NE:2 * NE], ones, ch[:, 0], start=False, stop=True)
            MM(ps[:, 1, 2 * NE:3 * NE], ones, ch[:, 0], start=True, stop=False)
            MM(ps[:, 1, 2 * NE:3 * NE], ones, ch[:, 1], start=False, stop=True).then_inc(s["pos_pe"], 1)
            pe.wait_ge(s["rounds_ready"], 1)
            pe.wait_ge(s["h_lo_done"], 1)
            rounds = pe.value_load(n_rounds_i[0:1, 0:1], min_val=1, max_val=S // SLOTS)

            def slot_gates(q):
                pe.wait_ge(s["selected"], q + 1)
                pe.wait_ge(s["gu_moved"], FREE + 2 * EPG * q)
                for e in range(EPG):
                    for i in range(NT):
                        ins = MM(ps[:, 1, e * EPG:(e + 1) * EPG], f32(sel[:, i, e, :]), gcur[:, i * EPG:(i + 1) * EPG],
                                 start=i == 0, stop=i == NT - 1)
                ins.then_inc(s["wslot_pe"], 1)

            def gather(q, tiles):
                for t in tiles:
                    if t == 1:
                        pe.wait_ge(s["wslot_moved"], q + 1)
                    if t >= 2:
                        pe.wait_ge(s["gath_moved"], KD * q + (t - 1))
                    for k, hh in enumerate((h_hi, h_lo)):
                        for i in range(NT):
                            ins = MM(ps[:, t % 2, k * EPG * SLOTS:(k + 1) * EPG * SLOTS], hh[:, i, t * P:(t + 1) * P],
                                     sel[:, i, :, 0:SLOTS], start=i == 0, stop=i == NT - 1)
                    ins.then_inc(s["gath_pe"], 1)

            def turn_selection(q):
                pe.wait_ge(s["ylo_done"], FREE + EPG * q)
                for e in range(EPG):
                    for i in range(NT):
                        ins = turn(ps[:, 2 + e // 2, (e % 2 * NT + i) * P:(e % 2 * NT + i + 1) * P], f32(sel[:, i, e, :]), P)
                    if e % 2:
                        ins.then_inc(s["selT_pe"], 1)

            def e_block(q, n, lhs, bank, first, last):
                b, nt = NB1 + n, 4 - direct.get(n, 0)
                raw = e_slot(n)[0]
                for k, (done, w) in enumerate(((hi_done, w_hi), (lo_done, w_lo))):
                    pe.wait_ge(done, GB * q + (b + 1))
                    for t in range(nt):
                        ins = MM(ps[:, bank, :], lhs[t], w[:, b % RING, t * COLS:(t + 1) * COLS],
                                 start=first and not k and t == 0, stop=last and k == 1 and t == 3)
                for t in range(nt, 4):
                    ins = MM(ps[:, bank, :], f32(lhs[t]), raw[:, t * COLS:(t + 1) * COLS], start=False, stop=last and t == 3)
                ins.then_inc(mm_done, 1)
                return ins

            def wide(q, j, n, bank):
                for half in range(2):
                    e_block(q, n + half, [xg[:, 4 * half + t, j, :] for t in range(4)], bank, half == 0, half == 1)

            def e_turn(q, j):
                pe.wait_ge(s["gu_moved"], FREE + 2 * (EPG * q + j) + 2)
                pe.wait_ge(s["ylo_done"], FREE + EPG * q + j)
                if j == 0:
                    pe.wait_ge(s["selT_done"], 2 * q + 2)
                for k in range(2):
                    for f in range(FF // P):
                        ins = MM(ps[:, 2 + k, f * P:(f + 1) * P], gu[:, k, f:FF:FF // P], both, start=True, stop=True)
                ins.then_inc(s["et_pe"], 1)

            def e_scatter(q, j):
                pe.wait_ge(s["ylo_done"], FREE + EPG * q + (j + 1))
                for i in range(NT):
                    for half in range(2):
                        for y in (y_hi, y_lo):
                            ins = MM(ps[:, 4 + 2 * i + half, :], selT[:, j, i * P:(i + 1) * P],
                                     y[:, half * COLS:(half + 1) * COLS], start=False, stop=False, skip_group_check=True)
                ins.then_inc(s["scat_pe"], 1)

            def e_down(q, j, m, half):
                pe.wait_ge(s["a_ready"], EPG * q + (j + 1))
                e_block(q, 2 * m + half, [a_st[:, t, :] for t in range(4)], 2 + half, True, True)

            def expert_group(q, more):
                pe.wait_ge(s["gath_moved"], KD * (q + 1))
                for m, (j, which) in enumerate(ex_order[:-1]):
                    if which == "gate":
                        wide(q, j, 2 * m, 0)
                        if j == 0:
                            turn_selection(q)
                    elif which == "up":
                        wide(q, j, 2 * m, 1)
                        if j:
                            e_scatter(q, j - 1)
                        e_turn(q, j)
                    else:
                        for half in range(2):
                            e_down(q, j, m, half)
                if more:
                    slot_gates(q + 1)
                    gather(q + 1, range(0, 2))
                e_down(q, EPG - 1, len(ex_order) - 1, 0)
                if more:
                    gather(q + 1, range(2, 4))
                e_down(q, EPG - 1, len(ex_order) - 1, 1)
                if more:
                    gather(q + 1, range(4, KD))
                e_scatter(q, EPG - 1)

            pe.drain().then_inc(s["scat_pe"], FREE)
            with pe.Fori(0, rounds) as r:
                slot_gates(r * NG)
                gather(r * NG, range(KD))
                with pe.Fori(0, NG - 1) as g:
                    expert_group(r * NG + g, True)
                expert_group(r * NG + (NG - 1), False)
            MM(ps[:, 0, 0:P], zeros, zeros, start=True, stop=True).then_inc(s["moe_done"], 1)


_INS = ["x", "mem", "norm_mix", "w_in", "mlstm_conv", "mlstm_gate_b", "mlstm_norm", "attn_qk_norm", "gmlp_norm",
        "gmlp_ws", "gmlp_bs", "w_branch_a", "w_branch_b", "w_branch_c", "w_out", "rel_bias", "norm_xattn", "norm_mem",
        "w_xq", "w_xkv", "xattn_qk_norm", "w_xo", "norm_ffn", "router_w", "router_b", "w_expert_gate", "w_expert_up",
        "w_expert_down"]


def kernel(**inputs):
    import concourse.bacc as bacc
    from concourse.bass_utils import run_bass_kernel_spmd

    nc = bacc.Bacc("TRN2", target_bir_lowering=False, num_devices=1, dynamic_dma_scratch_size=1024)
    arrays, aps = {}, {}
    given = {name: np.ascontiguousarray(inputs[name]) for name in _INS}
    given.update(zip(("c_ident", "c_const", "c_onehot"), shape_constants()))
    for name, a in given.items():
        arrays[f"in_{name}"] = a
        aps[name] = nc.dram_tensor(f"in_{name}", a.shape, mybir.dt.from_np(a.dtype), kind="ExternalInput").ap()
    out = nc.dram_tensor("out_0", (1, S, D), mybir.dt.float32, kind="ExternalOutput").ap()
    build_program(nc, aps, out)
    result = run_bass_kernel_spmd(nc, [arrays], core_ids=[0])
    return result.results[0]["out_0"]
```

```python
import math
from contextlib import ExitStack

import numpy as np
import concourse.bass as bass
from concourse import mybir

P = 128
S = 256
NT = S // P
D = 1024
EPS = 1e-6
MH, MDH = 4, 128
MW = MH * MDH
AG, AHG, ADH = 3, 4, 64
AH = AG * AHG
AW = AH * ADH
DILATION = (1, 4, 16)
STEPS = 128
GG, GC = 4, 128
GW = GG * GC
XH, XDH = 4, 128
XW = XH * XDH
REL_BUCKETS, REL_MAX_DIST = 32, 2048
NE, NG, EPG, FF = 16, 4, 4, 512
SLOTS = 64
NEG = -1.0e30
KD = D // P
COLS = 512
BLK = 2048
RING = 4
E_RING = 8
DIRECT = (0, 0, 0, 1, 1, 1, 2, 1, 1, 1, 1, 0)
TOEP = 384

C_IF = 4 * MW
C_AQ = C_IF + 2 * MH
C_GU = C_AQ + 3 * AW
C_GATE = C_GU + 2 * GW
N_IN = C_GATE + 3 * D
C_WIDE = 264


def shape_constants():
    r = np.arange(P)
    ident = np.eye(P, dtype=np.float32)
    neg_future = np.where(r[:, None] > r[None, :], np.float32(NEG), np.float32(0))
    before = (r[:, None] < r[None, :]).astype(np.float32)
    keep_past = (r[:, None] >= r[None, :]).astype(np.float32)
    ones = np.ones((P, P), np.float32)
    minus_head = np.zeros((P, MH, P), np.float32)
    for h in range(MH):
        minus_head[h, h] = -1
    iota = np.tile(np.arange(SLOTS, dtype=np.float32), 2)[None].repeat(P, 0)
    tie = (np.arange(EPG)[None, :] < np.arange(EPG)[:, None]).astype(np.float32)
    tie = tie.reshape(1, -1).repeat(P, 0)
    both = np.tile(np.eye(SLOTS, dtype=np.float32), (2, 2))
    minus_half = np.full((P, 48), -0.5, np.float32)
    parts = [neg_future, before, keep_past, ones, minus_head.reshape(P, -1), iota, tie, both, minus_half]
    onehot = np.zeros((REL_BUCKETS + 1, AG, TOEP), np.float32)
    exact = REL_BUCKETS // 2
    for g, dil in enumerate(DILATION):
        for y in range(TOEP):
            d = S - 1 - y
            if d < 0 or d % dil or d // dil > STEPS:
                onehot[REL_BUCKETS, g, y] = 1
            elif d < exact:
                onehot[d, g, y] = 1
            else:
                b = exact + int(math.log(d / exact) / math.log(REL_MAX_DIST / exact) * (REL_BUCKETS - exact))
                onehot[min(b, REL_BUCKETS - 1), g, y] = 1
    return ident, np.ascontiguousarray(np.concatenate(parts, 1)), onehot.reshape(REL_BUCKETS + 1, -1)


N_CONST = P * 4 + MH * P + P + EPG * EPG + P + 48


def build_program(nc, d_in, out):
    fp32, f32r, i32 = mybir.dt.float32, mybir.dt.float32r, mybir.dt.int32
    ALU, ACT, AX = mybir.AluOpType, mybir.ActivationFunctionType, mybir.AxisListType
    scratch = nc.dram_tensor("bias_rows", (AG * AHG, TOEP), fp32)
    bias_square = nc.dram_tensor("bias_square", (AG * AHG, P, S), fp32).ap()

    ctx = ExitStack()
    with ctx:
        base = -(-nc.sbuf_base // 64) * 64
        place = {"at": base}

        def region(nbytes):
            at = place["at"]
            place["at"] += -(-nbytes // 32) * 32
            assert place["at"] <= nc.sbuf_usable_end, place["at"]
            return at

        def at(name, offset, shape, dt=fp32):
            return nc.alloc_sbuf_tensor_at(name, shape, dt, offset=offset)

        def sb(name, shape, dt=fp32):
            return at(name, region(4 * int(np.prod(shape[1:]))), shape, dt)

        w_raw = sb("w_raw", [P, RING, BLK])
        w_hi = sb("w_hi", [P, RING, BLK], f32r)
        w_lo = sb("w_lo", [P, RING, BLK], f32r)
        x_res = sb("x_res", [P, NT, D])
        act_at = place["at"]
        act_hi = sb("act_hi", [P, KD, S], f32r)
        act_lo = sb("act_lo", [P, KD, S], f32r)
        e_raw_4, e_raw_5 = at("e_raw_4", act_at, [P, BLK]), at("e_raw_5", act_at + 4 * KD * S, [P, BLK])
        ident = sb("ident", [P, P])
        const = sb("const", [P, N_CONST])
        off = 0

        def part(n):
            nonlocal off
            v = const[:, off:off + n]
            off += n
            return v

        neg_future, before, keep_past, ones = part(P), part(P), part(P), part(P)
        minus_head = part(MH * P).rearrange("p (h c) -> p h c", h=MH)
        iota = part(P)
        tie = part(EPG * EPG).rearrange("p (j i) -> p j i", j=EPG)
        both = part(P)
        minus_half = part(48)
        gains = sb("gains", [P, 2 * KD + 4])
        g_mix, g_mem, g_mls = gains[:, 0:8], gains[:, 8:16], gains[:, 16:20]
        vec_cols = sb("vec_cols", [P, 8 + 2 * KD])
        g_xat, g_ffn = vec_cols[:, 8:8 + KD], vec_cols[:, 8 + KD:8 + 2 * KD]
        g_qk, g_xqk, gs_b = vec_cols[:, 0:2], vec_cols[:, 2:4], vec_cols[:, 4:8]
        gate_bi, gate_bf = sb("gate_bi", [MH, 1]), sb("gate_bf", [MH, 1])
        stat = sb("stat", [P, 320])
        router_b = sb("router_b", [P, NE])
        n_rounds_i = sb("n_rounds_i", [1, 1], i32)

        q_at = region(8192)
        zq_at, vx_at, zo_at = region(8192), region(NT * MH * 130 * 4), region(4096)
        zqk_at, zv_at, zg_at, tg_at = region(NT * 1536 * 4), region(NT * AW * 4), region(8192), region(NT * 3 * D * 4)
        zif_at = region(NT * 8 * 4)
        m_at = region(8832 + 8192)
        end_at = place["at"]

        mem_x = at("mem_x", q_at, [P, NT, D])
        lg0 = at("lg0", m_at + 12288, [P, AG, S])
        lg1 = at("lg1", q_at, [P, AG, S])
        pT = at("pT", q_at + 3072, [P, AG * S])
        zq = at("zq", zq_at, [P, NT, 2 * MW])
        vx = at("vx", vx_at, [P, NT, MH, 130])
        zo = at("zo", zo_at, [P, NT, MW])
        zqk = at("zqk", zqk_at, [P, NT, 2 * AW])
        zv = at("zv", zv_at, [P, NT, AW])
        zg = at("zg", zg_at, [P, NT, 2 * GW])
        tg = at("tg", tg_at, [P, NT, 3 * D])
        merged = tg[:, :, 0:D]
        zif = at("zif", zif_at, [P, NT, 8])
        pre = at("pre", m_at, [P, KD, S + 3])
        post = at("post", m_at + 8832, [P, KD, S])
        rows = at("rows", zq_at, [MH, 6, S])
        wgt = at("wgt", m_at, [P, 3 * P])
        pm = at("pm", m_at + 1536, [P, 2, 3 * P])
        numer = at("numer", m_at + 4608, [P, NT, MH, 130])
        cw = sb("cw", [P, 32])
        conv_rows = at("conv_rows", tg_at + 14336, [32, P])
        toep = at("toep", zq_at, [P, AH, S])
        qkT = at("qkT", m_at, [P, 12, S])
        table = sb("table", [REL_BUCKETS + 1, AH])
        onehot = at("onehot", tg_at, [REL_BUCKETS + 1, AG, TOEP])
        bias_row = at("bias_row", tg_at + AG * TOEP * 4, [AHG, AG, TOEP])
        yb_hi = at("yb_hi", zqk_at, [P, 6, S], f32r)
        yb_lo = at("yb_lo", zqk_at + 6144, [P, 6, S], f32r)
        vec_rows = at("vec_rows", tg_at + 14848, [8 + 2 * KD, P])
        ws_t = at("ws_t", tg_at + 12288, [P, GG, P])
        wT = sb("wT", [P, GG, P])
        gs_gain = sb("gs_gain", [P, GW])
        ya_hi, ya_lo = at("ya_hi", m_at, [P, 4, S], f32r), at("ya_lo", m_at + 4096, [P, 4, S], f32r)
        yc_hi, yc_lo = at("yc_hi", m_at + 8192, [P, 4, S], f32r), at("yc_lo", m_at + 12288, [P, 4, S], f32r)
        xkv = at("xkv", zq_at, [P, NT, 2 * XW])
        xkT = at("xkT", vx_at, [P, XH, S])
        xq = at("xq", zqk_at, [P, NT, XW])
        xqT = at("xqT", zqk_at + 4096, [P, XH, S])
        sq_s = at("sq_s", q_at, [P, 2 * D])
        mg_hi, mg_lo = at("mg_hi", m_at, [P, KD, S], f32r), at("mg_lo", m_at + 8192, [P, KD, S], f32r)
        sq_g = at("sq_g", q_at + 4096, [P, NT, GW])
        junk_x = at("junk_x", m_at, [P, NT, D])
        junk_1 = at("junk_1", q_at, [P, NT, D])
        junk_mem = at("junk_mem", act_at + 4 * KD * S, [P, NT, D])
        sq_k = at("sq_k", zv_at, [P, NT, XW])
        sq_q = at("sq_q", zv_at, [P, NT, XW])
        xp = at("xp", tg_at, [P, NT, XH * S])
        xpT = at("xpT", tg_at + 8192, [P, XH, NT, S])
        oT_hi, oT_lo = at("oT_hi", zg_at, [P, XH, S], f32r), at("oT_lo", zg_at + 4096, [P, XH, S], f32r)

        place["at"] = zq_at
        xg_at = region(KD * EPG * P * 4)
        xg = at("xg", xg_at, [P, KD, EPG, P], f32r)
        x2T = at("x2T", xg_at, [P, KD, S])
        junk_2 = at("junk_2", xg_at + 8192, [P, NT, D])
        h_hi, h_lo = sb("h_hi", [P, NT, D], f32r), sb("h_lo", [P, NT, D], f32r)
        h_full = sb("h_full", [P, NT, D])
        sel = sb("sel", [P, NT, EPG, P], f32r)
        selT = sb("selT", [P, EPG, S], f32r)
        gates_split = sb("gates_split", [P, NT, 2, NE], f32r)
        gcur = sb("gcur", [P, NT, 2, EPG], f32r)
        w_slot, w_slot_next = sb("w_slot", [P, EPG]), sb("w_slot_next", [P, EPG])
        gu = sb("gu", [P, 2, FF])
        e_act = sb("e_act", [P, 2, FF // P, SLOTS])
        a_st = sb("a_st", [P, FF // P, P], f32r)
        y_hi, y_lo = sb("y_hi", [P, D], f32r), sb("y_lo", [P, D], f32r)
        route = sb("route", [P, 1024])
        router_w = sb("router_w", [P, KD, NE])
        g_ffn_row = sb("g_ffn_row", [P, D])
        zeros = sb("zeros", [P, P])[:]
        assert place["at"] <= m_at + 8832, (place["at"], m_at)
        e_raw = [None] * RING + [e_raw_4, e_raw_5, at("e_raw_6", q_at, [P, BLK]), at("e_raw_7", m_at + 8832, [P, BLK])]

        ps = ctx.enter_context(nc.psum_tensor("ps", [P, 8, 512], fp32))

        def sem(name):
            return ctx.enter_context(nc.semaphore(name))

        w_in_slot = [sem(f"w_landed_{i}") for i in range(RING)]
        e_in_slot = [None] * RING + [sem(f"e_landed_{i}") for i in range(RING, E_RING)]
        hi_done, lo_done = sem("w_hi_done"), sem("w_lo_done")
        mm_done = sem("w_block_used")
        ev_act, ev_dve = sem("chunk_moved_by_act"), sem("chunk_moved_by_dve")
        ld = {n: sem("loaded_" + n) for n in (
            "x", "ident", "const", "aux", "small", "mem", "toep", "bias_rows", "moe", "out")}
        ST = ("x", "mem", "a", "c", "merged", "x1", "o", "x2")
        sT = {n: sem(f"turned_{n}") for n in ST}
        sH = {n: sem(f"hi_of_{n}") for n in ST}
        sL = {n: sem(f"lo_of_{n}") for n in ST}
        RM = ("x", "mls", "att", "gml", "mem", "xk", "x1", "xq", "x2")
        s_sq = {n: sem(f"squared_{n}") for n in RM}
        s_ms = {n: sem(f"mean_square_{n}") for n in RM}
        s_rs = {n: sem(f"rsqrt_{n}") for n in RM}
        names = """aux_turned aux_moved qk_turned conv_in_ready conv_done qk_tanh_done qk_silu_done
            gates_turned neg_abs_f_done log_done decay_done floor_rows_done cols_turned cols_moved
            decay_exponents_done scores_done decay_weights_done m_probs_ready numer_done numer_moved
            numer_used ya_done aqk_squares_read aqk_ready aqk_turned aqk_moved a_logits_done
            a_logits_moved a_max_done a_exp_done a_probs_ready a_probs_turned a_probs_moved
            a_out_done a_out_hi_done a_out_lo_done gelu_done gv_ready gv_mixed yc_done xk_ready
            xk_turned xk_moved xq_turned xq_moved x_logits_done x_max_done x_exp_done x_probs_ready
            x_probs_turned x_probs_moved merged_ready x2T_moved router_logits_done router_max_taken
            router_exp_done chosen places_done rounds_ready h_full_done h_hi_done h_lo_done
            sel_ready sel_turned selT_moved gathered gathered_moved slot_gates_done gu_moved
            gu_turned gate_tanh_done a_ready y_hi_done y_lo_done scattered moe_done ws_masked
            out_ready half_rsqrt_ready slot_gates_moved xq_ready zeros_written""".split()
        s = {n: sem(n) for n in names}

        win = d_in["w_in"][0].rearrange("(p t) n -> p t n", t=KD)

        def rows_of(w, t):
            return w[0].rearrange("(p t) n -> p t n", t=t)

        def tiles_of(w, t):
            return w[0].rearrange("(t p) n -> p t n", t=t)

        cols = [(c * COLS, COLS) for c in range(4)] + [(C_IF, C_WIDE)]
        cols += [(C_IF + C_WIDE + c * COLS, COLS) for c in range(12)]
        chunks = [[win[:, 4 * k:4 * k + 4, c0:c0 + n] for k in range(2)] for c0, n in cols]

        def halves(v, nt, width):
            per = nt if nt <= 4 else nt // 2
            return [[v[:, k:k + per, n:n + COLS] for k in range(0, nt, per)] for n in range(0, width, COLS)]

        keys, values = halves(rows_of(d_in["w_xkv"], KD), KD, 2 * XW)
        chunks += halves(tiles_of(d_in["w_branch_b"], 6), 6, D)
        chunks += halves(rows_of(d_in["w_branch_a"], 4), 4, D)
        chunks += halves(rows_of(d_in["w_branch_c"], 4), 4, D)
        chunks += [keys]
        chunks += halves(tiles_of(d_in["w_out"], KD), KD, D)
        chunks += [values[:1]] + halves(tiles_of(d_in["w_xq"], KD), KD, XW) + [values[1:]]
        chunks += halves(tiles_of(d_in["w_xo"], XH), XH, D)
        C_B, C_A, C_C, C_K, C_OUT, C_V0, C_XQ, C_V1, C_XO = 17, 19, 21, 23, 24, 26, 27, 28, 29
        by_act = [c for c in range(C_B)] + [C_K, C_V1]
        by_dve = [c for c in range(C_B, C_XO + 2) if c not in by_act and c != C_V0]

        def moved(c):
            return (ev_act, by_act.index(c) + 1) if c in by_act else (ev_dve, by_dve.index(c) + 1)

        blocks = [b for c in chunks for b in c]
        first_block = [sum(len(c) for c in chunks[:n]) for n in range(len(chunks) + 1)]
        NB1 = len(blocks)
        GB = 6 * EPG
        assert NB1 % 2 == 0 and GB % RING == 0
        ex_order = []
        for j in range(EPG):
            ex_order += [(j, "gate")] + ([(j - 1, "down")] if j else []) + [(j, "up")]
        ex_order += [(EPG - 1, "down")]
        ex_block = {k: 2 * n for n, k in enumerate(ex_order)}
        direct = {2 * m: tiles for m, tiles in enumerate(DIRECT) if tiles}

        FREE = 1

        def split_steps(m, more, ahead=0):
            return range(max(2 * m - 2 + ahead, 0) + RING, min(2 * m + ahead + RING, GB + RING if more else GB))

        def bview(t, b, shape):
            n = int(np.prod(shape[1:]))
            return t[:, b % RING, 0:n].rearrange("p (t n) -> p t n", t=shape[1])

        def bc(v, shape):
            return v.to_broadcast(list(shape))

        rt_at = [0]

        def rt(*shape):
            n = int(np.prod(shape))
            v = route[:, rt_at[0]:rt_at[0] + n]
            rt_at[0] += n
            assert rt_at[0] <= 1024
            return v

        prob, posm, gates, chosen, topw = (rt(NT * NE) for _ in range(5))
        gt, ge = rt(NT * NE * EPG), rt(NT * NE * EPG)
        rank, r2 = rt(NT * NE), rt(NT * NE)
        score, eq, earlier, first = (rt(NT * NG) for _ in range(4))
        rmax, rsum, rrec, best = rt(NT), rt(NT), rt(NT), rt(NT)
        total = rt(NE)

        st_at = {}

        def stats(name, n):
            if name not in st_at:
                st_at[name] = (sum(v[1] for v in st_at.values()), n)
            o, m = st_at[name]
            assert o + m <= 320
            return stat[:, o:o + m]

        ss_x, rs_x, rsh_x = stats("ss_x", 2), stats("rs_x", 2), stats("rsh_x", 2)
        aT, emT, den, rden = stats("aT", 8), stats("emT", 8), stats("den", 8), stats("rden", 8)
        ss_m, rs_m = stats("ss_m", 8), stats("rs_m", 8)
        ss_a, rs_a = stats("ss_a", 48), stats("rs_a", 48)
        a_nm, a_sum, a_rec = stats("a_nm", 8), stats("a_sum", 8), stats("a_rec", 8)
        ss_g, rs_g = stats("ss_g", 8), stats("rs_g", 8)
        ss_mem, rs_mem = stats("ss_mem", 2), stats("rs_mem", 2)
        ss_k, rs_k, ss_q, rs_q = stats("ss_k", 8), stats("rs_k", 8), stats("ss_q", 8), stats("rs_q", 8)
        x_nm, x_sum, x_rec = stats("x_nm", 8), stats("x_sum", 8), stats("x_rec", 8)
        ss_1, rs_1, ss_2, rs_2 = stats("ss_1", 2), stats("rs_1", 2), stats("ss_2", 2), stats("rs_2", 2)
        ss_2h = stats("ss_2h", 4)

        turn_fills = [[(0, 3)], [(0, 4), (4, 2)]]
        filled = (0, 1, 2, 4, 5, 6)
        blocks_before = [sum(v < u for v in filled) for u in range(9)]
        fills_before = [sum(len(turn_fills[v // 2 % 2]) for v in range(u)) for u in range(9)]
        scratch_rows = scratch.ap().rearrange("(g h) y -> h g y", g=AG)
        bias_shifted = bass.AP(tensor=scratch.ap().tensor, offset=P - 1, ap=[[TOEP, AH], [-1, P], [1, S]])

        def e_slot(n):
            k = n % E_RING
            if k >= RING:
                return e_raw[k], e_in_slot[k], n // E_RING + 1
            k = (NB1 + k) % RING
            return w_raw[:, k, :], w_in_slot[k], -(-(NB1 - k) // RING) + n // E_RING + 1

        expert_block = [(j, which, half) for j, which in ex_order for half in range(2)]

        block = ctx.enter_context(nc.Block())

        def f32(v):
            return v.bitcast(fp32)

        @block.sync
        def _(sp):
            def load(name, *pairs):
                for dst, src in pairs:
                    sp.dma_start(dst, src).then_inc(ld[name], 16)

            def col(v):
                return v.rearrange("(n o) -> n o", o=1)

            def weight_block(b):
                if b >= RING:
                    sp.wait_ge(hi_done, b - RING + 1)
                    sp.wait_ge(lo_done, b - RING + 1)
                sp.dma_start(bview(w_raw, b, blocks[b].shape), blocks[b]).then_inc(w_in_slot[b % RING], 16)

            load("x", *[(x_res[:, i, :], d_in["x"][0, i * P:(i + 1) * P, :]) for i in range(NT)])
            load("ident", (ident[:], d_in["c_ident"]), (g_mix, d_in["norm_mix"][0].rearrange("(p t) -> p t", t=KD)))
            for b in range(4):
                weight_block(b)
            load("const", (const[:], d_in["c_const"]))
            load("aux", (conv_rows[:], d_in["mlstm_conv"][0].rearrange("w (f p) -> (w f) p", p=P)),
                 (ws_t[:], d_in["gmlp_ws"][0].rearrange("g t s -> t g s")),
                 (table[0:REL_BUCKETS, :], d_in["rel_bias"]),
                 (vec_rows[0:2, 0:ADH], d_in["attn_qk_norm"][0]), (vec_rows[0:2, ADH:P], d_in["attn_qk_norm"][0]),
                 (vec_rows[2:4, :], d_in["xattn_qk_norm"][0]), (vec_rows[4:8, :], d_in["gmlp_bs"][0]),
                 (onehot[:], d_in["c_onehot"].rearrange("b (g y) -> b g y", g=AG)))
            load("aux", (vec_rows[8:8 + KD, :], d_in["norm_xattn"][0].rearrange("(t p) -> t p", t=KD)),
                 (vec_rows[8 + KD:8 + 2 * KD, :], d_in["norm_ffn"][0].rearrange("(t p) -> t p", t=KD)))
            load("aux", (gate_bi[:], col(d_in["mlstm_gate_b"][0, 0:MH])),
                 (gate_bf[:], col(d_in["mlstm_gate_b"][0, MH:2 * MH])))
            for b in range(4, 8):
                weight_block(b)
            load("small", (g_mls, d_in["mlstm_norm"][0].rearrange("(p t) -> p t", t=4)),
                 (g_mem, d_in["norm_mem"][0].rearrange("(p t) -> p t", t=KD)),
                 (gs_gain[:], d_in["gmlp_norm"].to_broadcast([P, GW])),
                 (router_b[:], d_in["router_b"].rearrange("(o n) -> o n", o=1).to_broadcast([P, NE])))
            for b in range(8, NB1):
                weight_block(b)

            expert_w = {"gate": d_in["w_expert_gate"], "up": d_in["w_expert_up"], "down": d_in["w_expert_down"]}

            def expert_loads(r, g):
                q = r * NG + g
                for n, (j, which, half) in enumerate(expert_block):
                    b = NB1 + n
                    sp.wait_ge(hi_done, q * GB + (b - E_RING + 1))
                    sp.wait_ge(lo_done, q * GB + (b - E_RING + 1))
                    if (n - E_RING) % GB in direct:
                        sp.wait_ge(mm_done, q * GB + (b - E_RING + 1))
                    w = expert_w[which][0, bass.ds(g * EPG + j, 1), :, :]
                    if which == "down":
                        src = w.rearrange("e (p t) n -> p (e t) n", t=4)[:, :, half * COLS:(half + 1) * COLS]
                    else:
                        src = w.rearrange("e (p t) n -> p (e t) n", t=KD)[:, 4 * half:4 * half + 4, :]
                    raw, landed, _ = e_slot(n)
                    sp.dma_start(raw[:, :].rearrange("p (t n) -> p t n", t=4), src).then_inc(landed, 16)

            sp.wait_ge(hi_done, NB1)
            sp.wait_ge(lo_done, NB1)
            sp.wait_ge(mm_done, first_block[C_V1 + 1])
            with sp.Fori(0, NG) as g:
                expert_loads(0, g)
            sp.wait_ge(s["rounds_ready"], 1)
            rounds = sp.value_load(n_rounds_i[0:1, 0:1], min_val=1, max_val=S // SLOTS)
            with sp.If(rounds > 1):
                with sp.Fori(1, rounds) as r:
                    with sp.Fori(0, NG) as g:
                        expert_loads(r, g)
            with sp.Else():
                sp.nop()
            for i in range(NT):
                sp.wait_ge(s["out_ready"], i + 1)
                sp.dma_start(out[0, i * P:(i + 1) * P, :], x_res[:, i, :]).then_inc(ld["out"], 16)
            sp.wait_ge(ld["out"], 16 * NT)

        @block.scalar
        def _(act):
            A = nc.scalar.activation

            def w_hi_part(b):
                act.wait_ge(w_in_slot[b % RING], 16 * (b // RING + 1))
                if b >= RING:
                    act.wait_ge(mm_done, b - RING + 1)
                A(bview(w_hi, b, blocks[b].shape), bview(w_raw, b, blocks[b].shape), ACT.Copy).then_inc(hi_done, 1)

            def w_chunk(c):
                for b in range(first_block[c], first_block[c + 1]):
                    w_hi_part(b)

            def acc(c, i, n=COLS):
                return ps[:, (c % 2) * 2 + i, 0:n]

            def move(c, *triples):
                act.wait_ge(mm_done, first_block[c + 1])
                for k, (dst, src, func, scale) in enumerate(triples):
                    ins = A(dst, src, func, scale=scale)
                ins.then_inc(ev_act, 1)

            def act_hi_part(n, banks, dst, gain=None, bank0=4):
                for hb in banks:
                    act.wait_ge(sT[n], hb + 1)
                    if gain is None:
                        ins = A(dst[:, 2 * hb:2 * hb + 2, :],
                                ps[:, bank0 + hb, :].rearrange("p (k s) -> p k s", k=2), ACT.Copy)
                    else:
                        for k in range(2):
                            ins = A(dst[:, 2 * hb + k, :], ps[:, bank0 + hb, k * S:(k + 1) * S], ACT.Copy,
                                    scale=gain[:, 2 * hb + k:2 * hb + k + 1])
                    ins.then_inc(sH[n], 1)

            def numer_out(h):
                act.wait_ge(s["numer_done"], h + 1)
                A(numer[:, :, h, 0:MDH + 1], ps[:, 6 + h % 2, :].rearrange("p (i n) -> p i n", i=NT)[:, :, 0:MDH + 1],
                  ACT.Copy).then_inc(s["numer_moved"], 1)

            def attn_out(u):
                jp, t, jo = u // 4, u // 2 % 2, u % 2
                if u >= 1:
                    act.wait_ge(s["a_out_done"], u)
                for f, (lo, n) in enumerate(turn_fills[t]):
                    act.wait_ge(s["a_probs_turned"], fills_before[u] + f + 1)
                    A(pT[:, lo * P:(lo + n) * P], ps[:, 6, 0:n * P], ACT.Copy).then_inc(s["a_probs_moved"], 1)
                if jo:
                    act.wait_ge(s["a_out_done"], u + 1)
                    A(yb_hi[:, jp:jp + 5:2, t * P:(t + 1) * P], ps[:, 7, 0:AG * P].rearrange("p (g t) -> p g t", g=AG),
                      ACT.Copy).then_inc(s["a_out_hi_done"], 1)

            for k in range(2):
                act_hi_part("x", range(2 * k, 2 * k + 2), act_hi, g_mix)
                w_hi_part(k)
            for i in range(NT):
                ins = A(junk_x[:, i, :], x_res[:, i, :], ACT.Square, accum_out=ss_x[:, i:i + 1])
            ins.then_inc(s_sq["x"], 1)
            w_chunk(1)
            act.wait_ge(s_rs["x"], 1)
            for c in range(2):
                move(c, *[(zq[:, i, c * MW:(c + 1) * MW], acc(c, i), ACT.Copy, rs_x[:, i:i + 1]) for i in range(NT)])
                w_chunk(c + 2)
            move(2, *[(vx[:, i, :, 0:MDH], acc(2, i).rearrange("p (h d) -> p h d", h=MH), ACT.Copy, rs_x[:, i:i + 1])
                      for i in range(NT)])
            w_chunk(4)
            act.wait_ge(s["half_rsqrt_ready"], 1)
            move(3, *[(zo[:, i, :], acc(3, i), ACT.Tanh, rsh_x[:, i:i + 1]) for i in range(NT)])
            w_chunk(5)
            act.wait_ge(s["aux_moved"], 1)
            act.dma_start(scratch_rows, bias_row[:]).then_inc(ld["bias_rows"], 16)
            move(4, *[m for i in range(NT) for m in (
                (zif[:, i, :], acc(4, i)[:, 0:8], ACT.Copy, rs_x[:, i:i + 1]),
                (zqk[:, i, 0:256], acc(4, i)[:, 8:C_WIDE], ACT.Copy, rs_x[:, i:i + 1]))])
            for hb in range(4):
                act.wait_ge(s["qk_turned"], hb + 1)
                A(pre[:, 2 * hb:2 * hb + 2, 3:S + 3], ps[:, 4 + hb, :].rearrange("p (k s) -> p k s", k=2),
                  ACT.Copy).then_inc(s["conv_in_ready"], 1)
            act.wait_ge(s["neg_abs_f_done"], 1)
            A(rows[:, 3, :], rows[:, 2, :], ACT.Exp)
            act.drain()
            A(rows[:, 4, :], rows[:, 3, :], ACT.Ln, bias=1.0).then_inc(s["log_done"], 1)
            w_chunk(6)

            def attn_in(c):
                lo = C_WIDE - 8 + (c - 5) * COLS
                out_ = []
                for i in range(NT):
                    nqk = min(COLS, max(0, 2 * AW - lo))
                    if nqk:
                        out_.append((zqk[:, i, lo:lo + nqk], acc(c, i)[:, 0:nqk], ACT.Copy, rs_x[:, i:i + 1]))
                    if nqk < COLS:
                        v0 = lo + nqk - 2 * AW
                        out_.append((zv[:, i, v0:v0 + COLS - nqk], acc(c, i)[:, nqk:COLS], ACT.Copy, rs_x[:, i:i + 1]))
                move(c, *out_)

            attn_in(5)
            w_chunk(7)
            act.wait_ge(s["decay_done"], 1)
            A(rows[:, 5, :], rows[:, 4, :], ACT.Exp, scale=-1.0).then_inc(s["floor_rows_done"], 1)
            attn_in(6)
            w_chunk(8)
            act.wait_ge(s["conv_done"], 1)
            A(pre[:, :, 0:S], post[:], ACT.Tanh, scale=0.5).then_inc(s["qk_tanh_done"], 1)
            attn_in(7)
            act.wait_ge(ld["bias_rows"], 16)
            act.dma_start(bias_square, bias_shifted).then_inc(ld["bias_rows"], 16)

            def qk_squares(i):
                if i:
                    act.wait_ge(s["aqk_squares_read"], i)
                A(sq_s[:, 0:2 * AW], zqk[:, i, :], ACT.Square).then_inc(s_sq["att"], 1)

            def gmlp_in(c):
                move(c, *[(zg[:, i, (c - 9) * GW:(c - 8) * GW], acc(c, i), ACT.Copy, rs_x[:, i:i + 1])
                          for i in range(NT)])

            def gate_in(c):
                o = (c - 11) * COLS
                move(c, *[(tg[:, i, o:o + COLS], acc(c, i), ACT.Tanh, rsh_x[:, i:i + 1]) for i in range(NT)])

            w_chunk(9)
            act.wait_ge(ev_act, moved(7)[1])
            qk_squares(0)
            attn_in(8)
            w_chunk(10)
            qk_squares(1)
            gmlp_in(9)
            for b in range(22, 25):
                w_hi_part(b)
            act.wait_ge(s["qk_silu_done"], 1)
            act.wait_ge(s["cols_moved"], 1)
            for h in range(MH):
                act.wait_ge(s["decay_exponents_done"], h + 1)
                if h >= 1:
                    act.wait_ge(s["m_probs_ready"], h)
                A(wgt[:, 0:2 * P], ps[:, 4, 0:2 * P], ACT.Exp, bias=aT[:, h:h + 1])
                A(wgt[:, 2 * P:3 * P], ps[:, 4, 2 * P:3 * P], ACT.Exp, bias=aT[:, MH + h:MH + h + 1]).then_inc(s["decay_weights_done"], 1)
                if h == 0:
                    gmlp_in(10)
                else:
                    numer_out(h - 1)
                if h == 2:
                    gate_in(11)
                w_hi_part(25 + h)
            numer_out(MH - 1)
            act.wait_ge(ld["bias_rows"], 32)
            act.dma_start(toep[:], bias_square.rearrange("h p x -> p h x")).then_inc(ld["toep"], 16)
            act.wait_ge(s["numer_moved"], MH)
            act.wait_ge(s["aqk_squares_read"], NT)
            A(sq_s[:, 0:MH * NT * P].rearrange("p (i h d) -> p i h d", i=NT, h=MH), numer[:, :, :, 0:MDH],
              ACT.Square).then_inc(s_sq["mls"], 1)
            gate_in(12)
            A(zg[:], zg[:], ACT.Gelu_apprx_tanh).then_inc(s["gelu_done"], 1)
            act.wait_ge(s["gelu_done"], 1)
            A(sq_g[:], zg[:, :, GW:2 * GW], ACT.Square).then_inc(s_sq["gml"], 1)
            w_hi_part(29)
            act.wait_ge(s["numer_used"], 1)
            for n in range(6):
                if n == 4:
                    w_hi_part(30)
                act.wait_ge(s["aqk_turned"], n + 1)
                A(qkT[:, 2 * n:2 * n + 2, :], ps[:, 4 + n % 4, :].rearrange("p (k s) -> p k s", k=2), ACT.Copy,
                  scale=g_qk[:, n // 3:n // 3 + 1]).then_inc(s["aqk_moved"], 1)
            gate_in(13)

            def attn_exp(u):
                t = u // 2 % 2
                lg = (lg0, lg1)[u % 2]
                act.wait_ge(s["a_max_done"], u + 1)
                A(lg[:, :, 0:(t + 1) * P], lg[:, :, 0:(t + 1) * P], ACT.Exp, bias=a_nm[:, u:u + 1],
                  accum_out=a_sum[:, u:u + 1]).then_inc(s["a_exp_done"], 1)

            attn_exp(0)
            for u in range(8):
                if u in filled:
                    w_hi_part(31 + blocks_before[u])
                if u < 7:
                    attn_exp(u + 1)
                attn_out(u)
                if u in filled and blocks_before[u + 1] % 2 == 0:
                    gate_in(13 + blocks_before[u + 1] // 2)
            w_hi_part(37)
            act.wait_ge(s["a_out_done"], 8)
            for i in range(NT):
                act.dma_start(mem_x[:, i, :], d_in["mem"][0, i * P:(i + 1) * P, :]).then_inc(ld["mem"], 16)
            w_hi_part(38)
            act_hi_part("a", range(2), ya_hi, g_mls)
            act_hi_part("c", range(2), yc_hi, bank0=6)
            w_hi_part(39)
            act.wait_ge(ld["mem"], 16 * NT)
            for i in range(NT):
                ins = A(junk_mem[:, i, :], mem_x[:, i, :], ACT.Square, accum_out=ss_mem[:, i:i + 1])
            ins.then_inc(s_sq["mem"], 1)
            w_hi_part(40)
            act_hi_part("mem", range(4), act_hi, g_mem)
            for b in range(41, 46):
                w_hi_part(b)
            act_hi_part("merged", range(2), mg_hi)
            w_hi_part(46)
            act_hi_part("merged", range(2, 4), mg_hi)
            act.wait_ge(s_rs["mem"], 1)
            move(C_K, *[(xkv[:, i, 0:XW], acc(C_K, i), ACT.Copy, rs_mem[:, i:i + 1]) for i in range(NT)])
            w_hi_part(47)
            act.wait_ge(*moved(C_K))
            A(sq_k[:], xkv[:, :, 0:XW], ACT.Square).then_inc(s_sq["xk"], 1)
            w_hi_part(48)
            w_hi_part(49)
            act_hi_part("x1", range(2), mg_hi, g_xat)
            w_hi_part(50)
            w_hi_part(51)
            act.wait_ge(*moved(C_OUT + 1))
            for i in range(NT):
                ins = A(junk_1[:, i, :], x_res[:, i, :], ACT.Square, accum_out=ss_1[:, i:i + 1])
            ins.then_inc(s_sq["x1"], 1)
            act_hi_part("x1", range(2, 4), mg_hi, g_xat)
            w_hi_part(52)
            w_hi_part(53)
            for hb in range(2):
                act.wait_ge(s["xk_turned"], hb + 1)
                A(xkT[:, 2 * hb:2 * hb + 2, :], ps[:, 6 + hb, :].rearrange("p (k s) -> p k s", k=2), ACT.Copy,
                  scale=g_xqk[:, 1:2]).then_inc(s["xk_moved"], 1)
            act.wait_ge(*moved(C_XQ))
            A(sq_q[:], xq[:], ACT.Square).then_inc(s_sq["xq"], 1)
            act.dma_start(router_w[:], d_in["router_w"].rearrange("(t p) e -> p t e", t=KD)).then_inc(ld["moe"], 16)
            act.dma_start(g_ffn_row[:], d_in["norm_ffn"].to_broadcast([P, D])).then_inc(ld["moe"], 16)
            move(C_V1, *[(xkv[:, i, XW:2 * XW], acc(C_V1, i), ACT.Copy, rs_mem[:, i:i + 1]) for i in range(NT)])
            for hb in range(2):
                act.wait_ge(s["xq_turned"], hb + 1)
                A(xqT[:, 2 * hb:2 * hb + 2, :], ps[:, 4 + hb, :].rearrange("p (k s) -> p k s", k=2), ACT.Copy,
                  scale=g_xqk[:, 0:1]).then_inc(s["xq_moved"], 1)
            for v in range(2 * NT):
                act.wait_ge(s["x_max_done"], v + 1)
                for k in range(2):
                    ins = A(xp[:, v // 2, (v % 2 * 2 + k) * S:(v % 2 * 2 + k + 1) * S], ps[:, 4 + v, k * S:(k + 1) * S],
                            ACT.Exp, scale=XDH ** -0.5, bias=x_nm[:, 2 * v + k:2 * v + k + 1],
                            accum_out=x_sum[:, 2 * v + k:2 * v + k + 1])
                ins.then_inc(s["x_exp_done"], 1)
            for t in range(NT):
                for hb in range(2):
                    act.wait_ge(s["x_probs_turned"], 2 * t + hb + 1)
                    A(xpT[:, 2 * hb:2 * hb + 2, :, t * P:(t + 1) * P],
                      ps[:, 4 + 2 * t + hb, :].rearrange("p (h m t) -> p h m t", h=2, m=NT), ACT.Copy).then_inc(s["x_probs_moved"], 1)
            act_hi_part("o", range(2), oT_hi)

            def e_hi(q, n):
                b, nt = NB1 + n, 4 - direct.get(n % GB, 0)
                raw, landed, nth = e_slot(n)
                act.wait_ge(landed, 16 * (GB // E_RING) * q + 16 * nth)
                act.wait_ge(mm_done, GB * q + (b - RING + 1))
                A(w_hi[:, b % RING, 0:nt * COLS], raw[:, 0:nt * COLS], ACT.Copy).then_inc(hi_done, 1)

            for n in range(2):
                e_hi(0, n)

            act.wait_ge(*moved(C_XO))

            def x2_out(hb):
                act.wait_ge(sT["x2"], hb + 1)
                for k in range(2):
                    ins = A(x2T[:, 2 * hb + k, :], ps[:, 4 + hb, k * S:(k + 1) * S], ACT.Copy,
                            scale=g_ffn[:, 2 * hb + k:2 * hb + k + 1])
                ins.then_inc(s["x2T_moved"], 1)

            x2_out(0)
            x2_out(1)
            for n in range(2):
                if n:
                    act.wait_ge(*moved(C_XO + 1))
                for i in range(NT):
                    cs = slice(n * COLS, (n + 1) * COLS)
                    ins = A(junk_2[:, i, cs], x_res[:, i, cs], ACT.Square, accum_out=ss_2h[:, 2 * n + i:2 * n + i + 1])
            ins.then_inc(s_sq["x2"], 1)
            x2_out(2)
            x2_out(3)
            act.wait_ge(s["h_full_done"], 1)
            A(h_hi[:].rearrange("q i (t p) -> q i t p", t=KD), h_full[:].rearrange("q i (p t) -> q i t p", t=KD),
              ACT.Copy).then_inc(s["h_hi_done"], 1)
            act.wait_ge(s["router_max_taken"], 1)
            A(prob[:], prob[:], ACT.Exp).then_inc(s["router_exp_done"], 1)
            for n in range(2, RING):
                e_hi(0, n)

            act.wait_ge(s["rounds_ready"], 1)
            rounds = act.value_load(n_rounds_i[0:1, 0:1], min_val=1, max_val=S // SLOTS)

            def gathered(q, tiles):
                for t in tiles:
                    act.wait_ge(s["gathered"], FREE + KD * q + (t + 1))
                    A(xg[:, t, :, :].rearrange("p e (w c) -> p w e c", w=2),
                      ps[:, t % 2, :].rearrange("p (w e c) -> p w e c", w=2, e=EPG), ACT.Copy).then_inc(s["gathered_moved"], 1)

            def y_hi_part(q, m, j):
                act.wait_ge(mm_done, GB * q + (NB1 + 2 * m + 2))
                act.wait_ge(s["scattered"], FREE + EPG * q + j)
                for half in range(2):
                    ins = A(y_hi[:, half * COLS:(half + 1) * COLS], ps[:, 2 + half, :], ACT.Copy, scale=w_slot[:, j:j + 1])
                ins.then_inc(s["y_hi_done"], 1)

            def expert_group(q, more):
                for m, (j, which) in enumerate(ex_order[:-1]):
                    early, late = list(split_steps(m, more, ahead=1)), []
                    if which == "up":
                        early, late = early[:1], early[1:]
                    for n in early:
                        e_hi(q, n)
                    if which == "gate":
                        act.wait_ge(mm_done, GB * q + (NB1 + 2 * m + 2))
                        A(gu[:, 0, :], ps[:, 0, :], ACT.Copy).then_inc(s["gu_moved"], 1)
                        if j == 0:
                            for half in range(2):
                                act.wait_ge(s["sel_turned"], FREE + 2 * q + (half + 1))
                                A(selT[:, 2 * half:2 * half + 2, :], ps[:, 2 + half, :].rearrange("p (e t) -> p e t", e=2),
                                  ACT.Copy).then_inc(s["selT_moved"], 1)
                    elif which == "up":
                        act.wait_ge(mm_done, GB * q + (NB1 + 2 * m + 2))
                        A(gu[:, 1, :], ps[:, 1, :], ACT.Copy).then_inc(s["gu_moved"], 1)
                        for n in late:
                            e_hi(q, n)
                        act.wait_ge(s["gu_turned"], EPG * q + (j + 1))
                        A(e_act[:, 0], ps[:, 2, :].rearrange("p (k c) -> p k c", c=P)[:, :, 0:SLOTS], ACT.Tanh,
                          scale=0.5).then_inc(s["gate_tanh_done"], 1)
                    else:
                        y_hi_part(q, m, j)
                if more:
                    b1, b2 = split_steps(len(ex_order) - 1, more, ahead=1)
                    gathered(q + 1, range(0, 2))
                    e_hi(q, b1)
                    gathered(q + 1, range(2, 4))
                y_hi_part(q, len(ex_order) - 1, EPG - 1)
                if more:
                    gathered(q + 1, range(4, 6))
                    e_hi(q, b2)
                    gathered(q + 1, range(6, KD))
                for n in split_steps(len(ex_order), more, ahead=1):
                    e_hi(q, n)

            for name in ("y_hi_done", "gu_moved"):
                act.drain().then_inc(s[name], FREE)
            with act.Fori(0, rounds) as r:
                gathered(r * NG, range(KD))
                with act.If(r > 0):
                    for n in range(RING):
                        e_hi(r * NG, n)
                with act.Fori(0, NG - 1) as g:
                    expert_group(r * NG + g, True)
                expert_group(r * NG + (NG - 1), False)

        @block.gpsimd
        def _(pool):
            def rsqrt(n, dst, src, w):
                pool.wait_ge(s_ms[n], 1)
                nc.gpsimd.tensor_tensor(dst, src, minus_half[:, 0:w], ALU.pow).then_inc(s_rs[n], 1)

            pool.wait_ge(ld["const"], 16)
            rsqrt("x", rs_x, ss_x, 2)
            rsqrt("att", rs_a, ss_a, 48)
            rsqrt("mls", rs_m, ss_m, 8)
            rsqrt("gml", rs_g, ss_g, 8)
            rsqrt("mem", rs_mem, ss_mem, 2)
            rsqrt("xk", rs_k, ss_k, 8)
            rsqrt("x1", rs_1, ss_1, 2)
            rsqrt("xq", rs_q, ss_q, 8)
            rsqrt("x2", rs_2, ss_2, 2)
            pool.wait_ge(s["h_hi_done"], 1)
            nc.gpsimd.tensor_tensor(h_lo[:].rearrange("q i (t p) -> q i t p", t=KD),
                                    h_full[:].rearrange("q i (p t) -> q i t p", t=KD),
                                    f32(h_hi[:]).rearrange("q i (t p) -> q i t p", t=KD),
                                    ALU.subtract).then_inc(s["h_lo_done"], 1)

        @block.vector
        def _(dve):
            V = nc.vector

            def w_lo_part(b):
                dve.wait_ge(hi_done, b + 1)
                if b >= RING:
                    dve.wait_ge(mm_done, b - RING + 1)
                sh = blocks[b].shape
                V.tensor_tensor(bview(w_lo, b, sh), bview(w_raw, b, sh), f32(bview(w_hi, b, sh)),
                                ALU.subtract).then_inc(lo_done, 1)

            def w_chunk(c):
                for b in range(first_block[c], first_block[c + 1]):
                    w_lo_part(b)

            def act_lo_part(n, banks, dst, hi, gain=None, bank0=4):
                for hb in banks:
                    dve.wait_ge(sH[n], hb + 1)
                    if gain is None:
                        ins = V.tensor_tensor(dst[:, 2 * hb:2 * hb + 2, :],
                                              ps[:, bank0 + hb, :].rearrange("p (k s) -> p k s", k=2),
                                              f32(hi[:, 2 * hb:2 * hb + 2, :]), ALU.subtract)
                    else:
                        for k in range(2):
                            ins = V.scalar_tensor_tensor(dst[:, 2 * hb + k, :], ps[:, bank0 + hb, k * S:(k + 1) * S],
                                                         gain[:, 2 * hb + k:2 * hb + k + 1], f32(hi[:, 2 * hb + k, :]),
                                                         ALU.mult, ALU.subtract)
                    ins.then_inc(sL[n], 1)

            def mean_square(n, ss, width, sq_=None):
                dve.wait_ge(s_sq[n], 1)
                if sq_ is not None:
                    V.reduce_sum(ss, sq_, AX.X)
                    dve.drain()
                V.tensor_scalar(ss, ss, 1.0 / width, EPS, ALU.mult, ALU.add).then_inc(s_ms[n], 1)

            def acc(c, i, n=COLS):
                return ps[:, (c % 2) * 2 + i, 0:n]

            def by_row(v, n, m):
                return bc(v.unsqueeze(2), (P, n, m))

            for k in range(2):
                act_lo_part("x", range(2 * k, 2 * k + 2), act_lo, act_hi, g_mix)
                w_lo_part(k)
            mean_square("x", ss_x, D)
            w_chunk(1)
            V.memset(vx[:, :, :, MDH:MDH + 2], 1.0)
            V.memset(pre[:, :, 0:3], 0.0)
            dve.wait_ge(s_rs["x"], 1)
            V.tensor_scalar(rsh_x, rs_x, 0.5, None, ALU.mult).then_inc(s["half_rsqrt_ready"], 1)
            w_chunk(2)
            w_chunk(3)
            dve.wait_ge(ld["aux"], 192)
            dve.wait_ge(ld["const"], 16)
            V.memset(table[REL_BUCKETS:REL_BUCKETS + 1, :], NEG)
            V.tensor_tensor(ws_t[:], ws_t[:], bc(keep_past.unsqueeze(1), (P, GG, P)), ALU.mult).then_inc(s["ws_masked"], 1)
            w_chunk(4)
            dve.wait_ge(s["aux_turned"], 1)
            V.tensor_copy(cw[:], ps[:, 4, 0:32])
            V.tensor_copy(vec_cols[:], ps[:, 4, 32:40 + 2 * KD])
            V.tensor_copy(wT[:], ps[:, 5, :].rearrange("p (g t) -> p g t", g=GG))
            V.tensor_copy(bias_row[:, 0, :], ps[0:AHG, 6, 0:TOEP])
            V.tensor_copy(bias_row[:, 1, :], ps[0:AHG, 7, 0:TOEP])
            V.tensor_copy(bias_row[:, 2, :], ps[0:AHG, 4, P:P + TOEP]).then_inc(s["aux_moved"], 1)
            w_chunk(5)
            dve.wait_ge(s["gates_turned"], 1)
            V.memset(rows[:, 5, :], 1.0)
            V.tensor_scalar(rows[:, 0, :], ps[0:MH, 4, 0:S], gate_bi[:], None, ALU.add)
            V.tensor_scalar(rows[:, 1, :], ps[0:MH, 4, S:2 * S], gate_bf[:], None, ALU.add)
            dve.drain()
            V.scalar_tensor_tensor(rows[:, 2, :], rows[:, 1, :], -1.0, rows[:, 1, :], ALU.mult, ALU.min).then_inc(s["neg_abs_f_done"], 1)
            w_chunk(6)
            dve.wait_ge(s["log_done"], 1)
            V.scalar_tensor_tensor(rows[:, 1, :], rows[:, 1, :], 0.0, rows[:, 4, :], ALU.min, ALU.subtract)
            dve.drain()
            V.tensor_tensor_scan(rows[:, 2, :], rows[:, 5, :], rows[:, 1, :], 0.0, ALU.mult, ALU.add)
            dve.drain()
            V.tensor_tensor(rows[:, 0, :], rows[:, 0, :], rows[:, 2, :], ALU.subtract)
            dve.drain()
            V.tensor_tensor_scan(rows[:, 3, :], rows[:, 5, :], rows[:, 0, :], 0.0, ALU.mult, ALU.max)
            dve.drain()
            V.tensor_tensor(rows[:, 4, :], rows[:, 2, :], rows[:, 3, :], ALU.add).then_inc(s["decay_done"], 1)
            w_chunk(7)
            dve.wait_ge(s["conv_in_ready"], 4)

            def tap(w):
                for f in range(KD):
                    c = cw[:, w * KD + f:w * KD + f + 1]
                    if w == 0:
                        ins = V.tensor_scalar(post[:, f, :], pre[:, f, 0:S], c, None, ALU.mult)
                    else:
                        ins = V.scalar_tensor_tensor(post[:, f, :], pre[:, f, w:w + S], c, post[:, f, :], ALU.mult, ALU.add)
                return ins

            tap(0)
            dve.drain()
            tap(1)
            w_chunk(8)
            dve.drain()
            tap(2)
            dve.drain()
            tap(3).then_inc(s["conv_done"], 1)
            w_chunk(9)
            dve.wait_ge(s["cols_turned"], 1)
            V.tensor_copy(stat[:, st_at["aT"][0]:st_at["aT"][0] + 16], ps[:, 5, 0:16]).then_inc(s["cols_moved"], 1)
            dve.wait_ge(s["qk_tanh_done"], 1)
            V.scalar_tensor_tensor(post[:], pre[:, :, 0:S], 1.0, post[:], ALU.add, ALU.mult).then_inc(s["qk_silu_done"], 1)
            w_chunk(10)
            for i in range(NT):
                dve.wait_ge(s_sq["att"], i + 1)
                V.reduce_sum(ss_a[:, 24 * i:24 * i + 24], sq_s[:, 0:2 * AW].rearrange("p (n d) -> p n d", d=ADH),
                             AX.X).then_inc(s["aqk_squares_read"], 1)
            dve.drain()
            V.tensor_scalar(ss_a, ss_a, 1.0 / ADH, EPS, ALU.mult, ALU.add).then_inc(s_ms["att"], 1)
            for b in range(22, 25):
                w_lo_part(b)
            for h in range(MH):
                dve.wait_ge(s["scores_done"], h + 1)
                dve.wait_ge(s["decay_weights_done"], h + 1)
                if h >= 2:
                    dve.wait_ge(s["numer_done"], h - 1)
                V.scalar_tensor_tensor(pm[:, h % 2, :], ps[:, 5, 0:3 * P], 0.25 * MDH ** -0.5, wgt[:], ALU.mult,
                                       ALU.mult).then_inc(s["m_probs_ready"], 1)
                w_lo_part(25 + h)
                if h == 0:
                    dve.wait_ge(s_rs["att"], 1)
                    zqk48 = zqk[:].rearrange("p i (n d) -> p (i n) d", d=ADH)
                    V.tensor_tensor(zqk48, zqk48, by_row(rs_a, 48, ADH), ALU.mult).then_inc(s["aqk_ready"], 1)
            dve.wait_ge(s["numer_moved"], MH)
            dn = numer[:, :, :, MDH]
            v8 = lambda v: v.rearrange("p (i h) -> p i h", i=NT)
            V.scalar_tensor_tensor(v8(den), dn, -1.0, dn, ALU.mult, ALU.max)
            zo8 = zo[:].rearrange("p i (h d) -> p (i h) d", d=MDH)
            V.scalar_tensor_tensor(zo8, zo8, 1.0, numer[:].rearrange("p i h d -> p (i h) d")[:, :, 0:MDH], ALU.add,
                                   ALU.mult).then_inc(s["numer_used"], 1)
            dve.drain()
            V.tensor_tensor(den, den, emT, ALU.max)
            dve.drain()
            V.reciprocal(rden, den)
            dve.wait_ge(s_sq["mls"], 1)
            V.reduce_sum(ss_m, sq_s[:, 0:NT * MW].rearrange("p (n d) -> p n d", d=MDH), AX.X)
            dve.drain()
            V.tensor_tensor(ss_m, ss_m, rden, ALU.mult)
            dve.drain()
            V.tensor_tensor(ss_m, ss_m, rden, ALU.mult)
            dve.drain()
            V.tensor_scalar(ss_m, ss_m, 1.0 / MDH, EPS, ALU.mult, ALU.add).then_inc(s_ms["mls"], 1)
            mean_square("gml", ss_g, GC, sq_g[:].rearrange("p i (n d) -> p (i n) d", d=GC))
            w_lo_part(29)
            dve.wait_ge(s_rs["mls"], 1)
            V.scalar_tensor_tensor(den, rden, 0.5, rs_m, ALU.mult, ALU.mult)
            dve.drain()
            V.tensor_tensor(zo8, zo8, by_row(den, NT * MH, MDH), ALU.mult).then_inc(s["ya_done"], 1)
            dve.wait_ge(s_rs["gml"], 1)
            for i in range(NT):
                gv = zg[:, i, GW:2 * GW].rearrange("p (n d) -> p n d", d=GC)
                V.tensor_tensor(gv, gv, by_row(rs_g[:, GG * i:GG * i + GG], GG, GC), ALU.mult)
            dve.drain()
            dve.wait_ge(ld["small"], 16 * 4)
            for i in range(NT):
                ins = V.tensor_tensor(zg[:, i, GW:2 * GW], zg[:, i, GW:2 * GW], gs_gain[:], ALU.mult)
            ins.then_inc(s["gv_ready"], 1)
            w_lo_part(30)
            dve.wait_ge(ld["toep"], 16)

            def attn_logits(u):
                jp, t, jo = u // 4, u // 2 % 2, u % 2
                j, w = 2 * jp + jo, (t + 1) * P
                lg = (lg0, lg1)[u % 2]
                dve.wait_ge(s["a_logits_done"], u + 1)
                if u >= 2:
                    dve.wait_ge(s["a_probs_turned"], fills_before[u - 1])
                else:
                    dve.wait_ge(s["aqk_moved"], 6)
                heads = toep[:, :, P * (1 - t):P * (1 - t) + w]
                V.scalar_tensor_tensor(lg[:, 0:2, 0:w], ps[:, 4, :].rearrange("p (g x) -> p g x", g=2)[:, :, 0:w],
                                       ADH ** -0.5, heads[:, j:j + 5:4, :], ALU.mult, ALU.add)
                V.scalar_tensor_tensor(lg[:, 2, 0:w], ps[:, 5, 0:w], ADH ** -0.5, heads[:, 8 + j, :], ALU.mult,
                                       ALU.add).then_inc(s["a_logits_moved"], 1)
                dve.drain()
                V.tensor_reduce(a_nm[:, u:u + 1], lg[:, :, 0:w], AX.XY, ALU.max, negate=True).then_inc(s["a_max_done"], 1)

            def attn_norm(u):
                t = u // 2 % 2
                lg = (lg0, lg1)[u % 2]
                dve.wait_ge(s["a_exp_done"], u + 1)
                V.reciprocal(a_rec[:, u:u + 1], a_sum[:, u:u + 1])
                dve.drain()
                V.tensor_scalar(lg[:, :, 0:(t + 1) * P], lg[:, :, 0:(t + 1) * P], a_rec[:, u:u + 1], None,
                                ALU.mult).then_inc(s["a_probs_ready"], 1)

            def attn_lo(u):
                jp, t, jo = u // 4, u // 2 % 2, u % 2
                dve.wait_ge(s["a_out_hi_done"], u // 2 + 1)
                V.tensor_tensor(yb_lo[:, jp:jp + 5:2, t * P:(t + 1) * P],
                                ps[:, 7, 0:AG * P].rearrange("p (g t) -> p g t", g=AG),
                                f32(yb_hi[:, jp:jp + 5:2, t * P:(t + 1) * P]), ALU.subtract).then_inc(s["a_out_lo_done"], 1)

            attn_logits(0)
            for n in range(NT):
                dve.wait_ge(s["gv_mixed"], n + 1)
                for g in range(GG):
                    u_ = zg[:, n, g * GC:(g + 1) * GC]
                    ins = V.scalar_tensor_tensor(u_, ps[:, 6 + n, g * GC:(g + 1) * GC], gs_b[:, g:g + 1], u_, ALU.add, ALU.mult)
                ins.then_inc(s["yc_done"], 1)
            attn_norm(0)
            for u in range(8):
                if u < 7:
                    attn_logits(u + 1)
                if u in filled:
                    w_lo_part(31 + blocks_before[u])
                if u < 7:
                    attn_norm(u + 1)
                if u % 2:
                    attn_lo(u)

            def branch(c):
                k, n = {C_B: 1, C_A: 0, C_C: 2}[c - (c - C_B) % 2], (c - C_B) % 2
                dve.wait_ge(mm_done, first_block[c + 1])
                for i in range(NT):
                    t_ = tg[:, i, k * D + n * COLS:k * D + (n + 1) * COLS]
                    ins = V.scalar_tensor_tensor(t_, t_, 1.0, acc(c, i), ALU.add, ALU.mult)
                ins.then_inc(ev_dve, 1)
                if c >= C_A:
                    other = 2 if k else 1
                    dve.drain()
                    for i in range(NT):
                        m_ = merged[:, i, n * COLS:(n + 1) * COLS]
                        ins = V.tensor_tensor(m_, m_, tg[:, i, other * D + n * COLS:other * D + (n + 1) * COLS], ALU.add)
                    if k == 2:
                        ins.then_inc(s["merged_ready"], 1)
                    dve.drain()

            def residual_add(c, n, scale):
                dve.wait_ge(mm_done, first_block[c + 1])
                for i in range(NT):
                    x_ = x_res[:, i, n * COLS:(n + 1) * COLS]
                    ins = V.scalar_tensor_tensor(x_, acc(c, i), scale, x_, ALU.mult, ALU.add)
                ins.then_inc(ev_dve, 1)

            w_lo_part(37)
            w_lo_part(38)
            act_lo_part("a", range(2), ya_lo, ya_hi, g_mls)
            act_lo_part("c", range(2), yc_lo, yc_hi, bank0=6)
            branch(C_B)
            w_lo_part(39)
            mean_square("mem", ss_mem, D)
            w_lo_part(40)
            branch(C_B + 1)
            act_lo_part("mem", range(4), act_lo, act_hi, g_mem)
            w_lo_part(41)
            branch(C_A)
            w_lo_part(42)
            branch(C_A + 1)
            w_lo_part(43)
            branch(C_C)
            w_lo_part(44)
            branch(C_C + 1)
            w_lo_part(45)
            act_lo_part("merged", range(2), mg_lo, mg_hi)
            w_lo_part(46)
            act_lo_part("merged", range(2, 4), mg_lo, mg_hi)
            w_lo_part(47)
            mean_square("xk", ss_k, XDH, sq_k[:].rearrange("p i (h d) -> p (i h) d", d=XDH))
            w_lo_part(48)
            dve.wait_ge(s_rs["xk"], 1)
            for i in range(NT):
                kk = xkv[:, i, 0:XW].rearrange("p (n d) -> p n d", d=XDH)
                ins = V.tensor_tensor(kk, kk, by_row(rs_k[:, XH * i:XH * i + XH], XH, XDH), ALU.mult)
            ins.then_inc(s["xk_ready"], 1)
            residual_add(C_OUT, 0, 0.5)
            w_lo_part(49)
            act_lo_part("x1", range(2), mg_lo, mg_hi, g_xat)
            w_lo_part(50)
            residual_add(C_OUT + 1, 1, 0.5)
            w_lo_part(51)
            mean_square("x1", ss_1, D)
            act_lo_part("x1", range(2, 4), mg_lo, mg_hi, g_xat)
            w_lo_part(52)
            w_lo_part(53)
            dve.wait_ge(s_rs["x1"], 1)
            dve.wait_ge(mm_done, first_block[C_XQ + 1])
            for i in range(NT):
                ins = V.tensor_scalar(xq[:, i, :], acc(C_XQ, i), rs_1[:, i:i + 1], None, ALU.mult)
            ins.then_inc(ev_dve, 1)
            dve.wait_ge(*moved(C_XQ))
            mean_square("xq", ss_q, XDH, sq_q[:].rearrange("p i (h d) -> p (i h) d", d=XDH))
            dve.wait_ge(s_rs["xq"], 1)
            qv = xq[:].rearrange("p i (h d) -> p (i h) d", d=XDH)
            V.tensor_tensor(qv, qv, by_row(rs_q, NT * XH, XDH), ALU.mult).then_inc(s["xq_ready"], 1)

            def x_maxima(v):
                dve.wait_ge(s["x_logits_done"], v + 1)
                nm = x_nm[:, 2 * v:2 * v + 2]
                V.reduce_max(nm, ps[:, 4 + v, :].rearrange("p (h m) -> p h m", h=2), AX.X)
                dve.drain()
                V.tensor_scalar(nm, nm, -(XDH ** -0.5), None, ALU.mult).then_inc(s["x_max_done"], 1)

            def x_normalise(v):
                dve.wait_ge(s["x_exp_done"], v + 1)
                V.reciprocal(x_rec[:, 2 * v:2 * v + 2], x_sum[:, 2 * v:2 * v + 2])
                dve.drain()
                pv_ = xp[:, v // 2, v % 2 * 2 * S:(v % 2 + 1) * 2 * S].rearrange("p (h m) -> p h m", h=2)
                V.tensor_tensor(pv_, pv_, by_row(x_rec[:, 2 * v:2 * v + 2], 2, S), ALU.mult).then_inc(s["x_probs_ready"], 1)

            x_maxima(0)
            x_maxima(1)
            for v in range(2 * NT):
                if v + 2 < 2 * NT:
                    x_maxima(v + 2)
                x_normalise(v)
            act_lo_part("o", range(2), oT_lo, oT_hi)
            V.memset(zeros, 0.0).then_inc(s["zeros_written"], 1)

            def e_lo(q, n):
                b, nt = NB1 + n, 4 - direct.get(n % GB, 0)
                dve.wait_ge(hi_done, GB * q + (b + 1))
                V.tensor_tensor(w_lo[:, b % RING, 0:nt * COLS], e_slot(n)[0][:, 0:nt * COLS], f32(w_hi[:, b % RING, 0:nt * COLS]),
                                ALU.subtract).then_inc(lo_done, 1)

            for k in range(2):
                e_lo(0, k)
            for n in range(2):
                residual_add(C_XO + n, n, 1.0)
            dve.wait_ge(*moved(C_XO + 1))

            dve.wait_ge(s_sq["x2"], 1)
            V.tensor_tensor(ss_2, ss_2h[:, 0:2], ss_2h[:, 2:4], ALU.add)
            dve.drain()
            mean_square("x2", ss_2, D)
            dve.wait_ge(s_rs["x2"], 1)
            dve.wait_ge(ld["moe"], 32)
            for i in range(NT):
                ins = V.scalar_tensor_tensor(h_full[:, i, :], x_res[:, i, :], rs_2[:, i:i + 1], g_ffn_row[:], ALU.mult, ALU.mult)
            ins.then_inc(s["h_full_done"], 1)
            dve.wait_ge(s["router_logits_done"], 1)
            v2 = lambda v: v.rearrange("p (i e) -> p i e", i=NT)
            v84 = lambda v: v.rearrange("p (n e) -> p n e", e=EPG)
            v24 = lambda v: v.rearrange("p (i g) -> p i g", g=NG)

            def two(v, n):
                return bc(v.unsqueeze(2), (P, NT, n))

            for i in range(NT):
                V.scalar_tensor_tensor(prob[:, i * NE:(i + 1) * NE], ps[:, 2 + i, 0:NE], rs_2[:, i:i + 1],
                                       router_b[:], ALU.mult, ALU.add)
            dve.drain()
            V.reduce_max(rmax, v2(prob), AX.X)
            dve.drain()
            V.tensor_tensor(v2(prob), v2(prob), two(rmax, NE), ALU.subtract).then_inc(s["router_max_taken"], 1)
            dve.wait_ge(s["router_exp_done"], 1)
            V.reduce_sum(rsum, v2(prob), AX.X)
            dve.drain()
            V.reciprocal(rrec, rsum)
            dve.drain()
            V.tensor_tensor(v2(prob), v2(prob), two(rrec, NE), ALU.mult)
            dve.drain()
            four = (P, NT * NG, EPG, EPG)
            p_i, p_j = bc(v84(prob).unsqueeze(2), four), bc(v84(prob).unsqueeze(3), four)
            m4 = lambda v: v.rearrange("p (n j i) -> p n j i", j=EPG, i=EPG)
            V.tensor_tensor(m4(gt), p_i, p_j, ALU.is_gt)
            V.tensor_tensor(m4(ge), p_i, p_j, ALU.is_ge)
            dve.drain()
            V.tensor_tensor(ge, ge, gt, ALU.subtract)
            dve.drain()
            V.tensor_tensor(m4(ge), m4(ge), bc(tie.unsqueeze(1), four), ALU.mult)
            dve.drain()
            V.tensor_tensor(gt, gt, ge, ALU.add)
            dve.drain()
            V.reduce_sum(v84(rank), m4(gt), AX.X)
            dve.drain()
            V.scalar_tensor_tensor(r2, rank, 2.0, prob, ALU.is_lt, ALU.mult)
            dve.drain()
            V.reduce_sum(score, v84(r2), AX.X)
            dve.drain()
            V.reduce_max(best, v24(score), AX.X)
            V.memset(earlier, 0.0)
            dve.drain()
            V.tensor_tensor(v24(eq), v24(score), two(best, NG), ALU.is_equal)
            dve.drain()
            for g in range(1, NG):
                V.tensor_tensor(v24(earlier)[:, :, g], v24(earlier)[:, :, g - 1], v24(eq)[:, :, g - 1], ALU.add)
                dve.drain()
            V.scalar_tensor_tensor(first, earlier, 0.0, eq, ALU.is_equal, ALU.mult)
            dve.drain()
            one_group = bc(first.unsqueeze(2), (P, NT * NG, EPG))
            V.tensor_tensor(v84(topw), v84(r2), one_group, ALU.mult)
            V.scalar_tensor_tensor(v84(chosen), v84(rank), 2.0, one_group, ALU.is_lt, ALU.mult).then_inc(s["chosen"], 1)
            dve.drain()
            V.reduce_sum(rsum, v2(topw), AX.X)
            dve.drain()
            V.reciprocal(rrec, rsum)
            dve.drain()
            V.tensor_tensor(v2(gates), v2(topw), two(rrec, NE), ALU.mult)
            dve.drain()
            V.tensor_copy(gates_split[:, :, 0], v2(gates))
            dve.drain()
            V.tensor_tensor(gates_split[:, :, 1], v2(gates), f32(gates_split[:, :, 0]), ALU.subtract)
            dve.wait_ge(s["places_done"], 1)
            V.scalar_tensor_tensor(posm, ps[:, 1, 0:NT * NE], 1.0, chosen, ALU.add, ALU.mult)
            V.reduce_max(total[:, 0:1], ps[:, 1, NT * NE:NT * NE + NE], AX.X)
            dve.drain()
            V.tensor_scalar(posm, posm, -1.0, None, ALU.add)
            V.tensor_scalar(total[:, 1:2], total[:, 0:1], float(SLOTS), 1.0, ALU.is_gt, ALU.add)
            dve.drain()
            for k in range(2, S // SLOTS):
                V.scalar_tensor_tensor(total[:, 1:2], total[:, 0:1], float(k * SLOTS), total[:, 1:2], ALU.is_gt, ALU.add)
                dve.drain()
            V.tensor_copy(n_rounds_i[:], total[0:1, 1:2]).then_inc(s["rounds_ready"], 1)

            dve.wait_ge(s["rounds_ready"], 1)
            rounds = dve.value_load(n_rounds_i[0:1, 0:1], min_val=1, max_val=S // SLOTS)

            def select(q, g):
                dve.wait_ge(s["gathered"], FREE + KD * q)
                dve.wait_ge(s["sel_turned"], FREE + 2 * q)
                for i in range(NT):
                    V.tensor_copy(gcur[:, i], f32(gates_split[:, i, :, bass.ds(g * EPG, EPG)]))
                    ins = V.tensor_tensor(sel[:, i], bc(iota.unsqueeze(1), (P, EPG, P)),
                                          bc(v2(posm)[:, i, bass.ds(g * EPG, EPG)].unsqueeze(2), (P, EPG, P)), ALU.is_equal)
                ins.then_inc(s["sel_ready"], 1)

            def slot_gates(q):
                dve.wait_ge(s["slot_gates_done"], q + 1)
                diagonal = lambda o: ps[:, 1, o:o + (EPG - 1) * (2 * EPG + 1) + 1:2 * EPG + 1]
                V.tensor_copy(w_slot_next[:], diagonal(0))
                dve.drain()
                V.tensor_tensor(w_slot_next[:], w_slot_next[:], diagonal(EPG), ALU.add).then_inc(s["slot_gates_moved"], 1)

            def y_lo_part(q, j):
                dve.wait_ge(s["y_hi_done"], FREE + EPG * q + (j + 1))
                for half in range(2):
                    cs = slice(half * COLS, (half + 1) * COLS)
                    ins = V.scalar_tensor_tensor(y_lo[:, cs], ps[:, 2 + half, :], w_slot[:, j:j + 1], f32(y_hi[:, cs]),
                                                 ALU.mult, ALU.subtract)
                ins.then_inc(s["y_lo_done"], 1)

            def expert_group(q, g, more):
                dve.drain()
                dve.wait_ge(s["y_hi_done"], FREE + EPG * q)
                V.tensor_copy(w_slot[:], w_slot_next[:])
                for m, (j, which) in enumerate(ex_order[:-1]):
                    for n in split_steps(m, more):
                        e_lo(q, n)
                    if which == "up":
                        kc = lambda v: v.rearrange("p (k c) -> p k c", c=P)[:, :, 0:SLOTS]
                        dve.wait_ge(s["gate_tanh_done"], EPG * q + (j + 1))
                        V.scalar_tensor_tensor(e_act[:, 1], e_act[:, 0], 1.0, kc(ps[:, 2, :]), ALU.add, ALU.mult)
                        dve.drain()
                        V.tensor_tensor(e_act[:, 1], e_act[:, 1], kc(ps[:, 3, :]), ALU.mult)
                        dve.drain()
                        dve.wait_ge(mm_done, GB * q + (NB1 + (ex_block[j - 1, "down"] + 2 if j else 0)))
                        V.tensor_copy(a_st[:, :, 0:SLOTS], e_act[:, 1])
                        dve.drain()
                        V.tensor_tensor(a_st[:, :, SLOTS:P], e_act[:, 1], f32(a_st[:, :, 0:SLOTS]),
                                        ALU.subtract).then_inc(s["a_ready"], 1)
                    elif which == "down":
                        y_lo_part(q, j)
                        if more and j == 1:
                            select(q + 1, g + 1)
                if more:
                    slot_gates(q + 1)
                for n in split_steps(len(ex_order) - 1, more):
                    e_lo(q, n)
                y_lo_part(q, EPG - 1)
                for n in split_steps(len(ex_order), more):
                    e_lo(q, n)

            select(0, 0)
            dve.drain().then_inc(s["y_lo_done"], FREE)
            with dve.Fori(0, rounds) as r:
                slot_gates(r * NG)
                with dve.If(r > 0):
                    for n in range(RING):
                        e_lo(r * NG, n)
                with dve.Else():
                    for n in range(2, RING):
                        e_lo(0, n)
                with dve.Fori(0, NG - 1) as g:
                    expert_group(r * NG + g, g, True)
                expert_group(r * NG + (NG - 1), NG - 1, False)
                V.tensor_scalar(iota, iota, float(SLOTS), None, ALU.add)
                dve.drain()
                select(r * NG + NG, 0)
            dve.wait_ge(s["moe_done"], 1)
            for i in range(NT):
                for half in range(2):
                    x_ = x_res[:, i, half * COLS:(half + 1) * COLS]
                    ins = V.scalar_tensor_tensor(x_, ps[:, 4 + 2 * i + half, :], 0.5, x_, ALU.mult, ALU.add)
                ins.then_inc(s["out_ready"], 1)

        @block.tensor
        def _(pe):
            MM = nc.tensor.matmul

            def turn(dst, src, n):
                return nc.tensor.transpose(dst, src, ident[0:n, 0:n])

            def turn_act(name, src, nt, banks, tiled=False, bank0=4):
                for hb in banks:
                    for k in range(2):
                        f = 2 * hb + k
                        for i in range(NT):
                            ins = turn(ps[:, bank0 + hb, (k * NT + i) * P:(k * NT + i + 1) * P],
                                       src[:, i, f * P:(f + 1) * P] if tiled else src[:, i, f:nt * P:nt], P)
                    ins.then_inc(sT[name], 1)

            def hi_products(slot, nth, xh, xl, t0, nt, width, banks, first):
                wh = w_hi[:, slot, 0:nt * width].rearrange("p (t n) -> p t n", t=nt)
                pe.wait_ge(hi_done, nth + 1)
                for i in range(NT):
                    for k in range(nt):
                        o = ps[:, banks + i, 0:width]
                        MM(o, xh[:, t0 + k, i * P:(i + 1) * P], wh[:, k], start=first and k == 0, stop=False)
                        MM(o, xl[:, t0 + k, i * P:(i + 1) * P], wh[:, k], start=False, stop=False)

            def lo_products(slot, nth, xh, t0, nt, width, banks, last):
                wl = w_lo[:, slot, 0:nt * width].rearrange("p (t n) -> p t n", t=nt)
                pe.wait_ge(lo_done, nth + 1)
                for i in range(NT):
                    for k in range(nt):
                        ins = MM(ps[:, banks + i, 0:width], xh[:, t0 + k, i * P:(i + 1) * P], wl[:, k], start=False,
                                 stop=last and k == nt - 1)
                ins.then_inc(mm_done, 1)

            def use_block(slot, nth, xh, xl, t0, nt, width, banks, first, last):
                hi_products(slot, nth, xh, xl, t0, nt, width, banks, first)
                lo_products(slot, nth, xh, t0, nt, width, banks, last)

            def in_block(b, xh, xl, t0=None, first=None, last=None, part="both"):
                c = max(c for c in range(len(chunks)) if first_block[c] <= b)
                k = b - first_block[c]
                _, nt, width = blocks[b].shape
                t0 = k * nt if t0 is None else t0
                first = k == 0 if first is None else first
                last = b == first_block[c + 1] - 1 if last is None else last
                if part != "lo":
                    if first and c >= 2:
                        pe.wait_ge(*moved(c - 2))
                    hi_products(b % RING, b, xh, xl, t0, nt, width, c % 2 * 2, first)
                if part != "hi":
                    lo_products(b % RING, b, xh, t0, nt, width, c % 2 * 2, last)

            def chunk(c, xh=None, xl=None):
                for b in range(first_block[c], first_block[c + 1]):
                    in_block(b, xh or act_hi, xl or act_lo)

            pe.wait_ge(ld["x"], 16 * NT)
            pe.wait_ge(ld["ident"], 32)
            turn_act("x", x_res, KD, range(4))

            def pair_loop(c0, count):
                b0, per = first_block[c0], first_block[c0 + 2] - first_block[c0]
                with pe.Fori(0, count) as it:
                    for k in range(2):
                        c = c0 + k
                        if c0 >= 2 or count == 1:
                            pe.wait_ge(ev_act, it * 2 + (c - 1))
                        for hb in range(2):
                            b = b0 + 2 * k + hb
                            use_block(b % RING, it * per + b, act_hi, act_lo, 4 * hb, 4, COLS, (c % 2) * 2, hb == 0, hb == 1)

            for k in range(2):
                pe.wait_ge(sL["x"], 2 * k + 2)
                in_block(k, act_hi, act_lo)
            chunk(1)
            pair_loop(2, 1)
            pe.wait_ge(s["ws_masked"], 1)
            turn(ps[:, 4, 0:32], conv_rows[:], 32)
            turn(ps[:, 4, 32:40 + 2 * KD], vec_rows[:], 8 + 2 * KD)
            for g in range(GG):
                turn(ps[:, 5, g * P:(g + 1) * P], ws_t[:, g, :], P)
            for g, (bank, o) in enumerate(((6, 0), (7, 0), (4, P))):
                ins = MM(ps[0:AHG, bank, o:o + TOEP], table[:, AHG * g:AHG * (g + 1)], onehot[:, g, :], start=True, stop=True)
            ins.then_inc(s["aux_turned"], 1)
            chunk(4)
            pe.wait_ge(s["aux_moved"], 1)
            pe.wait_ge(ev_act, 2)
            for f in range(KD):
                for i in range(NT):
                    ins = turn(ps[:, 4 + f // 2, (f % 2 * NT + i) * P:(f % 2 * NT + i + 1) * P], zq[:, i, f * P:(f + 1) * P], P)
                if f % 2:
                    ins.then_inc(s["qk_turned"], 1)
            pe.wait_ge(ev_act, 5)
            pe.wait_ge(s["conv_in_ready"], 4)
            for k in range(2):
                for i in range(NT):
                    ins = turn(ps[0:MH, 4, (k * NT + i) * P:(k * NT + i + 1) * P], zif[:, i, k * MH:(k + 1) * MH], P)
            ins.then_inc(s["gates_turned"], 1)
            pair_loop(5, 1)
            pe.wait_ge(s["floor_rows_done"], 1)
            for k, row in enumerate((0, 5)):
                for i in range(NT):
                    ins = turn(ps[:, 5, (k * NT + i) * MH:(k * NT + i + 1) * MH], rows[:, row, i * P:(i + 1) * P], MH)
            ins.then_inc(s["cols_turned"], 1)
            pair_loop(7, 2)
            pe.wait_ge(s["qk_silu_done"], 1)
            pe.wait_ge(s["cols_moved"], 1)

            def mlstm_values(h):
                pe.wait_ge(s["m_probs_ready"], h + 1)
                if h >= 2:
                    pe.wait_ge(s["numer_moved"], h - 1)
                b = 6 + h % 2
                MM(ps[:, b, 0:MDH + 1], pm[:, h % 2, 0:P], vx[:, 0, h, 0:MDH + 1], start=True, stop=True)
                MM(ps[:, b, S:S + MDH + 1], pm[:, h % 2, P:2 * P], vx[:, 0, h, 0:MDH + 1], start=True, stop=False)
                MM(ps[:, b, S:S + MDH + 1], pm[:, h % 2, 2 * P:3 * P], vx[:, 1, h, 0:MDH + 1], start=False,
                   stop=True).then_inc(s["numer_done"], 1)

            for h in range(MH):
                if h >= 1:
                    pe.wait_ge(s["decay_weights_done"], h)
                MM(ps[:, 4, 0:S], minus_head[0:MH, h, :], rows[:, 3, :], start=True, stop=False, skip_group_check=True)
                MM(ps[:, 4, 0:P], ident[:], neg_future, start=False, stop=False, skip_group_check=True)
                MM(ps[:, 4, S:S + P], minus_head[0:MH, h, :], rows[:, 3, P:S], start=False, stop=False, skip_group_check=True)
                MM(ps[:, 4, S:S + P], ident[:], neg_future, start=False, stop=True,
                   skip_group_check=True).then_inc(s["decay_exponents_done"], 1)
                if h >= 1:
                    pe.wait_ge(s["m_probs_ready"], h)
                MM(ps[:, 5, 0:S], post[:, MH + h, 0:P], post[:, h, :], start=True, stop=True)
                MM(ps[:, 5, S:S + P], post[:, MH + h, P:S], post[:, h, P:S], start=True, stop=True).then_inc(s["scores_done"], 1)
                if h >= 1:
                    mlstm_values(h - 1)
                in_block(22 + h, act_hi, act_lo)
            mlstm_values(MH - 1)
            in_block(26, act_hi, act_lo)
            pe.wait_ge(s["aqk_ready"], 1)
            pe.wait_ge(s["numer_moved"], MH)
            for n in range(6):
                if n == 4:
                    in_block(27, act_hi, act_lo)
                if n >= 4:
                    pe.wait_ge(s["aqk_moved"], n - 3)
                for k in range(2):
                    for i in range(NT):
                        f = 2 * n + k
                        ins = turn(ps[:, 4 + n % 4, (k * NT + i) * P:(k * NT + i + 1) * P], zqk[:, i, f * P:(f + 1) * P], P)
                ins.then_inc(s["aqk_turned"], 1)
            pe.wait_ge(s["aqk_moved"], 6)

            def attn_scores(u):
                jp, t, jo = u // 4, u // 2 % 2, u % 2
                w = (t + 1) * P
                if u >= 1:
                    pe.wait_ge(s["a_logits_moved"], u)
                for g in range(AG):
                    hd = AHG * g + 2 * jp + jo
                    r0 = hd % 2 * ADH
                    ins = MM(ps[:, 4 + g // 2, g % 2 * S:g % 2 * S + w], qkT[r0:r0 + ADH, hd // 2, t * P:(t + 1) * P],
                             qkT[r0:r0 + ADH, 6 + hd // 2, 0:w], start=True, stop=True)
                ins.then_inc(s["a_logits_done"], 1)

            squares = [[(g, m) for g in range(AG) for m in range(t + 1)] for t in range(NT)]

            def turn_probs(u, f):
                t = u // 2 % 2
                pe.wait_ge(s["a_probs_ready"], u + 1)
                if fills_before[u] + f:
                    pe.wait_ge(s["a_probs_moved"], fills_before[u] + f)
                lo, n = turn_fills[t][f]
                for x in range(lo, lo + n):
                    g, m = squares[t][x]
                    ins = turn(ps[:, 6, (x - lo) * P:(x - lo + 1) * P], (lg0, lg1)[u % 2][:, g, m * P:(m + 1) * P], P)
                ins.then_inc(s["a_probs_turned"], 1)

            def attn_values(u):
                jp, t, jo = u // 4, u // 2 % 2, u % 2
                pe.wait_ge(s["a_probs_moved"], fills_before[u + 1])
                if u >= 2 and not jo:
                    pe.wait_ge(s["a_out_lo_done"], u // 2)
                for x, (g, m) in enumerate(squares[t]):
                    hd = AHG * g + 2 * jp + jo
                    ins = MM(ps[jo * ADH:(jo + 1) * ADH, 7, g * P:(g + 1) * P], zv[:, m, hd * ADH:(hd + 1) * ADH],
                             pT[:, x * P:(x + 1) * P], start=m == 0, stop=m == t)
                ins.then_inc(s["a_out_done"], 1)

            attn_scores(0)
            pe.wait_ge(s["gv_ready"], 1)
            for n in range(NT):
                for g in range(GG):
                    ins = MM(ps[:, 6 + n, g * GC:(g + 1) * GC], wT[:, g, :], zg[:, n, GW + g * GC:GW + (g + 1) * GC],
                             start=True, stop=True)
                ins.then_inc(s["gv_mixed"], 1)
            for u in range(8):
                b = 28 + blocks_before[u]
                if u < 7:
                    attn_scores(u + 1)
                if u in filled:
                    in_block(b, act_hi, act_lo, part="hi")
                if u == 0:
                    pe.wait_ge(s["yc_done"], NT)
                turn_probs(u, 0)
                if u in filled:
                    in_block(b, act_hi, act_lo, part="lo")
                if u // 2 % 2:
                    turn_probs(u, 1)
                attn_values(u)
            pe.wait_ge(s["ya_done"], 1)
            pe.wait_ge(s["a_logits_moved"], 8)
            turn_act("a", zo, 4, range(2))
            pe.wait_ge(s["a_out_lo_done"], 4)
            chunk(C_B, yb_hi, yb_lo)
            turn_act("c", zg, 4, range(2), bank0=6)
            chunk(C_B + 1, yb_hi, yb_lo)
            pe.wait_ge(sL["a"], 2)
            pe.wait_ge(sL["c"], 2)
            pe.wait_ge(ld["mem"], 16 * NT)
            turn_act("mem", mem_x, KD, range(4))
            for n in range(2):
                chunk(C_A + n, ya_hi, ya_lo)
            for n in range(2):
                chunk(C_C + n, yc_hi, yc_lo)
            pe.wait_ge(sL["mem"], KD // 2)
            for n in range(2):
                in_block(first_block[C_K] + n, act_hi, act_lo)
                pe.wait_ge(s["merged_ready"], n + 1)
                turn_act("merged", merged, KD, range(2 * n, 2 * n + 2), tiled=True)
            for c in range(C_OUT, C_OUT + 2):
                for k in range(2):
                    pe.wait_ge(sL["merged"], 2 * k + 2)
                    in_block(first_block[c] + k, mg_hi, mg_lo)
                    if c > C_OUT and k == 0:
                        pe.wait_ge(*moved(C_OUT))
                        turn_act("x1", x_res, KD, range(2), tiled=True)
            in_block(first_block[C_V0], act_hi, act_lo, t0=0, first=True, last=False)
            pe.wait_ge(*moved(C_OUT + 1))
            turn_act("x1", x_res, KD, range(2, 4), tiled=True)
            for k in range(2):
                pe.wait_ge(sL["x1"], 2 * k + 2)
                in_block(first_block[C_XQ] + k, mg_hi, mg_lo)
            pe.wait_ge(s["xk_ready"], 1)

            def turn_heads(src, name, bank0):
                for h in range(XH):
                    for i in range(NT):
                        ins = turn(ps[:, bank0 + h // 2, (h % 2 * NT + i) * P:(h % 2 * NT + i + 1) * P],
                                   src[:, i, h * P:(h + 1) * P], P)
                    if h % 2:
                        ins.then_inc(s[name], 1)

            turn_heads(xkv, "xk_turned", 6)
            in_block(first_block[C_V1], act_hi, act_lo, t0=4, first=False, last=True)
            pe.wait_ge(s["xq_ready"], 1)
            turn_heads(xq, "xq_turned", 4)
            pe.wait_ge(s["xq_moved"], 2)
            pe.wait_ge(s["xk_moved"], 2)
            for t in range(NT):
                for h in range(XH):
                    ins = MM(ps[:, 4 + 2 * t + h // 2, h % 2 * S:(h % 2 + 1) * S], xqT[:, h, t * P:(t + 1) * P], xkT[:, h, :],
                             start=True, stop=True)
                    if h % 2:
                        ins.then_inc(s["x_logits_done"], 1)
            pe.wait_ge(*moved(C_V1))
            for t in range(NT):
                for h in range(XH):
                    if h % 2 == 0:
                        pe.wait_ge(s["x_probs_ready"], 2 * t + h // 2 + 1)
                    for m in range(NT):
                        ins = turn(ps[:, 4 + 2 * t + h // 2, (h % 2 * NT + m) * P:(h % 2 * NT + m + 1) * P],
                                   xp[:, t, h * S + m * P:h * S + (m + 1) * P], P)
                    if h % 2:
                        ins.then_inc(s["x_probs_turned"], 1)
            pe.wait_ge(s["x_probs_moved"], 2 * NT)
            for h in range(XH):
                for m in range(NT):
                    ins = MM(ps[:, 4 + h // 2, h % 2 * S:(h % 2 + 1) * S], xkv[:, m, XW + h * XDH:XW + (h + 1) * XDH],
                             xpT[:, h, m, :], start=m == 0, stop=m == NT - 1)
                if h % 2:
                    ins.then_inc(sT["o"], 1)
            pe.wait_ge(sL["o"], 2)
            chunk(C_XO, oT_hi, oT_lo)
            last_block = first_block[C_XO + 1]
            in_block(last_block, oT_hi, oT_lo, part="hi")
            pe.wait_ge(*moved(C_XO))
            turn_act("x2", x_res, KD, range(2), tiled=True)
            in_block(last_block, oT_hi, oT_lo, part="lo")

            def router_products(k0):
                for i in range(NT):
                    for k in range(k0, k0 + KD // 2):
                        ins = MM(ps[:, 2 + i, 0:NE], x2T[:, k, i * P:(i + 1) * P], router_w[:, k, :], start=k == 0,
                                 stop=k == KD - 1)
                return ins

            pe.wait_ge(ld["moe"], 32)
            pe.wait_ge(s["x2T_moved"], 2)
            router_products(0)
            pe.wait_ge(*moved(C_XO + 1))
            turn_act("x2", x_res, KD, range(2, 4), tiled=True)
            pe.wait_ge(s["x2T_moved"], 4)
            router_products(KD // 2).then_inc(s["router_logits_done"], 1)
            pe.wait_ge(s["zeros_written"], 1)
            for b in range(4, 8):
                for k in range(4):
                    MM(ps[:, b, k * P:(k + 1) * P], zeros, zeros, start=k == 0, stop=False, skip_group_check=True)
            for name in ("gathered", "sel_turned"):
                pe.drain().then_inc(s[name], FREE)
            pe.wait_ge(s["chosen"], 1)
            ch = chosen.rearrange("p (i e) -> p i e", i=NT)
            MM(ps[:, 1, 0:NE], before, ch[:, 0], start=True, stop=True)
            MM(ps[:, 1, NE:2 * NE], before, ch[:, 1], start=True, stop=False)
            MM(ps[:, 1, NE:2 * NE], ones, ch[:, 0], start=False, stop=True)
            MM(ps[:, 1, 2 * NE:3 * NE], ones, ch[:, 0], start=True, stop=False)
            MM(ps[:, 1, 2 * NE:3 * NE], ones, ch[:, 1], start=False, stop=True).then_inc(s["places_done"], 1)
            pe.wait_ge(s["rounds_ready"], 1)
            pe.wait_ge(s["h_lo_done"], 1)
            rounds = pe.value_load(n_rounds_i[0:1, 0:1], min_val=1, max_val=S // SLOTS)

            def slot_gates(q):
                pe.wait_ge(s["sel_ready"], q + 1)
                pe.wait_ge(s["gu_moved"], FREE + 2 * EPG * q)
                for e in range(EPG):
                    for i in range(NT):
                        ins = MM(ps[:, 1, e * 2 * EPG:(e + 1) * 2 * EPG], sel[:, i, e, :],
                                 gcur[:, i].rearrange("p k e -> p (k e)"), start=i == 0, stop=i == NT - 1)
                ins.then_inc(s["slot_gates_done"], 1)

            def gather(q, tiles):
                for t in tiles:
                    if t == 1:
                        pe.wait_ge(s["slot_gates_moved"], q + 1)
                    if t >= 2:
                        pe.wait_ge(s["gathered_moved"], KD * q + (t - 1))
                    for k, hh in enumerate((h_hi, h_lo)):
                        for i in range(NT):
                            ins = MM(ps[:, t % 2, k * EPG * SLOTS:(k + 1) * EPG * SLOTS], hh[:, i, t * P:(t + 1) * P],
                                     sel[:, i, :, 0:SLOTS], start=i == 0, stop=i == NT - 1)
                    ins.then_inc(s["gathered"], 1)

            def turn_selection(q):
                pe.wait_ge(s["y_lo_done"], FREE + EPG * q)
                for e in range(EPG):
                    for i in range(NT):
                        ins = turn(ps[:, 2 + e // 2, (e % 2 * NT + i) * P:(e % 2 * NT + i + 1) * P], f32(sel[:, i, e, :]), P)
                    if e % 2:
                        ins.then_inc(s["sel_turned"], 1)

            def e_block(q, n, lhs, bank, first, last):
                b, nt = NB1 + n, 4 - direct.get(n, 0)
                raw = e_slot(n)[0]
                for k, (done, w) in enumerate(((hi_done, w_hi), (lo_done, w_lo))):
                    pe.wait_ge(done, GB * q + (b + 1))
                    for t in range(nt):
                        ins = MM(ps[:, bank, :], lhs[t], w[:, b % RING, t * COLS:(t + 1) * COLS],
                                 start=first and not k and t == 0, stop=last and k == 1 and t == 3)
                for t in range(nt, 4):
                    ins = MM(ps[:, bank, :], f32(lhs[t]), raw[:, t * COLS:(t + 1) * COLS], start=False, stop=last and t == 3)
                ins.then_inc(mm_done, 1)
                return ins

            def wide(q, j, n, bank):
                for half in range(2):
                    if j == 0:
                        pe.wait_ge(s["gathered_moved"], KD * q + (KD - 1 + half))
                    e_block(q, n + half, [xg[:, 4 * half + t, j, :] for t in range(4)], bank, half == 0, half == 1)

            def e_turn(q, j):
                pe.wait_ge(s["gu_moved"], FREE + 2 * (EPG * q + j) + 2)
                pe.wait_ge(s["y_lo_done"], FREE + EPG * q + j)
                if j == 0:
                    pe.wait_ge(s["selT_moved"], 2 * q + 2)
                for k in range(2):
                    for f in range(FF // P):
                        ins = MM(ps[:, 2 + k, f * P:(f + 1) * P], gu[:, k, f:FF:FF // P], both, start=True, stop=True)
                ins.then_inc(s["gu_turned"], 1)

            def e_scatter(q, j):
                pe.wait_ge(s["y_lo_done"], FREE + EPG * q + (j + 1))
                for i in range(NT):
                    for half in range(2):
                        for y in (y_hi, y_lo):
                            ins = MM(ps[:, 4 + 2 * i + half, :], selT[:, j, i * P:(i + 1) * P],
                                     y[:, half * COLS:(half + 1) * COLS], start=False, stop=False, skip_group_check=True)
                ins.then_inc(s["scattered"], 1)

            def e_down(q, j, m, half):
                pe.wait_ge(s["a_ready"], EPG * q + (j + 1))
                e_block(q, 2 * m + half, [a_st[:, t, :] for t in range(4)], 2 + half, True, True)

            def expert_group(q, more):
                for m, (j, which) in enumerate(ex_order[:-1]):
                    if which == "gate":
                        wide(q, j, 2 * m, 0)
                        if j == 0:
                            turn_selection(q)
                    elif which == "up":
                        wide(q, j, 2 * m, 1)
                        if j:
                            e_scatter(q, j - 1)
                        e_turn(q, j)
                    else:
                        for half in range(2):
                            e_down(q, j, m, half)
                if more:
                    slot_gates(q + 1)
                    gather(q + 1, range(0, 2))
                e_down(q, EPG - 1, len(ex_order) - 1, 0)
                if more:
                    gather(q + 1, range(2, 4))
                e_down(q, EPG - 1, len(ex_order) - 1, 1)
                if more:
                    gather(q + 1, range(4, KD))
                e_scatter(q, EPG - 1)

            pe.drain().then_inc(s["scattered"], FREE)
            with pe.Fori(0, rounds) as r:
                slot_gates(r * NG)
                gather(r * NG, range(KD))
                with pe.Fori(0, NG - 1) as g:
                    expert_group(r * NG + g, True)
                expert_group(r * NG + (NG - 1), False)
            MM(ps[:, 0, 0:P], zeros, zeros, start=True, stop=True).then_inc(s["moe_done"], 1)


_INS = ["x", "mem", "norm_mix", "w_in", "mlstm_conv", "mlstm_gate_b", "mlstm_norm", "attn_qk_norm", "gmlp_norm",
        "gmlp_ws", "gmlp_bs", "w_branch_a", "w_branch_b", "w_branch_c", "w_out", "rel_bias", "norm_xattn", "norm_mem",
        "w_xq", "w_xkv", "xattn_qk_norm", "w_xo", "norm_ffn", "router_w", "router_b", "w_expert_gate", "w_expert_up",
        "w_expert_down"]


def kernel(**inputs):
    import concourse.bacc as bacc
    from concourse.bass_utils import run_bass_kernel_spmd

    nc = bacc.Bacc("TRN2", target_bir_lowering=False, num_devices=1, dynamic_dma_scratch_size=1024)
    arrays, aps = {}, {}
    given = {name: np.ascontiguousarray(inputs[name]) for name in _INS}
    given.update(zip(("c_ident", "c_const", "c_onehot"), shape_constants()))
    for name, a in given.items():
        arrays[f"in_{name}"] = a
        aps[name] = nc.dram_tensor(f"in_{name}", a.shape, mybir.dt.from_np(a.dtype), kind="ExternalInput").ap()
    out = nc.dram_tensor("out_0", (1, S, D), mybir.dt.float32, kind="ExternalOutput").ap()
    build_program(nc, aps, out)
    result = run_bass_kernel_spmd(nc, [arrays], core_ids=[0])
    return result.results[0]["out_0"]
```
